# Optimizing a Trainium2 kernel written in Bass

```python
import math
import jax, jax.numpy as jnp
from jax import lax
import numpy as np
import jax
import jax.numpy as jnp

D_MODEL = 1024
BATCH = 1
SEQ = 256
DEPTH = 1

D_MIX = D_MODEL
ATTN_WIDTH = D_MIX // 2
CONV_WIDTH = D_MIX - ATTN_WIDTH
N_HEADS = 8
HEAD_DIM = ATTN_WIDTH // N_HEADS
CONV_KERNEL = 31
MOBA_BLOCK = 256
MOBA_TOPK = 3
Q_CHUNK = 64
ROPE_THETA = 10000.0
D_FF = -(-8 * D_MODEL // (3 * 256)) * 256
EPS = 1e-6
D_IN = 3 * ATTN_WIDTH + 2 * CONV_WIDTH


def rms_norm(x, g):
    xf = x.astype(jnp.float32)
    y = xf * lax.rsqrt(jnp.mean(xf * xf, axis=-1, keepdims=True) + EPS)
    return (y * g.astype(jnp.float32)).astype(x.dtype)

def layer_norm(x, g, b):
    xf = x.astype(jnp.float32)
    mu = jnp.mean(xf, axis=-1, keepdims=True)
    var = jnp.mean(jnp.square(xf - mu), axis=-1, keepdims=True)
    y = (xf - mu) * lax.rsqrt(var + EPS)
    return (y * g.astype(jnp.float32) + b.astype(jnp.float32)).astype(x.dtype)

def rope_tables(seq_len):
    pos = jnp.arange(seq_len, dtype=jnp.float32)
    inv_freq = ROPE_THETA ** (-jnp.arange(0, HEAD_DIM, 2, dtype=jnp.float32) / HEAD_DIM)
    ang = pos[:, None] * inv_freq[None, :]
    ang = jnp.concatenate([ang, ang], axis=-1)
    return jnp.cos(ang)[:, None, :], jnp.sin(ang)[:, None, :]

def apply_rope(x, cos, sin):
    xf = x.astype(jnp.float32)
    x1, x2 = jnp.split(xf, 2, axis=-1)
    rot = jnp.concatenate([-x2, x1], axis=-1)
    return (xf * cos + rot * sin).astype(x.dtype)

def moba_attention(q, k, v):
    B, H, S, Dh = q.shape
    n_blocks = -(-S // MOBA_BLOCK)
    pad = n_blocks * MOBA_BLOCK - S
    kp = jnp.pad(k, ((0, 0), (0, 0), (0, pad), (0, 0)))
    vp = jnp.pad(v, ((0, 0), (0, 0), (0, pad), (0, 0)))
    kb = kp.reshape(B, H, n_blocks, MOBA_BLOCK, Dh)
    vb = vp.reshape(B, H, n_blocks, MOBA_BLOCK, Dh)
    k_mean = jnp.mean(kb.astype(jnp.float32), axis=3)
    topk = min(MOBA_TOPK, n_blocks)
    scale = HEAD_DIM ** -0.5
    b_idx = jnp.arange(B)[:, None, None, None]
    h_idx = jnp.arange(H)[None, :, None, None]
    key_off = jnp.arange(MOBA_BLOCK)
    block_ids = jnp.arange(n_blocks)
    n_chunks = S // Q_CHUNK

    def chunk_fn(c):
        start = c * Q_CHUNK
        qc = lax.dynamic_slice_in_dim(q, start, Q_CHUNK, axis=2)
        q_pos = start + jnp.arange(Q_CHUNK)
        own = start // MOBA_BLOCK
        gate = jnp.einsum('bhqd,bhnd->bhqn', qc.astype(jnp.float32), k_mean)
        gate = jnp.where((block_ids < own)[None, None, None, :], gate, -jnp.inf)
        _, top_idx = lax.top_k(gate, topk)
        sel_valid = top_idx < own
        k_sel = kb[b_idx, h_idx, top_idx]
        v_sel = vb[b_idx, h_idx, top_idx]
        s_sel = jnp.einsum('bhqd,bhqnkd->bhqnk', qc, k_sel).astype(jnp.float32) * scale
        s_sel = jnp.where(sel_valid[..., None], s_sel, -jnp.inf)
        s_sel = s_sel.reshape(B, H, Q_CHUNK, topk * MOBA_BLOCK)
        k_own = lax.dynamic_slice_in_dim(kp, own * MOBA_BLOCK, MOBA_BLOCK, axis=2)
        v_own = lax.dynamic_slice_in_dim(vp, own * MOBA_BLOCK, MOBA_BLOCK, axis=2)
        s_own = jnp.einsum('bhqd,bhkd->bhqk', qc, k_own).astype(jnp.float32) * scale
        own_pos = own * MOBA_BLOCK + key_off
        s_own = jnp.where((own_pos[None, :] <= q_pos[:, None])[None, None], s_own, -jnp.inf)
        p = jax.nn.softmax(jnp.concatenate([s_own, s_sel], axis=-1), axis=-1)
        p_own = p[..., :MOBA_BLOCK].astype(v.dtype)
        p_sel = p[..., MOBA_BLOCK:].reshape(B, H, Q_CHUNK, topk, MOBA_BLOCK).astype(v.dtype)
        out = (jnp.einsum('bhqk,bhkd->bhqd', p_own, v_own)
               + jnp.einsum('bhqnk,bhqnkd->bhqd', p_sel, v_sel))
        return out

    outs = lax.map(chunk_fn, jnp.arange(n_chunks))
    return outs.transpose(1, 2, 0, 3, 4).reshape(B, H, S, Dh)

def conformer_conv(u, glu_b, dw_w, dw_b, ln_g, ln_b):
    u = u + glu_b.astype(u.dtype)
    a, g = jnp.split(u, 2, axis=-1)
    h = a * jax.nn.sigmoid(g)
    h = jnp.pad(h, ((0, 0), (CONV_KERNEL - 1, 0), (0, 0)))
    h = lax.conv_general_dilated(
        h, dw_w[:, None, :].astype(h.dtype), window_strides=(1,), padding='VALID',
        dimension_numbers=('NWC', 'WIO', 'NWC'), feature_group_count=CONV_WIDTH)
    h = h + dw_b.astype(h.dtype)
    h = layer_norm(h, ln_g, ln_b)
    return jax.nn.silu(h)

def first_inputs(seed: int = 0) -> dict:
    key = jax.random.key(seed)
    ks = jax.random.split(key, 16)
    f32 = jnp.float32
    L = DEPTH

    def nrm(k, shape, scale):
        return jax.random.normal(k, shape, f32) * scale

    return {
        "x": jax.random.normal(ks[0], (BATCH, SEQ, D_MODEL), f32),
        "norm1_g": 1.0 + nrm(ks[1], (L, D_MODEL), 0.02),
        "w_in": nrm(ks[2], (L, D_MODEL, D_IN), D_MODEL ** -0.5),
        "glu_b": nrm(ks[3], (L, 2 * CONV_WIDTH), 0.02),
        "q_norm_g": 1.0 + nrm(ks[4], (L, HEAD_DIM), 0.02),
        "k_norm_g": 1.0 + nrm(ks[5], (L, HEAD_DIM), 0.02),
        "dw_w": nrm(ks[6], (L, CONV_KERNEL, CONV_WIDTH), CONV_KERNEL ** -0.5),
        "dw_b": nrm(ks[7], (L, CONV_WIDTH), 0.02),
        "conv_ln_g": 1.0 + nrm(ks[8], (L, CONV_WIDTH), 0.02),
        "conv_ln_b": nrm(ks[9], (L, CONV_WIDTH), 0.02),
        "w_out": nrm(ks[10], (L, D_MIX, D_MODEL), D_MIX ** -0.5),
        "norm2_g": 1.0 + nrm(ks[11], (L, D_MODEL), 0.02),
        "w_gate": nrm(ks[12], (L, D_MODEL, D_FF), D_MODEL ** -0.5),
        "w_up": nrm(ks[13], (L, D_MODEL, D_FF), D_MODEL ** -0.5),
        "w_down": nrm(ks[14], (L, D_FF, D_MODEL), D_FF ** -0.5),
    }

def first_block(x, norm1_g, w_in, glu_b, q_norm_g, k_norm_g, dw_w, dw_b, conv_ln_g,
              conv_ln_b, w_out, norm2_g, w_gate, w_up, w_down):
    B, S, _ = x.shape
    cos, sin = rope_tables(S)
    for l in range(DEPTH):
        h = rms_norm(x, norm1_g[l])
        proj = h @ w_in[l]
        q, k, v, u = jnp.split(proj, [ATTN_WIDTH, 2 * ATTN_WIDTH, 3 * ATTN_WIDTH], axis=-1)
        q = q.reshape(B, S, N_HEADS, HEAD_DIM)
        k = k.reshape(B, S, N_HEADS, HEAD_DIM)
        v = v.reshape(B, S, N_HEADS, HEAD_DIM)
        q = apply_rope(rms_norm(q, q_norm_g[l]), cos, sin)
        k = apply_rope(rms_norm(k, k_norm_g[l]), cos, sin)
        attn = moba_attention(q.transpose(0, 2, 1, 3), k.transpose(0, 2, 1, 3),
                              v.transpose(0, 2, 1, 3))
        attn = attn.transpose(0, 2, 1, 3).reshape(B, S, ATTN_WIDTH)
        conv = conformer_conv(u, glu_b[l], dw_w[l], dw_b[l], conv_ln_g[l], conv_ln_b[l])
        x = x + jnp.concatenate([attn, conv], axis=-1) @ w_out[l]
        h = rms_norm(x, norm2_g[l])
        x = x + (jax.nn.silu(h @ w_gate[l]) * (h @ w_up[l])) @ w_down[l]
    return x


DEPTH_2 = 2

CHUNK = 64
Q_BLOCK = 128
N_MIXERS = 2
N_HEADS_2 = 16
HEAD_DIM_2 = 64
D_ATT = N_HEADS_2 * HEAD_DIM_2
SSM_GROUP = 16
D_SSM = D_MODEL
N_GROUPS = D_SSM // SSM_GROUP
STATE = 64
_FF_RAW = -(-8 * D_MODEL // 3)
D_FF_2 = -(-_FF_RAW // 256) * 256
N_FOX = (DEPTH_2 + 1) // 2
N_S5 = DEPTH_2 // 2
DT_MIN = 1e-3
DT_MAX = 1e-1


def rmsnorm(x, gain):
    xf = x.astype(jnp.float32)
    y = xf * lax.rsqrt(jnp.mean(xf * xf, axis=-1, keepdims=True) + EPS)
    return (y * gain.astype(jnp.float32)).astype(x.dtype)

def fox_mixer(h, w_in, b_f, q_gain, k_gain, w_out):
    bsz, seq_len, _ = h.shape
    proj = h @ w_in
    q = proj[..., :D_ATT]
    k = proj[..., D_ATT:2 * D_ATT]
    v = proj[..., 2 * D_ATT:3 * D_ATT]
    gate = proj[..., 3 * D_ATT:4 * D_ATT]
    f_logit = proj[..., 4 * D_ATT:]

    def heads(t):
        return t.reshape(bsz, seq_len, N_HEADS_2, HEAD_DIM_2).transpose(0, 2, 1, 3)

    q = rmsnorm(heads(q), q_gain)
    k = rmsnorm(heads(k), k_gain)
    v = heads(v)
    log_f = jax.nn.log_sigmoid(f_logit.astype(jnp.float32) + b_f.astype(jnp.float32))
    c = jnp.cumsum(log_f, axis=1).transpose(0, 2, 1)
    scale = HEAD_DIM_2 ** -0.5

    outs = []
    for blk in range(seq_len // Q_BLOCK):
        q0 = blk * Q_BLOCK
        k_end = q0 + Q_BLOCK
        qb = q[:, :, q0:k_end]
        kb = k[:, :, :k_end]
        vb = v[:, :, :k_end]
        s = jnp.einsum('bhqd,bhkd->bhqk', qb, kb).astype(jnp.float32) * scale
        s = s + c[:, :, q0:k_end, None] - c[:, :, None, :k_end]
        q_pos = q0 + jnp.arange(Q_BLOCK)
        mask = q_pos[:, None] >= jnp.arange(k_end)[None, :]
        s = jnp.where(mask, s, -jnp.inf)
        p = jax.nn.softmax(s, axis=-1).astype(vb.dtype)
        outs.append(jnp.einsum('bhqk,bhkd->bhqd', p, vb))
    o = jnp.concatenate(outs, axis=2)
    o = o.transpose(0, 2, 1, 3).reshape(bsz, seq_len, D_ATT)
    o = o * jax.nn.sigmoid(gate)
    return o @ w_out

def _complex_linear_combine(e1, e2):
    a1r, a1i, b1r, b1i = e1
    a2r, a2i, b2r, b2i = e2
    return (a2r * a1r - a2i * a1i,
            a2r * a1i + a2i * a1r,
            a2r * b1r - a2i * b1i + b2r,
            a2r * b1i + a2i * b1r + b2i)

def s5_mixer(h, w_in, log_dt, lam_re, lam_im, b_re, b_im, c_re, c_im, d_skip, w_glu, w_out):
    f32 = jnp.float32
    bsz, seq_len, _ = h.shape
    u = (h @ w_in).astype(f32)
    lam_re = lam_re.astype(f32)
    lam_im = lam_im.astype(f32)
    dt = jnp.exp(log_dt.astype(f32))[:, None]
    mag = jnp.exp(lam_re * dt)
    a_re = mag * jnp.cos(lam_im * dt)
    a_im = mag * jnp.sin(lam_im * dt)
    den = lam_re * lam_re + lam_im * lam_im
    n_re = a_re - 1.0
    z_re = (n_re * lam_re + a_im * lam_im) / den
    z_im = (a_im * lam_re - n_re * lam_im) / den
    b_re = b_re.astype(f32)
    b_im = b_im.astype(f32)
    bb_re = z_re[..., None] * b_re - z_im[..., None] * b_im
    bb_im = z_re[..., None] * b_im + z_im[..., None] * b_re
    c_re = c_re.astype(f32)
    c_im = c_im.astype(f32)

    n_chunks = seq_len // CHUNK
    u_chunks = u.reshape(bsz, n_chunks, CHUNK, N_GROUPS, SSM_GROUP).transpose(1, 0, 2, 3, 4)

    def step(carry, u_c):
        s_re, s_im = carry
        bu_re = jnp.einsum('gpc,bkgc->bkgp', bb_re, u_c)
        bu_im = jnp.einsum('gpc,bkgc->bkgp', bb_im, u_c)
        bu_re = bu_re.at[:, 0].add(a_re * s_re - a_im * s_im)
        bu_im = bu_im.at[:, 0].add(a_re * s_im + a_im * s_re)
        a_seq_re = jnp.broadcast_to(a_re, bu_re.shape)
        a_seq_im = jnp.broadcast_to(a_im, bu_im.shape)
        _, _, x_re, x_im = lax.associative_scan(
            _complex_linear_combine, (a_seq_re, a_seq_im, bu_re, bu_im), axis=1)
        y = (jnp.einsum('gcp,bkgp->bkgc', c_re, x_re)
             - jnp.einsum('gcp,bkgp->bkgc', c_im, x_im))
        return (x_re[:, -1], x_im[:, -1]), y

    init = (jnp.zeros((bsz, N_GROUPS, STATE), f32), jnp.zeros((bsz, N_GROUPS, STATE), f32))
    _, y = lax.scan(step, init, u_chunks)
    y = y.transpose(1, 0, 2, 3, 4).reshape(bsz, seq_len, D_SSM)
    y = y + d_skip.astype(f32) * u
    y = jax.nn.gelu(y).astype(h.dtype)
    y = y * jax.nn.sigmoid(y @ w_glu)
    return y @ w_out

def swiglu(h, w_gate, w_up, w_down):
    return (jax.nn.silu(h @ w_gate) * (h @ w_up)) @ w_down

def second_inputs(seed: int = 0) -> dict:
    key = jax.random.key(seed)
    ks = jax.random.split(key, 24)
    f32 = jnp.float32

    def nrm(k, shape, scale):
        return jax.random.normal(k, shape, f32) * scale

    def gain(k, shape):
        return 1.0 + 0.02 * jax.random.normal(k, shape, f32)

    x = jax.random.normal(ks[0], (BATCH, SEQ, D_MODEL), f32)
    fox_w_in = nrm(ks[1], (N_FOX, D_MODEL, 4 * D_ATT + N_HEADS_2), D_MODEL ** -0.5)
    fox_b_f = jax.random.uniform(ks[2], (N_FOX, N_HEADS_2), f32, minval=1.0, maxval=5.0)
    fox_q_gain = gain(ks[3], (N_FOX, HEAD_DIM_2))
    fox_k_gain = gain(ks[4], (N_FOX, HEAD_DIM_2))
    fox_w_out = nrm(ks[5], (N_FOX, D_ATT, D_MODEL), D_ATT ** -0.5)
    s5_w_in = nrm(ks[6], (N_S5, D_MODEL, D_SSM), D_MODEL ** -0.5)
    s5_log_dt = jax.random.uniform(ks[7], (N_S5, N_GROUPS), f32,
                                   minval=math.log(DT_MIN), maxval=math.log(DT_MAX))
    s5_lam_re = -0.5 + 0.01 * jax.random.normal(ks[8], (N_S5, N_GROUPS, STATE), f32)
    s5_lam_im = (math.pi * jnp.arange(STATE, dtype=f32)
                 + 0.01 * jax.random.normal(ks[9], (N_S5, N_GROUPS, STATE), f32))
    s5_b_re = nrm(ks[10], (N_S5, N_GROUPS, STATE, SSM_GROUP), (2 * SSM_GROUP) ** -0.5)
    s5_b_im = nrm(ks[11], (N_S5, N_GROUPS, STATE, SSM_GROUP), (2 * SSM_GROUP) ** -0.5)
    s5_c_re = nrm(ks[12], (N_S5, N_GROUPS, SSM_GROUP, STATE), (2 * STATE) ** -0.5)
    s5_c_im = nrm(ks[13], (N_S5, N_GROUPS, SSM_GROUP, STATE), (2 * STATE) ** -0.5)
    s5_d = nrm(ks[14], (N_S5, D_SSM), 1.0)
    s5_w_glu = nrm(ks[15], (N_S5, D_SSM, D_SSM), D_SSM ** -0.5)
    s5_w_out = nrm(ks[16], (N_S5, D_SSM, D_MODEL), D_SSM ** -0.5)
    mix_pre_gain = gain(ks[17], (DEPTH_2, D_MODEL))
    mix_post_gain = gain(ks[18], (DEPTH_2, D_MODEL))
    ffn_pre_gain = gain(ks[19], (DEPTH_2, D_MODEL))
    ffn_post_gain = gain(ks[20], (DEPTH_2, D_MODEL))
    ffn_w_gate = nrm(ks[21], (DEPTH_2, D_MODEL, D_FF_2), D_MODEL ** -0.5)
    ffn_w_up = nrm(ks[22], (DEPTH_2, D_MODEL, D_FF_2), D_MODEL ** -0.5)
    ffn_w_down = nrm(ks[23], (DEPTH_2, D_FF_2, D_MODEL), D_FF_2 ** -0.5)
    return {
        'x': x,
        'fox_w_in': fox_w_in, 'fox_b_f': fox_b_f, 'fox_q_gain': fox_q_gain,
        'fox_k_gain': fox_k_gain, 'fox_w_out': fox_w_out,
        's5_w_in': s5_w_in, 's5_log_dt': s5_log_dt, 's5_lam_re': s5_lam_re,
        's5_lam_im': s5_lam_im, 's5_b_re': s5_b_re, 's5_b_im': s5_b_im,
        's5_c_re': s5_c_re, 's5_c_im': s5_c_im, 's5_d': s5_d,
        's5_w_glu': s5_w_glu, 's5_w_out': s5_w_out,
        'mix_pre_gain': mix_pre_gain, 'mix_post_gain': mix_post_gain,
        'ffn_pre_gain': ffn_pre_gain, 'ffn_post_gain': ffn_post_gain,
        'ffn_w_gate': ffn_w_gate, 'ffn_w_up': ffn_w_up, 'ffn_w_down': ffn_w_down,
    }

def second_block(x, fox_w_in, fox_b_f, fox_q_gain, fox_k_gain, fox_w_out,
              s5_w_in, s5_log_dt, s5_lam_re, s5_lam_im, s5_b_re, s5_b_im,
              s5_c_re, s5_c_im, s5_d, s5_w_glu, s5_w_out,
              mix_pre_gain, mix_post_gain, ffn_pre_gain, ffn_post_gain,
              ffn_w_gate, ffn_w_up, ffn_w_down):
    for i in range(DEPTH_2):
        j = i // N_MIXERS
        h = rmsnorm(x, mix_pre_gain[i])
        if i % N_MIXERS == 0:
            m = fox_mixer(h, fox_w_in[j], fox_b_f[j], fox_q_gain[j], fox_k_gain[j], fox_w_out[j])
        else:
            m = s5_mixer(h, s5_w_in[j], s5_log_dt[j], s5_lam_re[j], s5_lam_im[j],
                         s5_b_re[j], s5_b_im[j], s5_c_re[j], s5_c_im[j], s5_d[j],
                         s5_w_glu[j], s5_w_out[j])
        x = x + rmsnorm(m, mix_post_gain[i])
        h = rmsnorm(x, ffn_pre_gain[i])
        x = x + rmsnorm(swiglu(h, ffn_w_gate[i], ffn_w_up[i], ffn_w_down[i]), ffn_post_gain[i])
    return x


def setup_inputs(seed=0):
    out = dict(first_inputs(seed))
    for name, value in second_inputs(seed + 1).items():
        if name != "x":
            out[name + "_2"] = value
    return out


def reference(
    x, norm1_g, w_in, glu_b, q_norm_g, k_norm_g, dw_w, dw_b, conv_ln_g, conv_ln_b, w_out,
    norm2_g, w_gate, w_up, w_down, fox_w_in_2, fox_b_f_2, fox_q_gain_2, fox_k_gain_2,
    fox_w_out_2, s5_w_in_2, s5_log_dt_2, s5_lam_re_2, s5_lam_im_2, s5_b_re_2, s5_b_im_2,
    s5_c_re_2, s5_c_im_2, s5_d_2, s5_w_glu_2, s5_w_out_2, mix_pre_gain_2, mix_post_gain_2,
    ffn_pre_gain_2, ffn_post_gain_2, ffn_w_gate_2, ffn_w_up_2, ffn_w_down_2,
):
    x = first_block(
        x, norm1_g, w_in, glu_b, q_norm_g, k_norm_g, dw_w, dw_b, conv_ln_g, conv_ln_b, w_out,
        norm2_g, w_gate, w_up, w_down,
    )
    return second_block(
        x, fox_w_in_2, fox_b_f_2, fox_q_gain_2, fox_k_gain_2, fox_w_out_2, s5_w_in_2,
        s5_log_dt_2, s5_lam_re_2, s5_lam_im_2, s5_b_re_2, s5_b_im_2, s5_c_re_2, s5_c_im_2,
        s5_d_2, s5_w_glu_2, s5_w_out_2, mix_pre_gain_2, mix_post_gain_2, ffn_pre_gain_2,
        ffn_post_gain_2, ffn_w_gate_2, ffn_w_up_2, ffn_w_down_2,
    )


_drawn_inputs = setup_inputs


def setup_inputs(seed=0):
    import zlib

    import numpy as np

    out = dict(_drawn_inputs(seed))
    spreads = {}
    factors = {'norm1_g': 3.243,
     'glu_b': 3.31,
     'q_norm_g': 8.0,
     'k_norm_g': 8.0,
     'conv_ln_g': 3.288,
     'conv_ln_b': 3.356,
     'norm2_g': 2.704,
     'fox_q_gain_2': 4.9,
     'fox_k_gain_2': 4.862,
     's5_lam_re_2': 200.0,
     'mix_post_gain_2': 12.055,
     'ffn_pre_gain_2': 7.476,
     'ffn_post_gain_2': 42.208,
     's5_log_dt_2': 54.784,
     's5_lam_im_2': 50.032,
     's5_b_re_2': 64.0,
     's5_b_im_2': 64.0,
     's5_c_re_2': 64.0,
     's5_c_im_2': 64.0}
    for name, (base, spread) in spreads.items():
        noise = np.random.default_rng([zlib.crc32(name.encode()), seed]).standard_normal(out[name].shape)
        drawn = base * np.exp(spread * noise) if base else spread * noise
        out[name] = jnp.asarray(drawn.astype(out[name].dtype))
    for name, factor in factors.items():
        out[name] = (out[name] * factor).astype(out[name].dtype)
    return out
```

```python
import math
from contextlib import ExitStack

import numpy as np

import concourse.bass as bass
from concourse import mybir

F32 = mybir.dt.float32
F32R = mybir.dt.float32r
BF16 = mybir.dt.bfloat16
ACT = mybir.ActivationFunctionType
ALU = mybir.AluOpType
AX = mybir.AxisListType

P = 128
TOK = 256
RT = TOK // P
D = 1024
KT = D // P
DFF = 2816
FT = DFF // P
FP = FT // 2
EPS = 1e-6
HD = 64
H1 = 8
H2 = 16
AW = H1 * HD
TAPS = 31
NG = 64
SC = 16
T = 8
NCH = TOK // T
GB = 4
NBLK = NG // GB
UNIT = 2048
RAW = 4
RING = 2
NEG = -3.0e38


class Program:
    def __init__(self, nc, ctx, io):
        self.nc, self.ctx, self.io = nc, ctx, io
        self.sems = {}
        self.plan_units()
        self.place()

    KINDS = {
        "nat_ready": (("n1", "ao", "f1", "fp", "fo", "f2", "s", "yg", "yo", "f3"), 2),
        "transposed": (("n1", "ao", "f1", "fp", "fo", "f2", "s", "yg", "yo", "f3"), 8),
        "high_ready": (("n1", "ao", "f1", "fp", "fo", "f2", "s", "yg", "yo", "f3"), 8),
        "act_ready": (("n1", "ao", "f1", "fp", "fo", "f2", "s", "yg", "yo", "f3"), 8),
        "squares": (("n1", "f1", "fp", "pm0", "f2", "pf0", "s", "pm1", "f3", "pf1"), 2),
        "head_sums": (("q", "k", "ln", "blk0", "blk1", "blk2", "blk3"), 1),
        "var": (("n1", "q", "k", "ln", "f1", "fp", "blk0", "blk1", "blk2", "blk3", "pm0", "f2", "pf0", "s",
                 "pm1", "f3", "pf1"), 1),
        "rstd": (("n1", "q", "k", "ln", "f1", "fp", "blk0", "blk1", "blk2", "blk3", "pm0", "f2", "pf0", "s",
                  "pm1", "f3", "pf1"), 1),
        "x_ready": (("f1", "fp", "pm0", "pf0", "pm1", "pf1"), 2),
        "normed": (("pm0", "pf0", "pm1", "pf1"), 2),
        "sq": (("q", "k", "blk0", "blk1", "blk2", "blk3"), 2),
        "silu": (("f1", "f2", "f3"), FP), "prod": (("f1", "f2", "f3"), FP),
        "ghigh": (("f1", "f2", "f3"), FP), "glow": (("f1", "f2", "f3"), FP),
        "probs": (("a1", "a2"), {"a1": 2 * H1, "a2": 2 * H2}), "max": (("a1", "a2"), {"a1": 2 * H1, "a2": 2 * H2}),
        "scores": (("a1", "a2"), {"a1": H1, "a2": H2}), "turned": (("a1", "a2"), {"a1": H1, "a2": H2}),
        "pt": (("a1", "a2"), {"a1": H1, "a2": H2}), "out": (("a1", "a2"), {"a1": H1, "a2": H2}),
        "heads_in": (("a1", "a2"), {"a1": H1, "a2": H2}), "heads_out": (("a1", "a2"), {"a1": H1, "a2": H2}),
    }

    def resolve(self, name):
        stage, _, kind = name.partition("_")
        stages, count = self.KINDS.get(kind, ((), 0))
        if stage not in stages:
            return name, 0
        counts = {s: count[s] if isinstance(count, dict) else count for s in stages}
        if kind in ("transposed", "high_ready", "act_ready"):
            counts["ao"] = KT // 2
        return "all_" + kind, sum(counts[s] for s in stages[:stages.index(stage)])

    def sem(self, name):
        shared, _ = self.resolve(name)
        if shared not in self.sems:
            self.sems[shared] = self.ctx.enter_context(self.nc.semaphore(shared))
        return self.sems[shared]

    def past(self, name, value):
        return self.sem(name), self.resolve(name)[1] + value

    def plan_units(self):
        io = self.io
        self.units = []
        self.first = {}

        def rows_by(w, cols, width):
            return w[:, cols:cols + width].rearrange("(k p) c -> p k c", p=P)

        def feature_pairs(name, w, c0, n):
            self.first[name] = len(self.units)
            for i in range(n):
                self.units.append((rows_by(w, c0 + 256 * i, 256), 8))

        def half_k(name, w, c0, blocks):
            self.first[name] = len(self.units)
            for b in range(blocks):
                for hk in range(2):
                    v = w[hk * 512:(hk + 1) * 512, c0 + 512 * b:c0 + 512 * b + 512]
                    self.units.append((v.rearrange("(k p) c -> p k c", p=P), 4))

        def k_pairs(name, w, n):
            self.first[name] = len(self.units)
            for i in range(n):
                self.units.append((w[i * 256:(i + 1) * 256, :].rearrange("(k p) c -> p k c", p=P), 2))

        def ffn(name, wg, wu, wd):
            self.first[name + ".up"] = len(self.units)
            for f in range(FP):
                self.units.append((rows_by(wg, 256 * f, 256), 8))
                self.units.append((rows_by(wu, 256 * f, 256), 8))
            k_pairs(name + ".down", wd, FT // 2)

        w_in = io["w_in"][0]
        feature_pairs("u", w_in, 3 * AW, 4)
        half_k("q", w_in, 0, 1)
        half_k("k", w_in, AW, 1)
        half_k("v", w_in, 2 * AW, 1)
        k_pairs("o1", io["w_out"][0], 4)
        ffn("f1", io["w_gate"][0], io["w_up"][0], io["w_down"][0])
        fox = io["fox_w_in_2"][0]
        half_k("fk", fox, D, 2)
        half_k("fq", fox, 0, 2)
        half_k("fv", fox, 2 * D, 2)
        half_k("fg", fox, 3 * D, 2)
        k_pairs("o2", io["fox_w_out_2"][0], 4)
        ffn("f2", io["ffn_w_gate_2"][0], io["ffn_w_up_2"][0], io["ffn_w_down_2"][0])
        half_k("s", io["s5_w_in_2"][0], 0, 2)
        k_pairs("glu", io["s5_w_glu_2"][0], 4)
        k_pairs("o3", io["s5_w_out_2"][0], 4)
        ffn("f3", io["ffn_w_gate_2"][1], io["ffn_w_up_2"][1], io["ffn_w_down_2"][1])

    def place(self):
        nc, ctx = self.nc, self.ctx
        end = nc.sbuf_usable_end
        cur = (nc.sbuf_base + 63) // 64 * 64
        self.region_end = end

        def at(name, shape, dt, offset):
            return nc.alloc_sbuf_tensor_at(name, shape, dt, offset=offset)

        def fixed(name, shape, dt):
            nonlocal cur
            t = at(name, shape, dt, cur)
            self.where[name] = cur
            cur += (int(np.prod(shape[1:])) * (2 if dt == BF16 else 4) + 31) // 32 * 32
            return t

        self.where = {}
        self.x = fixed("x_res", [P, RT, D], F32)
        self.nat = fixed("nat", [P, RT, D], F32)
        self.actH = fixed("actH", [P, KT, TOK], F32R)
        self.actL = fixed("actL", [P, KT, TOK], F32R)
        self.wraw = fixed("wraw", [P, RAW, UNIT], F32)
        self.whi = fixed("whi", [P, RING, UNIT], F32R)
        self.wlo = fixed("wlo", [P, RING, UNIT], F32R)
        self.gb = [fixed(f"postgain{i}", [P, D], F32) for i in range(2)]
        self.ident = fixed("ident", [P, P], F32)
        self.ones = fixed("ones", [P, P], F32)
        self.tri = fixed("tri", [P, P], F32)
        self.swap = fixed("swap", [P, P], F32)
        self.identb = fixed("identb", [P, P], BF16)
        self.maskb = fixed("maskb", [P, P], BF16)
        self.vec = fixed("vec", [P, 68], F32)
        self.taps = fixed("taps", [P, TAPS * 4], F32)
        self.mhalf = fixed("mhalf", [P, 16], F32)
        self.halfpi = fixed("halfpi", [P, 1], F32)
        self.zero1 = fixed("zero1", [P, 1], F32)
        self.ss = fixed("ss", [P, 16], F32)
        self.rs = fixed("rs", [P, 16], F32)
        self.cosT = fixed("cosT", [P, NG], F32)
        self.sinT = fixed("sinT", [P, NG], F32)
        self.magT = fixed("magT", [P, NG], F32)
        self.qkg = fixed("qkg", [P, 4, HD], F32)
        self.nmax, self.rsum, self.rinv = (fixed(n, [P, RT, H2], F32) for n in ("nmax", "rsum", "rinv"))
        R0 = cur

        class Pen:
            def __init__(s, base, top=end):
                s.cur, s.top = base, top

            def __call__(s, name, shape, dt=F32):
                t = at(name, shape, dt, s.cur)
                self.where[name] = s.cur
                s.cur += (int(np.prod(shape[1:])) * (2 if dt == BF16 else 4) + 31) // 32 * 32
                assert s.cur <= s.top, (name, s.cur, s.top)
                return t

        prep_bytes = 4 * 4096 + 2 * 2304 + 2 * 2048
        work_bytes = 2 * 2048 + 2304 + 2 * 2304 + 2 * 2048 + 2 * 4096
        W0 = end - end % 32 - work_bytes
        P0 = W0 - prep_bytes
        pen = Pen(P0, W0)
        self.BB1, self.BB2 = pen("BB1", [P, NG, SC]), pen("BB2", [P, NG, SC])
        self.C1, self.C2 = pen("C1", [P, NG, SC]), pen("C2", [P, NG, SC])
        self.F1, self.F2 = pen("F1", [P, NG, T + 1]), pen("F2", [P, NG, T + 1])
        self.G1, self.G2 = pen("G1", [P, NG, T]), pen("G2", [P, NG, T])
        pen = Pen(W0)
        self.rtb = pen("rtb", [P, 2, GB, T, SC])
        self.ob = pen("ob", [P, 2, GB, T + 1, SC])
        self.otmp = pen("otmp", [P, GB, T + 1, SC])
        self.rsb = pen("rsb", [P, 2, GB, P])
        self.ksb = pen("ksb", [SC, 2, GB, 2 * P])
        pen = Pen(W0)
        self.Bre, self.Bim = pen("Bre", [P, NG, SC]), pen("Bim", [P, NG, SC])
        self.cnat = pen("cnat", [P, 2, 8, 2, HD])
        self.btmp = pen("btmp", [P, NG, SC])
        self.BASELEFT = pen.cur
        pen = Pen(W0)
        self.AR, self.AI = pen("AR", [P, NG, T + 1]), pen("AI", [P, NG, T + 1])
        self.atmp, self.atmp2 = pen("atmp", [P, NG, 4]), pen("atmp2", [P, NG, 4])
        pen = Pen(self.where["postgain0"], self.where["postgain0"] + 8192)
        self.small = {n: pen("s5_" + n, [P, NG]) for n in
                      ("LR LI ldt dt lr th k t thr ab sh tt lrc lrb eb r1 r2 den rden em ar ai nre zr zi "
                       "m1").split()}

        pen = Pen(R0, P0)
        self.hpad = pen("hpad", [P, 4, TAPS - 1 + TOK])
        self.cacc = pen("cacc", [P, 4, TOK])
        self.csig = pen("csig", [P, 4, TOK])
        self.qn, self.kn = pen("qn", [P, RT, AW]), pen("kn", [P, RT, AW])
        self.vn = pen("vn", [P, RT, AW])
        self.qt, self.kt1 = pen("qt1", [HD, H1, TOK]), pen("kt1", [HD, H1, TOK])
        self.p1 = pen("p1", [P, 2, 384])
        self.pt1 = pen("pt1", [P, 2, 384])
        self.ropeg = pen("ropeg", [P, 2, RT, 2, HD])
        self.sq1 = at("sq1", [P, RT, AW], F32, self.where["csig"])
        self.csq = at("csq", [P, 4, TOK], F32, self.where["csig"])
        self.rope = at("rope", [P, RT, 2, HD], F32, self.where["pt1"] + 2048)
        self.vrows = at("vrows", [68, P], F32, self.where["actH"])
        self.taprows = at("taprows", [TAPS * 4, P], F32, self.where["actH"] + 512)
        self.lamnat = at("lamnat", [NG, 2, 2, NG], F32, self.where["actH"] + 1024)
        self.diag = at("diag", [P, 2 * P], F32, self.where["p1"])
        self.rtmp = at("rtmp", [P, AW], F32, self.where["p1"])
        self.rtmp2 = at("rtmp2", [P, AW], F32, self.where["pt1"])

        pen = Pen(R0, P0)
        self.gH, self.gL = pen("gH", [P, FT, TOK], F32R), pen("gL", [P, FT, TOK], F32R)
        self.sg = pen("sg", [P, 2 * TOK])
        self.prod = pen("prod", [P, 2 * TOK])

        pen = Pen(R0)
        AUG = HD + 2
        self.qa, self.ka = pen("qa", [P, RT, H2, AUG]), pen("ka", [P, RT, H2, AUG])
        self.va = pen("va", [P, RT, D])
        self.ga = pen("ga", [P, RT, D])
        self.qt2, self.kt2 = pen("qt2", [AUG, H2, TOK]), pen("kt2", [AUG, H2, TOK])
        self.p2, self.pt2 = pen("p2", [P, 2, 384]), pen("pt2", [P, 2, 384])
        self.sq2 = pen("sq2", [P, RT, 512])
        self.wf = pen("wf", [P, KT, H2])
        self.wfH, self.wfL = pen("wfH", [P, KT, H2], F32R), pen("wfL", [P, KT, H2], F32R)
        self.fb = pen("fb", [P, H2])
        self.fl = pen("fl", [P, 4, RT, H2])

        pen = Pen(R0)
        self.RTab = pen("RTab", [P, NG, P])
        self.OTab = pen("OTab", [P, NG, P])
        self.Uall = pen("Uall", [P, 16, 4, NCH])
        self.CT, self.ST = pen("CT", [P, NG, NCH]), pen("ST", [P, NG, NCH])
        d0 = pen.cur
        self.D0 = pen("D0", [P, NG, NCH])
        self.X33 = at("X33", [P, NG, NCH + 1], F32, d0)
        self.dsk = self.gb[1]
        self.TTab = at("TTab", [P, NG, P], F32, R0)
        self.sgl = at("sgl", [P, RT, D], F32, R0)
        self.V = at("Vst", [P, NG, NCH], F32, self.where["actH"])
        self.W = at("Wst", [P, NG, NCH], F32, self.where["actL"])
        self.Un = at("Un", [P, T, 16, SC], F32, self.where["actH"])
        self.Ur = at("Ur", [P, 16, T, SC], F32, self.where["actL"])
        self.Ysb = at("Ysb", [P, T, 16, SC], F32, self.where["actH"])
        self.ud = at("ud", [P, RT, D], F32, self.where["actL"])
        self.ctmp1 = at("ctmp1", [P, NG, 16], F32, self.where["Uall"])
        self.ctmp2 = at("ctmp2", [P, NG, 16], F32, self.where["Uall"] + 4096)

        self.ps = ctx.enter_context(nc.psum_tensor("ps", [P, 8, 512], F32))
        dr = lambda n, s: nc.dram_tensor(n, s, F32, kind="Internal").ap()
        self.Rd, self.Od = dr("R_dram", [P, NG, P]), dr("O_dram", [P, NG, P])
        self.Kd = dr("K_dram", [SC, NG, 2 * P])
        self.ud_d, self.yd_d = dr("u_dram", [TOK, D]), dr("y_dram", [TOK, D])
        s = self.sem
        self.landed = [s(f"raw_landed{i}") for i in range(RAW)]
        self.hi_done, self.lo_done, self.used = s("hi_done"), s("lo_done"), s("unit_used")

    def load_unit(self, sp, n0, view, it=0):
        n = n0 + 4 * it
        if n0 >= RAW:
            sp.wait_ge(self.lo_done, n - RAW + 1)
        k = view.shape[1]
        dst = self.wraw[:, n0 % RAW, :].rearrange("p (k c) -> p k c", k=k)
        sp.dma_start(dst, view).then_inc(self.landed[n0 % RAW], 16)

    def split_high(self, act, n0, it=0):
        n = n0 + 4 * it
        act.wait_ge(self.landed[n0 % RAW], 16 * (n0 // RAW + 1) + 16 * it)
        if n0 >= RING:
            act.wait_ge(self.used, n - RING + 1)
        act.activation(self.whi[:, n0 % RING, :], self.wraw[:, n0 % RAW, :], ACT.Copy).then_inc(self.hi_done, 1)

    def split_low(self, dve, n0, it=0):
        n = n0 + 4 * it
        dve.wait_ge(self.hi_done, n + 1)
        dve.tensor_tensor(self.wlo[:, n0 % RING, :], self.wraw[:, n0 % RAW, :],
                          self.whi[:, n0 % RING, :].bitcast(F32), ALU.subtract).then_inc(self.lo_done, 1)

    def mm_features(self, pe, n0, bank, it=0, ready=None):
        pe.wait_ge(self.lo_done, n0 + 4 * it + 1)
        s = n0 % RING
        for f in range(2):
            out = self.ps[:, bank, f * TOK:(f + 1) * TOK]
            for k in range(KT):
                if ready is not None and f == 0:
                    pe.wait_ge(*self.past(ready, k + 1))
                c = k * 256 + f * P
                wh, wl = self.whi[:, s, c:c + P], self.wlo[:, s, c:c + P]
                pe.matmul(out, wh, self.actH[:, k, :], start=(k == 0), stop=False)
                pe.matmul(out, wh, self.actL[:, k, :], start=False, stop=False)
                last = pe.matmul(out, wl, self.actH[:, k, :], start=False, stop=(k == KT - 1))
        last.then_inc(self.used, 1)

    def mm_half_k(self, pe, n0, banks, half, ready=None):
        pe.wait_ge(self.lo_done, n0 + 1)
        s = n0 % RING
        for k in range(4):
            ka = 4 * half + k
            if ready is not None:
                pe.wait_ge(*self.past(ready, ka + 1))
            wh, wl = self.whi[:, s, k * 512:(k + 1) * 512], self.wlo[:, s, k * 512:(k + 1) * 512]
            for r in range(RT):
                out = self.ps[:, banks[r], :]
                xh, xl = self.actH[:, ka, r * P:(r + 1) * P], self.actL[:, ka, r * P:(r + 1) * P]
                pe.matmul(out, xh, wh, start=(ka == 0), stop=False)
                pe.matmul(out, xh, wl, start=False, stop=False)
                last = pe.matmul(out, xl, wh, start=False, stop=(ka == KT - 1))
        last.then_inc(self.used, 1)

    def mm_k_pair(self, pe, n0, base, xh, xl, k0, kn, waits=()):
        pe.wait_ge(self.lo_done, n0 + 1)
        s = n0 % RING
        for k in range(2):
            for name, value in waits:
                pe.wait_ge(*self.past(name, value + k))
            for r in range(RT):
                h, l = xh[:, k0 + k, r * P:(r + 1) * P], xl[:, k0 + k, r * P:(r + 1) * P]
                w = [[t[:, s, k * 1024 + c * 512:k * 1024 + (c + 1) * 512] for c in range(2)]
                     for t in (self.whi, self.wlo)]
                st, sp_ = k0 + k == 0, k0 + k == kn - 1
                for c in range(2):
                    pe.matmul(self.ps[:, base + 2 * r + c, :], h, w[0][c], start=st, stop=False)
                for c in range(2):
                    pe.matmul(self.ps[:, base + 2 * r + c, :], h, w[1][c], start=False, stop=False)
                for c in range(2):
                    last = pe.matmul(self.ps[:, base + 2 * r + c, :], l, w[0][c], start=False, stop=sp_)
        last.then_inc(self.used, 1)

    def tp_spot(self, kt, banks):
        b, h = banks[kt % len(banks)], kt // len(banks)
        return self.ps[:, b, h * TOK:(h + 1) * TOK]

    def pe_turn(self, pe, st, banks, n=KT, natural_ready=None):
        tp = self.sem(st + "_transposed")
        for kt in range(n):
            if kt >= len(banks):
                pe.wait_ge(*self.past(st + "_act_ready", kt - len(banks) + 1))
            for r in range(RT):
                if kt == 0:
                    pe.wait_ge(*self.past(st + "_nat_ready", r + 1))
                last = pe.transpose(self.tp_spot(kt, banks)[:, r * P:(r + 1) * P],
                                    self.nat[:, r, kt * P:(kt + 1) * P], self.ident[:])
            last.then_inc(tp, 1)

    def act_turn(self, act, st, banks, n=KT, gain=None):
        for kt in range(n):
            act.wait_ge(*self.past(st + "_transposed", kt + 1))
            g = 1.0 if gain is None else self.vec[:, gain + kt:gain + kt + 1]
            act.activation(self.actH[:, kt, :], self.tp_spot(kt, banks), ACT.Copy, scale=g)\
               .then_inc(self.sem(st + "_high_ready"), 1)

    def dve_turn(self, dve, st, banks, n=KT, gain=None):
        for kt in range(n):
            dve.wait_ge(*self.past(st + "_high_ready", kt + 1))
            hi = self.actH[:, kt, :].bitcast(F32)
            if gain is None:
                i = dve.tensor_tensor(self.actL[:, kt, :], self.tp_spot(kt, banks), hi, ALU.subtract)
            else:
                i = dve.scalar_tensor_tensor(self.actL[:, kt, :], self.tp_spot(kt, banks),
                                             self.vec[:, gain + kt:gain + kt + 1], hi, ALU.mult, ALU.subtract)
            i.then_inc(self.sem(st + "_act_ready"), 1)

    def act_squares(self, act, st, src, ready=None, values=None):
        for r in range(RT):
            if ready is not None:
                act.wait_ge(*self.past(ready, values[r]))
            act.activation(self.nat[:, r, :], src(r), ACT.Square, accum_out=self.ss[:, r:r + 1])\
               .then_inc(self.sem(st + "_squares"), 1)

    def pool_rstd(self, pool, st, n, mean_of, ready, value):
        pool.wait_ge(*self.past(ready, value))
        pool.tensor_scalar(self.rs[:, 0:n], self.ss[:, 0:n], 1.0 / mean_of, EPS, ALU.mult, ALU.add)\
            .then_inc(self.sem(st + "_var"), 1)
        pool.wait_ge(*self.past(st + "_var", 1))
        pool.tensor_tensor(self.rs[:, 0:n], self.rs[:, 0:n], self.mhalf[:, 0:n], ALU.pow)\
            .then_inc(self.sem(st + "_rstd"), 1)

    def dve_scale(self, dve, st):
        dve.wait_ge(*self.past(st + "_rstd", 1))
        for r in range(RT):
            dve.tensor_scalar(self.nat[:, r, :], self.x[:, r, :], self.rs[:, r:r + 1], None, ALU.mult)\
               .then_inc(self.sem(st + "_nat_ready"), 1)

    def acc_row(self, base, r):
        return self.ps[:, base + 2 * r:base + 2 * r + 2, :]

    def dve_postnorm(self, dve, st, base, gain, gain_ready, gain_value):
        dve.wait_ge(*self.past(st + "_rstd", 1))
        dve.wait_ge(*self.past(gain_ready, gain_value))
        g = gain[:].rearrange("p (a b) -> p a b", a=2)
        for r in range(RT):
            t = self.nat[:, r, :].rearrange("p (a b) -> p a b", a=2)
            dve.scalar_tensor_tensor(t, self.acc_row(base, r), self.rs[:, r:r + 1], g, ALU.mult, ALU.mult)\
               .then_inc(self.sem(st + "_normed"), 1)
        for r in range(RT):
            dve.wait_ge(*self.past(st + "_normed", r + 1))
            dve.tensor_tensor(self.x[:, r, :], self.x[:, r, :], self.nat[:, r, :], ALU.add)\
               .then_inc(self.sem(st + "_x_ready"), 1)

    def ffn_banks(self, a):
        return a, a + 1, (4 if a == 0 else 0)

    def pe_pair(self, pe, st, n0, a, f0, it=0, f_step=0, ready=None):
        f = f0 + f_step * it
        if f0 > 0:
            pe.wait_ge(*self.past(st + "_silu", f))
        self.mm_features(pe, n0, a, it, ready)
        if f0 > 0:
            pe.wait_ge(*self.past(st + "_prod", f))
        self.mm_features(pe, n0 + 1, a + 1, it)

    def act_pair(self, act, st, n0, a, f0, it=0, f_step=0):
        f = f0 + f_step * it
        act.wait_ge(self.used, n0 + 4 * it + 1)
        if f0 > 0:
            act.wait_ge(*self.past(st + "_prod", f))
        act.activation(self.sg[:], self.ps[:, a, :], ACT.Silu).then_inc(self.sem(st + "_silu"), 1)
        self.split_high(act, n0 + 2, it)
        self.split_high(act, n0 + 3, it)
        act.wait_ge(*self.past(st + "_prod", f + 1))
        dst = self.gH[:, bass.ds(2 * f, 2), :] if f_step else self.gH[:, 2 * f:2 * f + 2, :]
        act.activation(dst, self.prod[:].rearrange("p (a b) -> p a b", a=2), ACT.Copy)\
           .then_inc(self.sem(st + "_ghigh"), 1)

    def dve_pair(self, dve, st, n0, a, f0, it=0, f_step=0):
        f = f0 + f_step * it
        self.split_low(dve, n0 + 2, it)
        dve.wait_ge(self.used, n0 + 4 * it + 2)
        dve.wait_ge(*self.past(st + "_silu", f + 1))
        if f0 > 0:
            dve.wait_ge(*self.past(st + "_glow", f))
        dve.tensor_tensor(self.prod[:], self.sg[:], self.ps[:, a + 1, :], ALU.mult)\
           .then_inc(self.sem(st + "_prod"), 1)
        self.split_low(dve, n0 + 3, it)
        dve.wait_ge(*self.past(st + "_ghigh", f + 1))
        hi = self.gH[:, bass.ds(2 * f, 2), :] if f_step else self.gH[:, 2 * f:2 * f + 2, :]
        lo = self.gL[:, bass.ds(2 * f, 2), :] if f_step else self.gL[:, 2 * f:2 * f + 2, :]
        dve.tensor_tensor(lo, self.prod[:].rearrange("p (a b) -> p a b", a=2), hi.bitcast(F32), ALU.subtract)\
           .then_inc(self.sem(st + "_glow"), 1)

    def over_pairs(self, eng, one, prep=None):
        one(0, 0, 0, 0)
        if prep:
            prep(0, 0, 0)
        with eng.Fori(0, (FP - 1) // 2) as it:
            for j in range(2):
                one(2 + 2 * j, 1 + j, it, 2)
                if prep:
                    prep(1 + j, it, 2)

    def pe_ffn(self, pe, st, a, prep=False):
        n = self.first[st + ".up"]
        act_ready = st + "_act_ready"
        self.over_pairs(pe, lambda dn, f0, it, fs: self.pe_pair(
            pe, st, n + dn, a, f0, it, fs, act_ready if dn == 0 else None),
            (lambda b0, it, bs: self.pe_prep(pe, a, b0, it, bs)) if prep else None)
        n = self.first[st + ".down"]
        base = self.ffn_banks(a)[2]
        for i in range(FT // 2):
            if i == 0:
                pe.wait_ge(*self.past(act_ready, KT))
            pe.wait_ge(*self.past(st + "_glow", i + 1))
            self.mm_k_pair(pe, n + i, base, self.gH, self.gL, 2 * i, FT)
            if prep and i % 2 == 1:
                self.pe_prep(pe, a, FP + i // 2)

    def act_ffn(self, act, st, a, prep=False):
        n = self.first[st + ".up"]
        self.over_pairs(act, lambda dn, f0, it, fs: self.act_pair(act, st, n + dn, a, f0, it, fs),
                        (lambda b0, it, bs: self.act_prep(act, a, b0, it, bs)) if prep else None)
        n = self.first[st + ".down"]
        for i in range(FT // 2):
            if n + i + 2 < len(self.units) and i < FT // 2 - 1:
                self.split_high(act, n + i + 2)
            if prep and i % 2 == 1:
                self.act_prep(act, a, FP + i // 2)

    def dve_ffn(self, dve, st, a):
        n = self.first[st + ".up"]
        self.over_pairs(dve, lambda dn, f0, it, fs: self.dve_pair(dve, st, n + dn, a, f0, it, fs))
        n = self.first[st + ".down"]
        for i in range(FT // 2 - 1):
            if n + i + 2 < len(self.units):
                self.split_low(dve, n + i + 2)

    def pool_prep(self, pool, b0, it=0, step=0):
        b = b0 + step * it
        half = b0 // 2 + it if step else b0 // 2
        done = self.sem("prep_pool")
        s = b0 % 2
        if b0 > 0:
            pool.wait_ge(*self.past("prep_kmul", b if b0 == 1 else b - 1))
            pool.wait_ge(*self.past(f"prep_stored{s}", 48 * half + 1))
        g = bass.ds(GB * b, GB) if step else slice(GB * b, GB * b + GB)

        def times(out, f, w, n):
            return pool.tensor_tensor(out, f[:, g, :].unsqueeze(3).to_broadcast([P, GB, n, SC]),
                                      w[:, g, :].unsqueeze(2).to_broadcast([P, GB, n, SC]), ALU.mult)

        if b0 > 0:
            pool.wait_ge(done, 6 * b)
        r, o, t = self.rtb[:, s], self.ob[:, s], self.otmp
        times(r, self.G1, self.BB1, T).then_inc(done, 1)
        times(t[:, :, 0:T, :], self.G2, self.BB2, T).then_inc(done, 1)
        pool.wait_ge(done, 6 * b + 2)
        pool.tensor_tensor(r, r, t[:, :, 0:T, :], ALU.add).then_inc(done, 1)
        times(o, self.F1, self.C1, T + 1).then_inc(done, 1)
        pool.wait_ge(done, 6 * b + 3)
        times(t[:], self.F2, self.C2, T + 1).then_inc(done, 1)
        pool.wait_ge(done, 6 * b + 5)
        pool.tensor_tensor(o, o, t[:], ALU.add).then_inc(done, 1)

    def pe_prep(self, pe, a, b0, it=0, step=0):
        b = b0 + step * it
        s = b0 % 2
        pe.wait_ge(*self.past("prep_pool", 6 * b + 6))
        if b0 > 0:
            pe.wait_ge(*self.past("prep_rout", b))
            pe.wait_ge(*self.past("prep_kout", b))
        for i in range(GB):
            last = pe.transpose(self.ps[:, a + 2, i * P:(i + 1) * P],
                                self.rtb[:, s, i, :, :].rearrange("p t c -> p (t c)"), self.ident[:])
        last.then_inc(self.sem("prep_turned"), 1)
        for i in range(GB):
            last = pe.matmul(self.ps[0:SC, a + 3, i * P:(i + 1) * P], self.rtb[:, s, i, T - 1, :],
                             self.ob[:, s, i, 0:T, :].rearrange("p t c -> p (t c)"), start=True, stop=True)
        last.then_inc(self.sem("prep_kmul"), 1)

    def act_prep(self, act, a, b0, it=0, step=0):
        b = b0 + step * it
        half = b0 // 2 + it if step else b0 // 2
        s = b0 % 2
        act.wait_ge(*self.past("prep_turned", b + 1))
        act.wait_ge(*self.past(f"prep_stored{s}", 48 * half + 1))
        act.activation(self.rsb[:, s], self.ps[:, a + 2, :].rearrange("p (i c) -> p i c", i=GB), ACT.Copy)\
           .then_inc(self.sem("prep_rout"), 1)
        act.wait_ge(*self.past("prep_kmul", b + 1))
        act.activation(self.ksb[:, s, :, P:2 * P],
                       self.ps[0:SC, a + 3, :].rearrange("p (i c) -> p i c", i=GB), ACT.Copy)\
           .then_inc(self.sem("prep_kout"), 1)
        act.wait_ge(*self.past("prep_kout", b + 1))
        g = bass.ds(GB * b, GB) if step else slice(GB * b, GB * b + GB)
        stored = self.sem(f"prep_stored{s}")
        act.dma_start(self.Rd[:, g, :], self.rsb[:, s]).then_inc(stored, 16)
        act.dma_start(self.Kd[:, g, :], self.ksb[:, s]).then_inc(stored, 16)
        act.dma_start(self.Od[:, g, :].rearrange("p g (t c) -> p g t c", c=SC),
                      self.ob[:, s, :, 1:T + 1, :]).then_inc(stored, 16)

    def pe_attention(self, pe, st, H, qt, kt, v, p, pt, sb, tb, o_at):
        def scores(h):
            if h >= 2:
                pe.wait_ge(*self.past(st + "_probs", 2 * (h - 1)))
            b = sb[h % 2]
            for r in range(RT):
                c0, nk = (0, P) if r == 0 else (P, 2 * P)
                out = self.ps[:, b, c0:c0 + nk]
                pe.matmul(out, qt[:, h, r * P:(r + 1) * P], kt[:, h, 0:nk], start=True, stop=False)
                last = pe.matmul(self.ps[:, b, c0 + nk - P:c0 + nk], self.identb[:], self.maskb[:],
                                 start=False, stop=True)
            last.then_inc(self.sem(st + "_scores"), 1)

        def turn(h):
            pe.wait_ge(*self.past(st + "_probs", 2 * (h + 1)))
            if h >= 2:
                pe.wait_ge(*self.past(st + "_pt", h - 1))
            for i in range(3):
                last = pe.transpose(self.ps[:, tb[h % 2], i * P:(i + 1) * P], p[:, h % 2, i * P:(i + 1) * P],
                                    self.ident[:])
            last.then_inc(self.sem(st + "_turned"), 1)

        def values(h):
            pe.wait_ge(*self.past(st + "_pt", h + 1))
            for r in range(RT):
                for k in range(r + 1):
                    i = r + k
                    last = pe.matmul(o_at(r, h), pt[:, h % 2, i * P:(i + 1) * P],
                                     v[:, k, h * HD:(h + 1) * HD], start=(k == 0), stop=(k == r))
            last.then_inc(self.sem(st + "_out"), 1)

        for i in range(H + 2):
            if i < H:
                scores(i)
            if 1 <= i <= H:
                turn(i - 1)
            if i >= 2:
                values(i - 2)

    def act_attention(self, act, st, H, p, rsum, nmax, sb):
        for h in range(H):
            act.wait_ge(*self.past(st + "_max", 2 * (h + 1)))
            if h >= 2:
                act.wait_ge(*self.past(st + "_turned", h - 1))
            for r in range(RT):
                c0, nk = (0, P) if r == 0 else (P, 2 * P)
                act.activation(p[:, h % 2, c0:c0 + nk], self.ps[:, sb[h % 2], c0:c0 + nk], ACT.Exp,
                               bias=nmax[:, r, h:h + 1], accum_out=rsum[:, r, h:h + 1])\
                   .then_inc(self.sem(st + "_probs"), 1)

    def dve_attention(self, dve, st, H, pt, nmax, sb, tb, between=None):
        for h in range(H + 1):
            if h < H:
                dve.wait_ge(*self.past(st + "_scores", h + 1))
                for r in range(RT):
                    c0, nk = (0, P) if r == 0 else (P, 2 * P)
                    dve.reduce_max(nmax[:, r, h:h + 1], self.ps[:, sb[h % 2], c0:c0 + nk], AX.X, negate=True)\
                       .then_inc(self.sem(st + "_max"), 1)
            if h >= 1:
                g = h - 1
                dve.wait_ge(*self.past(st + "_turned", g + 1))
                if g >= 2:
                    dve.wait_ge(*self.past(st + "_out", g - 1))
                dve.tensor_copy(pt[:, g % 2, :], self.ps[:, tb[g % 2], 0:384]).then_inc(self.sem(st + "_pt"), 1)
            if between:
                between(h)

    def pe_heads(self, pe, st, name, src, H, ready, value, banks, first_fill):
        pe.wait_ge(*self.past(ready, value))
        w = src.shape[-1]
        for f in range(H // 2):
            n = first_fill + f
            if n >= 2:
                pe.wait_ge(*self.past(st + "_heads_out", n - 1))
            for i in range(2):
                for r in range(RT):
                    c = (2 * i + r) * P
                    last = pe.transpose(self.ps[0:w, banks[n % 2], c:c + P], src[:, r, 2 * f + i, :], self.ident[:])
            last.then_inc(self.sem(st + "_heads_in"), 1)

    def act_heads(self, act, st, dst, H, banks, first_fill):
        w = dst.shape[0]
        for f in range(H // 2):
            n = first_fill + f
            act.wait_ge(*self.past(st + "_heads_in", n + 1))
            act.activation(dst[:, 2 * f:2 * f + 2, :],
                           self.ps[0:w, banks[n % 2], :].rearrange("p (h t) -> p h t", h=2), ACT.Copy)\
               .then_inc(self.sem(st + "_heads_out"), 1)


class Chain:

    def __init__(self, eng, sem):
        self.eng, self.sem, self.n = eng, sem, 0

    def step(self, ins):
        ins.then_inc(self.sem, 1)
        self.n += 1
        return self.n

    def wait(self, n=None):
        self.eng.wait_ge(self.sem, self.n if n is None else n)

    def __call__(self, ins):
        self.step(ins)
        self.wait()


def pool_constants(m, pool):
    c = Chain(pool, m.sem("pool_chain"))
    for t, v in ((m.ident, 0.0), (m.ones, 1.0), (m.tri, 1.0), (m.swap, 0.0), (m.identb, 0.0), (m.maskb, 0.0),
                 (m.mhalf, -0.5), (m.halfpi, math.pi / 2), (m.hpad[:, :, 0:TAPS - 1], 0.0)):
        c.step(pool.memset(t[:] if not isinstance(t, bass.AP) else t, v))
    c.wait()

    def select(t, op, fill, base, step, mult):
        c.step(pool.affine_select(out=t, in_=t, compare_op=op, fill=fill, base=base,
                                  pattern=[[step, t.shape[-1]]], channel_multiplier=mult))

    select(m.ident[:], ALU.not_equal, 1.0, 0, -1, 1)
    select(m.identb[:], ALU.not_equal, 1.0, 0, -1, 1)
    select(m.tri[:], ALU.is_ge, 0.0, 0, 1, -1)
    select(m.maskb[:], ALU.is_ge, NEG, 0, -1, 1)
    select(m.swap[:, 0:64], ALU.not_equal, 1.0, -64, -1, 1)
    select(m.swap[:, 64:128], ALU.not_equal, 1.0, 0, -1, 1)
    c.wait()
    pool.memset(m.zero1[:], 0.0).then_inc(m.sem("consts"), 1)
    return c


def cmul(c, pool, out, x, y, tmp, shape):
    (orr, oi), (xr, xi), (yr, yi) = out, x, y
    t1, t2 = tmp
    c.step(pool.tensor_tensor(orr, xr, yr, ALU.mult))
    c.step(pool.tensor_tensor(t1, xi, yi, ALU.mult))
    c.step(pool.tensor_tensor(oi, xr, yi, ALU.mult))
    c.step(pool.tensor_tensor(t2, xi, yr, ALU.mult))
    c.wait()
    c.step(pool.tensor_tensor(orr, orr, t1, ALU.subtract))
    c.step(pool.tensor_tensor(oi, oi, t2, ALU.add))
    c.wait()


def powers(c, pool, tr, ti, base, tmp1, tmp2, count):
    c.step(pool.memset(tr[:, :, 0:1], 1.0))
    c.step(pool.memset(ti[:, :, 0:1], 0.0))
    c.step(pool.tensor_copy(tr[:, :, 1:2], base[0].unsqueeze(2)))
    c.step(pool.tensor_copy(ti[:, :, 1:2], base[1].unsqueeze(2)))
    c.wait()
    n = 1
    while n < count - 1:
        k = min(n, count - 1 - n)
        b = [t[:, :, n:n + 1].to_broadcast([P, NG, k]) for t in (tr, ti)]
        cmul(c, pool, (tr[:, :, n + 1:n + 1 + k], ti[:, :, n + 1:n + 1 + k]),
             (tr[:, :, 1:1 + k], ti[:, :, 1:1 + k]), b, (tmp1[:, :, 0:k], tmp2[:, :, 0:k]), None)
        n += k


TWO_PI = 2 * math.pi
PI_A = 6.28125
PI_B = math.floor((TWO_PI - PI_A) * 2 ** 21) / 2 ** 21
PI_C = float(np.float32(TWO_PI - PI_A - PI_B))
ROUND = 12582912.0


def pool_s5_scalars(m, c, pool):
    s = {k: v[:] for k, v in m.small.items()}
    pool.wait_ge(*m.past("lam_out", 1))
    pool.wait_ge(*m.past("dt", 1))
    tt, ts = pool.tensor_tensor, pool.tensor_scalar
    c.step(tt(s["lr"], s["LR"], s["dt"], ALU.mult))
    c.step(tt(s["th"], s["LI"], s["dt"], ALU.mult))
    c.wait()
    c.step(ts(s["lrc"], s["lr"], 1.0, None, ALU.min))
    c.step(ts(s["lrb"], s["lr"], 88.0, None, ALU.min))
    c(ts(s["k"], s["th"], 1.0 / TWO_PI, ROUND, ALU.mult, ALU.add))
    c(ts(s["k"], s["k"], ROUND, None, ALU.subtract))
    for i, part in enumerate((PI_A, PI_B, PI_C)):
        c(ts(s["t"], s["k"], part, None, ALU.mult))
        c(tt(s["thr"], s["th"] if i == 0 else s["thr"], s["t"], ALU.subtract))
    ts(s["thr"], s["thr"], 3.1415925, -3.1415925, ALU.min, ALU.max).then_inc(m.sem("angle"), 1)
    c.step(tt(s["den"], s["LR"], s["LR"], ALU.mult))
    c.step(tt(s["m1"], s["LI"], s["LI"], ALU.mult))
    c.wait()
    tt(s["den"], s["den"], s["m1"], ALU.add).then_inc(m.sem("den"), 1)
    pool.wait_ge(*m.past("s5_functions", 5))
    pool.wait_ge(*m.past("s5_recips", 2))
    c.step(ts(s["tt"], s["tt"], 2.0, None, ALU.mult))
    c.step(ts(s["eb"], s["eb"], 1.0, None, ALU.subtract))
    c.step(ts(s["m1"], s["lr"], 1.0, None, ALU.is_gt))
    c.wait()
    c(tt(s["em"], s["tt"], s["r1"], ALU.mult))
    c(tt(s["eb"], s["eb"], s["em"], ALU.subtract))
    c(tt(s["eb"], s["eb"], s["m1"], ALU.mult))
    c(tt(s["em"], s["em"], s["eb"], ALU.add))
    c.step(ts(m.magT[:], s["em"], 1.0, None, ALU.add))
    c.step(tt(s["nre"], s["em"], m.cosT[:], ALU.mult))
    c.step(tt(s["sh"], s["sh"], s["sh"], ALU.mult))
    c.wait()
    c.step(ts(s["sh"], s["sh"], 2.0, None, ALU.mult))
    c.step(tt(s["ar"], m.magT[:], m.cosT[:], ALU.mult))
    c.step(tt(s["ai"], m.magT[:], m.sinT[:], ALU.mult))
    c.wait()
    c(tt(s["nre"], s["nre"], s["sh"], ALU.subtract))
    for out, (a, b), (d, e), op in (("zr", ("nre", "LR"), ("ai", "LI"), ALU.add),
                                    ("zi", ("ai", "LR"), ("nre", "LI"), ALU.subtract)):
        c.step(tt(s[out], s[a], s[b], ALU.mult))
        c(tt(s["t"], s[d], s[e], ALU.mult))
        c(tt(s[out], s[out], s["t"], op))
        c(tt(s[out], s[out], s["rden"], ALU.mult))


def pool_s5_inputs(m, c, pool):
    s = m.small
    pool.wait_ge(*m.past("b_in", 64))
    z = [s[n][:].unsqueeze(2).to_broadcast([P, NG, SC]) for n in ("zr", "zi")]
    cmul2 = ((m.BB1, m.Bre, z[0], m.Bim, z[1], ALU.subtract), (m.BB2, m.Bim, z[0], m.Bre, z[1], ALU.add))
    for out, a, za, b, zb, op in cmul2:
        c.step(pool.tensor_tensor(out[:], a[:], za, ALU.mult))
        c(pool.tensor_tensor(m.btmp[:], b[:], zb, ALU.mult))
        c(pool.tensor_tensor(out[:], out[:], m.btmp[:], op))


def pool_s5_powers(m, c, pool):
    pool.wait_ge(*m.past("c_out", 4))
    powers(c, pool, m.AR, m.AI, (m.small["ar"][:], m.small["ai"][:]), m.atmp, m.atmp2, T + 1)
    up, dn = slice(0, 64), slice(64, 128)
    rev = slice(T - 1, None, -1)
    for out, top, sign_t, bottom, sign_b, ks in (
            (m.F1, m.AR, 1.0, m.AI, -1.0, slice(0, T + 1)), (m.F2, m.AI, -1.0, m.AR, -1.0, slice(0, T + 1)),
            (m.G1, m.AR, 1.0, m.AI, 1.0, rev), (m.G2, m.AI, -1.0, m.AR, 1.0, rev)):
        c.step(pool.tensor_scalar(out[up, :, :], top[up, :, ks], sign_t, None, ALU.mult))
        c.step(pool.tensor_scalar(out[dn, :, :], bottom[dn, :, ks], sign_b, None, ALU.mult))
    c.wait()
    for s in range(2):
        pool.memset(m.ksb[:, s, :, 0:P], 0.0).then_inc(m.sem(f"prep_stored{s}"), 1)


def pool_s5_phases(m, c, pool):
    t = [m.ctmp1[:, :, i] for i in range(6)]
    cr, ci, mg = m.cosT[:], m.sinT[:], m.magT[:]
    n = 1
    while n < T:
        c.step(pool.tensor_tensor(t[0], cr, cr, ALU.mult))
        c.step(pool.tensor_tensor(t[1], ci, ci, ALU.mult))
        c.step(pool.tensor_tensor(t[2], cr, ci, ALU.mult))
        c.step(pool.tensor_tensor(t[3], mg, mg, ALU.mult))
        c.wait()
        c.step(pool.tensor_tensor(cr, t[0], t[1], ALU.subtract))
        c.step(pool.tensor_scalar(ci, t[2], 2.0, None, ALU.mult))
        c.step(pool.tensor_copy(mg, t[3]))
        c.wait()
        n *= 2
    powers(c, pool, m.CT, m.ST, (cr, ci), m.ctmp1, m.ctmp2, NCH)
    c(pool.tensor_scalar(m.ST[64:128, :, :], m.ST[64:128, :, :], -1.0, None, ALU.mult))
    c.step(pool.memset(m.D0[:, :, 0:1], 0.0))
    c.step(pool.tensor_copy(m.D0[:, :, 1:NCH], mg.unsqueeze(2).to_broadcast([P, NG, NCH - 1])))
    c.wait()
    pool.memset(m.zero1[:], 0.0).then_inc(m.sem("phases"), 1)


N1, N2, MIXPRE, FFNPRE, GLUB, DWB, LNG, LNB = 0, 8, 16, 32, 48, 56, 60, 64


def build(nc, io, out):
    with ExitStack() as ctx:
        m = Program(nc, ctx, io)
        sem, ps, first = m.sem, m.ps, m.first
        nmax, rsum, rinv = m.nmax, m.rsum, m.rinv
        block = ctx.enter_context(nc.Block())
        X_IN = io["x"][0]

        @block.sync
        def _(sp):
            for r in range(RT):
                sp.dma_start(m.x[:, r, :], X_IN[r * P:(r + 1) * P, :]).then_inc(sem(f"x_in{r}"), 16)

            def ffn(st, wg, wu):
                n = first[st + ".up"]

                def pair(n0, c, it):
                    for i, w in enumerate((wg, wu)):
                        v = w[:, bass.ds(c, 256)] if it is not None else w[:, c:c + 256]
                        m.load_unit(sp, n0 + i, v.rearrange("(k p) c -> p k c", p=P), 0 if it is None else it)

                pair(n, 0, None)
                with sp.Fori(0, (FP - 1) // 2) as it:
                    for j in range(2):
                        pair(n + 2 + 2 * j, 256 * (1 + j) + 512 * it, it)
                return n + 2 * FP

            n = 0
            starts = {first["f1.up"]: ("f1", io["w_gate"][0], io["w_up"][0]),
                      first["f2.up"]: ("f2", io["ffn_w_gate_2"][0], io["ffn_w_up_2"][0]),
                      first["f3.up"]: ("f3", io["ffn_w_gate_2"][1], io["ffn_w_up_2"][1])}
            while n < len(m.units):
                if n in starts:
                    n = ffn(*starts[n])
                else:
                    m.load_unit(sp, n, m.units[n][0])
                    n += 1
            for r in range(RT):
                sp.wait_ge(*m.past("pf1_x_ready", r + 1))
                sp.dma_start(out[0, r * P:(r + 1) * P, :], m.x[:, r, :]).then_inc(sem("stored"), 16)
            sp.wait_ge(*m.past("stored", 16 * RT))

        @block.gpsimd
        def _(pool):
            c = pool_constants(m, pool)
            m.pool_rstd(pool, "n1", 2, D, "n1_squares", 2)
            pool.wait_ge(*m.past("qk_in", 16 * 6))
            for i in (0, 2):
                c(pool.tensor_scalar(m.qkg[:, i, :], m.qkg[:, i, :], HD ** -0.5, None, ALU.mult))
            for i in range(2):
                for r in range(RT):
                    g = m.qkg[:, i, :]
                    c.step(pool.tensor_tensor(m.ropeg[:, i, r, 0, :], m.rope[:, r, 0, :], g, ALU.mult))
                    for h in range(2):
                        a, b = slice(32 * h, 32 * h + 32), slice(32 - 32 * h, 64 - 32 * h)
                        last = pool.tensor_tensor(m.ropeg[:, i, r, 1, a], m.rope[:, r, 1, a], m.qkg[:, i, b],
                                                  ALU.mult)
                        if (i, r, h) == (1, RT - 1, 1):
                            last.then_inc(sem("rope_ready"), 1)
                        else:
                            c.step(last)
            pool_s5_scalars(m, c, pool)
            m.pool_rstd(pool, "q", 16, HD, "q_head_sums", 1)
            pool_s5_inputs(m, c, pool)
            m.pool_rstd(pool, "k", 16, HD, "k_head_sums", 1)
            m.pool_rstd(pool, "ln", 2, AW, "ln_head_sums", 1)
            pool_s5_powers(m, c, pool)
            m.pool_rstd(pool, "f1", 2, D, "f1_squares", 2)
            m.pool_prep(pool, 0)
            with pool.Fori(0, (FP - 1) // 2) as it:
                for j in range(2):
                    m.pool_prep(pool, 1 + j, it, 2)
            for b in range(FP, NBLK):
                m.pool_prep(pool, b)
            m.pool_rstd(pool, "fp", 2, D, "fp_squares", 2)
            for r in range(RT):
                c.step(pool.memset(m.qa[:, r, :, HD:HD + 1], 1.0))
                c.step(pool.memset(m.ka[:, r, :, HD + 1:HD + 2], 1.0))
            for i, (t, g) in enumerate(((m.ka, 3), (m.ka, 3), (m.qa, 2), (m.qa, 2))):
                m.pool_rstd(pool, f"blk{i}", 16, HD, f"blk{i}_head_sums", 1)
                for r in range(RT):
                    pool.wait_ge(*m.past(f"blk{i}_out", r + 1))
                    v = t[:, r, 8 * (i % 2):8 * (i % 2) + 8, 0:HD]
                    pool.tensor_tensor(v, v, m.qkg[:, g:g + 1, :].to_broadcast([P, 8, HD]), ALU.mult)\
                        .then_inc(sem("ka_ready" if i < 2 else "qa_ready"), 1)
            m.pool_rstd(pool, "pm0", 2, D, "pm0_squares", 2)
            m.pool_rstd(pool, "f2", 2, D, "f2_squares", 2)
            pool_s5_phases(m, c, pool)
            m.pool_rstd(pool, "pf0", 2, D, "pf0_squares", 2)
            m.pool_rstd(pool, "s", 2, D, "s_squares", 2)
            for j in range(4):
                pool.wait_ge(*m.past("vs_done", j + 1))
                g = slice(16 * j, 16 * j + 16)
                pool.tensor_tensor(m.V[:, g, :], m.V[:, g, :], m.CT[:, g, :], ALU.mult).then_inc(sem("vc"), 1)
            for j in range(4):
                pool.wait_ge(*m.past("zs_done", j + 1))
                g = slice(16 * j, 16 * j + 16)
                pool.tensor_tensor(m.W[:, g, :], m.W[:, g, :], m.CT[:, g, :], ALU.mult).then_inc(sem("zc"), 1)
            pool.wait_ge(*m.past("u_back", 32))
            pool.wait_ge(*m.past("d_in", 16))
            for r in range(RT):
                pool.tensor_tensor(m.ud[:, r, :], m.ud[:, r, :], m.dsk[:], ALU.mult).then_inc(sem("du"), 1)
            m.pool_rstd(pool, "pm1", 2, D, "pm1_squares", 2)
            m.pool_rstd(pool, "f3", 2, D, "f3_squares", 2)
            m.pool_rstd(pool, "pf1", 2, D, "pf1_squares", 2)

        @block.tensor
        def _(pe):
            idn = m.ident
            pe.wait_ge(*m.past("consts", 1))
            pe.wait_ge(*m.past("rows_in", 16 * 13))
            for i in range(2):
                pe.transpose(ps[:, 0, 64 * i:64 * i + 64], m.lamnat[:, i, :, :].rearrange("g a p -> g (a p)"),
                             idn[0:NG, 0:NG])
            pe.transpose(ps[:, 0, 128:196], m.vrows[:], idn[0:68, 0:68])
            pe.transpose(ps[:, 0, 256:256 + 4 * TAPS], m.taprows[:], idn[0:4 * TAPS, 0:4 * TAPS])\
              .then_inc(sem("rows_turned"), 1)
            m.pe_turn(pe, "n1", (4, 5, 6, 7))
            for i in range(4):
                if i == 0:
                    pe.wait_ge(*m.past("vec_out", 1))
                m.mm_features(pe, first["u"] + i, i, ready="n1_act_ready" if i == 0 else None)
            pe.wait_ge(*m.past("c_in", 64))
            for i in range(2):
                for t in range(8):
                    last = pe.transpose(ps[:, 4 + 2 * i + t // 4, (t % 4) * P:(t % 4 + 1) * P],
                                        m.cnat[:, i, t, :, :].rearrange("g a p -> g (a p)"), idn[:])
            last.then_inc(sem("c_turned"), 1)
            for name, banks, wait in (("q", (4, 5), ("c_out", 2)), ("k", (6, 7), ("c_out", 4)),
                                      ("v", (0, 1), ("glu", 4))):
                pe.wait_ge(*m.past(wait[0], wait[1]))
                for h in range(2):
                    m.mm_half_k(pe, first[name] + h, banks, h)
            m.pe_heads(pe, "a1", "q", m.qn[:].rearrange("p r (h d) -> p r h d", d=HD), H1, "q_ready", 2, (2, 3), 0)
            m.pe_heads(pe, "a1", "k", m.kn[:].rearrange("p r (h d) -> p r h d", d=HD), H1, "k_ready", 2, (2, 3),
                       H1 // 2)
            pe.wait_ge(*m.past("a1_heads_out", H1))
            pe.wait_ge(*m.past("v_out", 2))
            m.pe_attention(pe, "a1", H1, m.qt, m.kt1, m.vn, m.p1, m.pt1, (4, 5), (6, 7),
                           lambda r, h: ps[:, r, h * HD:(h + 1) * HD])
            m.pe_turn(pe, "ao", (6, 7), n=4)
            pe.wait_ge(*m.past("conv_done", 1))
            for j in range(4):
                last = pe.matmul(ps[:, 4, 0:TOK], m.ones[:], m.cacc[:, j, :], start=(j == 0), stop=(j == 3))
            last.then_inc(sem("ln_sum"), 1)
            n = first["o1"]
            ao = (("ao_act_ready", 1),)
            m.mm_k_pair(pe, n, 0, m.actH, m.actL, 0, KT, ao)
            pe.wait_ge(*m.past("ln_sq", 1))
            for r in range(RT):
                for j in range(4):
                    last = pe.matmul(ps[:, 5, r:r + 1], m.csq[:, j, r * P:(r + 1) * P], m.ones[:, 0:1],
                                     start=(j == 0), stop=(j == 3))
            last.then_inc(sem("ln_second"), 1)
            m.mm_k_pair(pe, n + 1, 0, m.actH, m.actL, 2, KT, (("ao_act_ready", 3),))
            pe.wait_ge(*m.past("ln_diag", 2))
            pe.matmul(ps[:, 4, 0:TOK], m.ones[:], m.diag[:], start=True, stop=True).then_inc(sem("ln_spread"), 1)
            pe.wait_ge(*m.past("cv_act_ready", 1))
            m.mm_k_pair(pe, n + 2, 0, m.actH, m.actL, 4, KT)
            m.mm_k_pair(pe, n + 3, 0, m.actH, m.actL, 6, KT)
            m.pe_turn(pe, "f1", (4, 5, 6, 7))
            m.pe_ffn(pe, "f1", 0, prep=True)
            m.pe_turn(pe, "fp", (0, 1, 2, 3))
            pe.wait_ge(*m.past("fp_act_ready", KT))
            pe.wait_ge(*m.past("wf_split", 2))
            for r in range(RT):
                for k in range(KT):
                    xh, xl = m.actH[:, k, r * P:(r + 1) * P], m.actL[:, k, r * P:(r + 1) * P]
                    o = ps[:, 0, H2 * r:H2 * r + H2]
                    pe.matmul(o, xh, m.wfH[:, k, :], start=(k == 0), stop=False)
                    pe.matmul(o, xh, m.wfL[:, k, :], start=False, stop=False)
                    last = pe.matmul(o, xl, m.wfH[:, k, :], start=False, stop=(k == KT - 1))
            last.then_inc(sem("f_done"), 1)
            blocks = [("fk", 0), ("fk", 1), ("fq", 0), ("fq", 1), ("fv", 0), ("fv", 1), ("fg", 0), ("fg", 1)]
            for i, (name, b) in enumerate(blocks):
                if i >= 2:
                    pe.wait_ge(*m.past(f"blk{i - 2}_out", 2))
                banks = (4, 5) if i % 2 == 0 else (6, 7)
                for h in range(2):
                    m.mm_half_k(pe, first[name] + 2 * b + h, banks, h)
                if i == 0:
                    pe.wait_ge(*m.past("logf", 1))
                    lf = m.fl[:, 1]
                    pe.matmul(ps[:, 1, 0:H2], m.tri[:], lf[:, 0, :], start=True, stop=True)
                    pe.matmul(ps[:, 1, H2:2 * H2], m.ones[:], lf[:, 0, :], start=True, stop=False)
                    pe.matmul(ps[:, 1, H2:2 * H2], m.tri[:], lf[:, 1, :], start=False, stop=True)\
                      .then_inc(sem("csum"), 1)
                if i == 4:
                    pe.wait_ge(*m.past("c_cols", 4))
                    m.pe_heads(pe, "a2", "k", m.ka, H2, "ka_ready", 4, (2, 3), 0)
                if i == 6:
                    m.pe_heads(pe, "a2", "q", m.qa, H2, "qa_ready", 4, (2, 3), H2 // 2)
            pe.wait_ge(*m.past("a2_heads_out", H2))
            pe.wait_ge(*m.past("blk6_out", 2))
            pe.wait_ge(*m.past("blk7_out", 2))
            m.pe_attention(pe, "a2", H2, m.qt2, m.kt2, m.va, m.p2, m.pt2, (0, 1), (2, 3),
                           lambda r, h: ps[:, 4 + 2 * r + h // 8, (h % 8) * HD:(h % 8 + 1) * HD])
            m.pe_turn(pe, "fo", (0, 1, 2, 3))
            for i in range(4):
                m.mm_k_pair(pe, first["o2"] + i, 4, m.actH, m.actL, 2 * i, KT,
                            (("fo_act_ready", 2 * i + 1),))
            m.pe_turn(pe, "f2", (0, 1, 2, 3))
            m.pe_ffn(pe, "f2", 4)
            m.pe_turn(pe, "s", (4, 5, 6, 7))
            for b in range(2):
                for h in range(2):
                    m.mm_half_k(pe, first["s"] + 2 * b + h, (2 * b, 2 * b + 1), h,
                                "s_act_ready" if b == 0 else None)
            pe.wait_ge(*m.past("ur_a", 1))
            pe.wait_ge(*m.past("ur_d", 1))
            for q in range(16):
                last = pe.transpose(ps[:, 4 + q // 4, (q % 4) * P:(q % 4 + 1) * P],
                                    m.Ur[:, q, :, :].rearrange("p t c -> p (t c)"), idn[:])
                if q % 4 == 3:
                    last.then_inc(sem("u_turned"), 1)
            pe.wait_ge(*m.past("u_out_a", 2))
            pe.wait_ge(*m.past("u_out_d", 2))
            pe.wait_ge(*m.past("r_in", 16))
            for j in range(4):
                for q in range(16):
                    last = pe.matmul(ps[:, j, q * NCH:(q + 1) * NCH], m.RTab[:, 16 * j + q, :], m.Uall[:, q, j, :],
                                     start=True, stop=True)
                last.then_inc(sem("v_done"), 1)

            def swap(j, src, bank, ready, value, done):
                pe.wait_ge(*m.past(ready, value))
                pe.matmul(ps[:, bank, :], m.swap[:],
                          src[:, 16 * j:16 * j + 16, :].rearrange("p g c -> p (g c)"), start=True, stop=True)\
                  .then_inc(sem(done), 1)

            for j in range(4):
                swap(j, m.V, 4 + j, "vo_a" if j < 2 else "vo_d", j % 2 + 1, "vs_done")
            for j in range(4):
                swap(j, m.W, j, "scanned", j + 1, "zs_done")
            pe.wait_ge(*m.past("t_in", 16 * T))
            pe.wait_ge(*m.past("o_in", 16))
            pe.wait_ge(*m.past("states", 4))
            for q in range(16):
                for j in range(4):
                    o = ps[32 * j:32 * j + 32, 4 + q // 4, (q % 4) * P:(q % 4 + 1) * P]
                    pe.matmul(o, m.Uall[:, q, j, :], m.TTab[:, 16 * j + q, :], start=True, stop=False)
                    last = pe.matmul(o, m.X33[:, 16 * j + q, 0:NCH], m.OTab[:, 16 * j + q, :], start=False, stop=True)
                if q % 4 == 3:
                    last.then_inc(sem("y_done"), 1)
            m.pe_turn(pe, "yg", (0, 1, 2, 3))
            for i in range(4):
                m.mm_k_pair(pe, first["glu"] + i, 4, m.actH, m.actL, 2 * i, KT, (("yg_act_ready", 2 * i + 1),))
            m.pe_turn(pe, "yo", (0, 1, 2, 3))
            for i in range(4):
                m.mm_k_pair(pe, first["o3"] + i, 4, m.actH, m.actL, 2 * i, KT, (("yo_act_ready", 2 * i + 1),))
            m.pe_turn(pe, "f3", (0, 1, 2, 3))
            m.pe_ffn(pe, "f3", 4)

        @block.scalar
        def _(act):
            s5 = {k: v[:] for k, v in m.small.items()}
            rows = sem("rows_in")
            for i, lam in enumerate((io["s5_lam_re_2"][0], io["s5_lam_im_2"][0])):
                for a in range(2):
                    act.dma_start(m.lamnat[:, i, a, :], lam).then_inc(rows, 16)
            for at, v in ((N1, io["norm1_g"][0]), (N2, io["norm2_g"][0]), (GLUB, io["glu_b"][0]), (DWB, io["dw_b"][0]),
                          (LNG, io["conv_ln_g"][0]), (LNB, io["conv_ln_b"][0])):
                k = v.shape[0] // P
                act.dma_start(m.vrows[at:at + k, :], v.rearrange("(k p) -> k p", p=P)).then_inc(rows, 16)
            for at, v in ((MIXPRE, io["mix_pre_gain_2"]), (FFNPRE, io["ffn_pre_gain_2"])):
                act.dma_start(m.vrows[at:at + 16, :], v.rearrange("l (k p) -> (l k) p", p=P)).then_inc(rows, 16)
            act.dma_start(m.taprows[:], io["dw_w"][0].rearrange("k (j p) -> (k j) p", p=P)).then_inc(rows, 16)
            act.dma_start(s5["ldt"], io["s5_log_dt_2"].to_broadcast([P, NG])).then_inc(sem("ldt_in"), 16)
            for r in range(RT):
                act.wait_ge(*m.past(f"x_in{r}", 16))
                act.activation(m.nat[:, r, :], m.x[:, r, :], ACT.Square, accum_out=m.ss[:, r:r + 1])\
                   .then_inc(sem("n1_squares"), 1)
            act.wait_ge(*m.past("rows_turned", 1))
            act.activation(s5["LR"], ps[:, 0, 0:64], ACT.Copy).then_inc(sem("lam_copy"), 1)
            act.activation(s5["LI"], ps[:, 0, 64:128], ACT.Copy).then_inc(sem("lam_out"), 1)
            act.activation(m.taps[:], ps[:, 0, 256:256 + 4 * TAPS], ACT.Copy).then_inc(sem("taps_out"), 1)
            act.activation(m.vec[:], ps[:, 0, 128:196], ACT.Copy).then_inc(sem("vec_out"), 1)
            m.split_high(act, 0)
            act.wait_ge(*m.past("vec_out", 1))
            m.act_turn(act, "n1", (4, 5, 6, 7), gain=N1)
            m.split_high(act, 1)
            for i, v in enumerate((io["q_norm_g"], io["k_norm_g"], io["fox_q_gain_2"], io["fox_k_gain_2"])):
                act.dma_start(m.qkg[:, i, :], v.to_broadcast([P, HD])).then_inc(sem("qk_in"), 16)
            for r in range(RT):
                act.dma_start(m.rope[:, r, :, :], io["rope"][r * P:(r + 1) * P]).then_inc(sem("qk_in"), 16)
            for i, v in enumerate((io["s5_c_re_2"][0], io["s5_c_im_2"][0])):
                for a in range(2):
                    act.dma_start(m.cnat[:, i, :, a, :], v.rearrange("(t g) c p -> (g c) t p", g=8))\
                       .then_inc(sem("c_in"), 16)
            for t, v in ((m.Bre, io["s5_b_re_2"][0]), (m.Bim, io["s5_b_im_2"][0])):
                for a in range(2):
                    act.dma_start(t[64 * a:64 * a + 64, :, :], v.rearrange("g p c -> p g c")).then_inc(sem("b_in"), 16)
            act.wait_ge(*m.past("ldt_in", 16))
            act.activation(s5["dt"], s5["ldt"], ACT.Exp).then_inc(sem("dt"), 1)
            m.split_high(act, 2)
            m.split_high(act, 3)
            m.split_high(act, 4)
            for j in range(4):
                act.wait_ge(m.used, first["u"] + 3 + j // 2)
                act.activation(m.csig[:, j, :], ps[:, 2 + j // 2, (j % 2) * TOK:(j % 2 + 1) * TOK], ACT.Sigmoid,
                               bias=m.vec[:, GLUB + 4 + j:GLUB + 5 + j]).then_inc(sem("sig"), 1)
            m.split_high(act, 5)
            act.wait_ge(*m.past("c_turned", 1))
            for i, t in enumerate((m.C1, m.C2)):
                for h in range(2):
                    act.activation(t[:, 32 * h:32 * h + 32, :],
                                   ps[:, 4 + 2 * i + h, :].rearrange("p (g c) -> p g c", c=SC), ACT.Copy)\
                       .then_inc(sem("c_out"), 1)
            f5 = sem("s5_functions")
            act.wait_ge(*m.past("angle", 1))
            act.activation(m.sinT[:], s5["thr"], ACT.Sin).then_inc(f5, 1)
            act.activation(s5["sh"], s5["thr"], ACT.Sin, scale=0.5).then_inc(f5, 1)
            act.activation(s5["tt"], s5["lrc"], ACT.Tanh, scale=0.5).then_inc(f5, 1)
            act.wait_ge(*m.past("abs_angle", 1))
            act.activation(m.cosT[:], s5["ab"], ACT.Sin, scale=-1.0, bias=m.halfpi[:]).then_inc(f5, 1)
            act.activation(s5["eb"], s5["lrb"], ACT.Exp).then_inc(f5, 1)
            m.split_high(act, 6)
            m.split_high(act, 7)

            def head_squares(st, banks, unit, sq):
                act.wait_ge(m.used, unit)
                for r in range(RT):
                    act.activation(sq[:, r, :], ps[:, banks[r], :], ACT.Square).then_inc(sem(st + "_sq"), 1)

            act.wait_ge(*m.past("glu", 4))
            head_squares("q", (4, 5), first["q"] + 2, m.sq1)
            m.split_high(act, 8)
            m.split_high(act, 9)
            act.wait_ge(*m.past("q_head_sums", 1))
            head_squares("k", (6, 7), first["k"] + 2, m.sq1)
            m.split_high(act, 10)
            m.split_high(act, 11)
            for r in range(RT):
                act.wait_ge(m.used, first["v"] + 2)
                act.activation(m.vn[:, r, :], ps[:, r, :], ACT.Copy).then_inc(sem("v_out"), 1)
            m.act_heads(act, "a1", m.qt, H1, (2, 3), 0)
            m.act_heads(act, "a1", m.kt1, H1, (2, 3), H1 // 2)
            m.act_attention(act, "a1", H1, m.p1, rsum, nmax, (4, 5))
            m.act_turn(act, "ao", (6, 7), n=4)
            act.wait_ge(*m.past("ln_centred", 1))
            act.activation(m.csq[:], m.cacc[:], ACT.Square).then_inc(sem("ln_sq"), 1)
            m.split_high(act, 12)
            m.split_high(act, 13)
            act.wait_ge(*m.past("ln_second", 1))
            act.wait_ge(*m.past("ln_normed", 1))
            for j in range(4):
                act.activation(m.csq[:, j, :], m.cacc[:, j, :], ACT.Silu, scale=m.vec[:, LNG + j:LNG + j + 1],
                               bias=m.vec[:, LNB + j:LNB + j + 1]).then_inc(sem("cv_silu"), 1)
            act.wait_ge(*m.past("cv_silu", 4))
            act.activation(m.actH[:, 4:8, :], m.csq[:], ACT.Copy).then_inc(sem("cv_high"), 1)
            m.split_high(act, 14)
            m.act_squares(act, "f1", lambda r: m.x[:, r, :], "f1_x_ready", (1, 2))
            m.act_turn(act, "f1", (4, 5, 6, 7), gain=N2)
            m.split_high(act, 15)
            m.act_ffn(act, "f1", 0, prep=True)
            for i in range(2):
                act.wait_ge(*m.past(f"prep_stored{i}", 48 * (NBLK // 2) + 1))
            act.dma_start(m.wf[:], io["fox_w_in_2"][0][:, 4 * D:4 * D + H2].rearrange("(k p) c -> p k c", p=P))\
               .then_inc(sem("wf_in"), 16)
            act.dma_start(m.fb[:], io["fox_b_f_2"].to_broadcast([P, H2])).then_inc(sem("fb_in"), 16)
            act.dma_start(m.gb[0][:], io["mix_post_gain_2"][0:1, :].to_broadcast([P, D])).then_inc(sem("gain0_in"), 16)
            act.dma_start(m.gb[1][:], io["ffn_post_gain_2"][0:1, :].to_broadcast([P, D])).then_inc(sem("gain1_in"), 16)
            m.act_squares(act, "fp", lambda r: m.x[:, r, :], "fp_x_ready", (1, 2))
            act.wait_ge(*m.past("wf_in", 16))
            act.activation(m.wfH[:], m.wf[:], ACT.Copy).then_inc(sem("wf_high"), 1)
            m.act_turn(act, "fp", (0, 1, 2, 3), gain=MIXPRE)
            m.split_high(act, first["fk"] + 1)
            act.wait_ge(*m.past("f_abs", 1))
            act.activation(m.fl[:, 2], m.fl[:, 1], ACT.Exp, scale=-1.0).then_inc(sem("f_exp"), 1)
            act.wait_ge(*m.past("f_exp", 1))
            act.activation(m.fl[:, 3], m.fl[:, 2], ACT.Ln, bias=1.0).then_inc(sem("f_ln"), 1)
            n = first["fk"]
            for i in range(8):
                banks = (4, 5) if i % 2 == 0 else (6, 7)
                for h in range(2):
                    m.split_high(act, n + 2 * i + 2 + h)
                if i < 4:
                    if i > 0:
                        act.wait_ge(*m.past(f"blk{i - 1}_head_sums", 1))
                    head_squares(f"blk{i}", banks, n + 2 * i + 2, m.sq2)
                else:
                    act.wait_ge(m.used, n + 2 * i + 2)
                    f, dst = (ACT.Copy, m.va) if i < 6 else (ACT.Sigmoid, m.ga)
                    for r in range(RT):
                        act.activation(dst[:, r, 512 * (i % 2):512 * (i % 2) + 512], ps[:, banks[r], :], f)\
                           .then_inc(sem(f"blk{i}_out"), 1)
                if i == 4:
                    m.act_heads(act, "a2", m.kt2, H2, (2, 3), 0)
                if i == 6:
                    m.act_heads(act, "a2", m.qt2, H2, (2, 3), H2 // 2)
            m.act_attention(act, "a2", H2, m.p2, rsum, nmax, (0, 1))
            m.act_turn(act, "fo", (0, 1, 2, 3))
            n = first["o2"]
            for i in range(3):
                m.split_high(act, n + 2 + i)
            act.wait_ge(m.used, n + 4)
            m.act_squares(act, "pm0", lambda r: m.acc_row(4, r))
            m.act_squares(act, "f2", lambda r: m.x[:, r, :], "pm0_x_ready", (1, 2))
            act.dma_start(m.gb[0][:], io["mix_post_gain_2"][1:2, :].to_broadcast([P, D])).then_inc(sem("gain0_in"), 16)
            m.act_turn(act, "f2", (0, 1, 2, 3), gain=FFNPRE)
            m.split_high(act, n + 5)
            m.act_ffn(act, "f2", 4)
            n = first["s"]
            act.wait_ge(m.used, n)
            m.act_squares(act, "pf0", lambda r: m.acc_row(0, r))
            act.dma_start(m.RTab[:], m.Rd).then_inc(sem("r_in"), 16)
            act.dma_start(m.OTab[:], m.Od).then_inc(sem("o_in"), 16)
            m.act_squares(act, "s", lambda r: m.x[:, r, :], "pf0_x_ready", (1, 2))
            act.dma_start(m.dsk[:], io["s5_d_2"].to_broadcast([P, D])).then_inc(sem("d_in"), 16)
            m.act_turn(act, "s", (4, 5, 6, 7), gain=MIXPRE + 8)
            m.split_high(act, n + 1)
            m.split_high(act, n + 2)
            m.split_high(act, n + 3)
            act.wait_ge(m.used, n + 2)
            act.activation(m.nat[:, 0, 0:512], ps[:, 0, :], ACT.Copy).then_inc(sem("u_nat_a"), 1)
            m.split_high(act, n + 4)
            act.wait_ge(m.used, n + 4)
            act.activation(m.nat[:, 0, 512:D], ps[:, 2, :], ACT.Copy).then_inc(sem("u_nat_a"), 1)
            act.wait_ge(*m.past("u_nat_a", 2))
            act.dma_start(m.ud_d[0:P, :], m.nat[:, 0, :]).then_inc(sem("u_stored"), 16)
            act.wait_ge(*m.past("u_nat_d", 2))
            act.dma_start(m.ud_d[P:2 * P, :], m.nat[:, 1, :]).then_inc(sem("u_stored"), 16)
            m.split_high(act, n + 5)
            act.wait_ge(*m.past("u_stored", 32))

            def chunked(dram, j):
                return dram.rearrange("(c t) f -> c t f", t=T)[:, :, 256 * j:256 * j + 256]

            for j in range(4):
                act.dma_start(m.Un[32 * j:32 * j + 32].rearrange("p t q c -> p t (q c)"), chunked(m.ud_d, j))\
                   .then_inc(sem("un_in"), 16)
            act.wait_ge(*m.past("un_in", 64))
            act.activation(m.Ur[:, 0:8, :, :], m.Un[:, :, 0:8, :].rearrange("p t q c -> p q t c"), ACT.Copy)\
               .then_inc(sem("ur_a"), 1)
            for b in range(2):
                act.wait_ge(*m.past("u_turned", b + 1))
                act.activation(m.Uall[:, 4 * b:4 * b + 4, :, :],
                               ps[:, 4 + b, :].rearrange("p (q j c) -> p q j c", q=4, j=4), ACT.Copy)\
                   .then_inc(sem("u_out_a"), 1)
            for j in range(2):
                act.wait_ge(*m.past("v_done", j + 1))
                act.activation(m.V[:, 16 * j:16 * j + 16, :], ps[:, j, :].rearrange("p (g c) -> p g c", c=NCH), ACT.Copy)\
                   .then_inc(sem("vo_a"), 1)
            act.wait_ge(*m.past("v_done", 4))
            for s in range(T):
                act.dma_start(m.TTab[SC * s:SC * s + SC, :, :], m.Kd[:, :, P - SC * s:2 * P - SC * s])\
                   .then_inc(sem("t_in"), 16)
            act.wait_ge(*m.past("states", 4))
            for r in range(RT):
                act.dma_start(m.ud[:, r, :], m.ud_d[r * P:(r + 1) * P, :]).then_inc(sem("u_back"), 16)
            for b in range(2):
                act.wait_ge(*m.past("y_done", b + 1))
                act.activation(m.Ysb[:, :, 4 * b:4 * b + 4, :].rearrange("p t q c -> p q t c"),
                               ps[:, 4 + b, :].rearrange("p (q t c) -> p q t c", q=4, t=T), ACT.Copy)\
                   .then_inc(sem("y_out_a"), 1)
            act.wait_ge(*m.past("y_out_a", 2))
            act.wait_ge(*m.past("y_out_d", 2))
            for j in range(4):
                act.dma_start(chunked(m.yd_d, j), m.Ysb[32 * j:32 * j + 32].rearrange("p t q c -> p t (q c)"))\
                   .then_inc(sem("y_stored"), 16)
            act.wait_ge(*m.past("y_stored", 64))
            for r in range(RT):
                act.dma_start(m.nat[:, r, :], m.yd_d[r * P:(r + 1) * P, :]).then_inc(sem(f"y_in{r}"), 16)
            act.wait_ge(*m.past("du", 2))
            act.dma_start(m.gb[1][:], io["ffn_post_gain_2"][1:2, :].to_broadcast([P, D])).then_inc(sem("gain1_in"), 16)
            for r in range(RT):
                act.wait_ge(*m.past("y_sum", r + 1))
                act.activation(m.nat[:, r, :], m.nat[:, r, :], ACT.Gelu_apprx_tanh).then_inc(sem("yg_nat_ready"), 1)
            m.act_turn(act, "yg", (0, 1, 2, 3))
            n = first["glu"]
            for i in range(3):
                m.split_high(act, n + 2 + i)
            act.wait_ge(m.used, n + 4)
            for r in range(RT):
                act.activation(m.sgl[:, r, :].rearrange("p (a b) -> p a b", a=2), m.acc_row(4, r), ACT.Sigmoid)\
                   .then_inc(sem("glu_sig"), 1)
            m.act_turn(act, "yo", (0, 1, 2, 3))
            n = first["o3"]
            for i in range(4):
                m.split_high(act, n + 1 + i)
            act.wait_ge(m.used, n + 4)
            m.act_squares(act, "pm1", lambda r: m.acc_row(4, r))
            m.act_squares(act, "f3", lambda r: m.x[:, r, :], "pm1_x_ready", (1, 2))
            m.act_turn(act, "f3", (0, 1, 2, 3), gain=FFNPRE + 8)
            m.split_high(act, n + 5)
            m.act_ffn(act, "f3", 4)
            act.wait_ge(m.used, len(m.units))
            m.act_squares(act, "pf1", lambda r: m.acc_row(0, r))

        @block.vector
        def _(dve):
            c = Chain(dve, sem("dve_chain"))
            s5 = {k: v[:] for k, v in m.small.items()}
            m.dve_scale(dve, "n1")
            m.split_low(dve, 0)
            dve.wait_ge(*m.past("vec_out", 1))
            m.dve_turn(dve, "n1", (4, 5, 6, 7), gain=N1)
            for i in range(1, 5):
                m.split_low(dve, i)
            for j in range(4):
                dve.wait_ge(*m.past("sig", j + 1))
                dve.scalar_tensor_tensor(m.hpad[:, j, TAPS - 1:], ps[:, j // 2, (j % 2) * TOK:(j % 2 + 1) * TOK],
                                         m.vec[:, GLUB + j:GLUB + j + 1], m.csig[:, j, :], ALU.add, ALU.mult)\
                   .then_inc(sem("glu"), 1)
            m.split_low(dve, 5)
            dve.wait_ge(*m.past("angle", 1))
            dve.scalar_tensor_tensor(s5["ab"], s5["thr"], -1.0, s5["thr"], ALU.mult, ALU.max)\
               .then_inc(sem("abs_angle"), 1)
            dve.wait_ge(*m.past("s5_functions", 3))
            c(dve.tensor_scalar(s5["r2"], s5["tt"], -1.0, 1.0, ALU.mult, ALU.add))
            dve.reciprocal(s5["r1"], s5["r2"]).then_inc(sem("s5_recips"), 1)
            dve.wait_ge(*m.past("den", 1))
            dve.reciprocal(s5["rden"], s5["den"]).then_inc(sem("s5_recips"), 1)

            taps_left = [(k, j) for k in range(TAPS) for j in range(4)]
            steps = {}

            def conv(count):
                for _ in range(min(count, len(taps_left))):
                    k, j = taps_left.pop(0)
                    w = m.taps[:, 4 * k + j:4 * k + j + 1]
                    src = m.hpad[:, j, k:k + TOK]
                    if k == 0:
                        if j == 0:
                            dve.wait_ge(*m.past("taps_out", 1))
                            dve.wait_ge(*m.past("glu", 4))
                        i = dve.tensor_scalar(m.cacc[:, j, :], src, w, m.vec[:, DWB + j:DWB + j + 1], ALU.mult, ALU.add)
                    else:
                        c.wait(steps[j])
                        i = dve.scalar_tensor_tensor(m.cacc[:, j, :], src, w, m.cacc[:, j, :], ALU.mult, ALU.add)
                    steps[j] = c.step(i)

            def head_norms(st, banks, t, ki):
                dve.wait_ge(*m.past(st + "_sq", 2))
                dve.reduce_sum(m.ss[:], m.sq1[:].rearrange("p r (h d) -> p (r h) d", d=HD), AX.X)\
                   .then_inc(sem(st + "_head_sums"), 1)
                conv(6)
                dve.wait_ge(*m.past(st + "_rstd", 1))
                dve.wait_ge(*m.past("rope_ready", 1))
                hd = lambda a: a.rearrange("p (h d) -> p h d", d=HD)
                for r in range(RT):
                    rs = m.rs[:, 8 * r:8 * r + 8].unsqueeze(2).to_broadcast([P, 8, HD])
                    c(dve.tensor_tensor(hd(m.rtmp[:]), hd(ps[:, banks[r], :]), rs, ALU.mult))
                    tb = [m.ropeg[:, ki, r, i:i + 1, :].to_broadcast([P, 8, HD]) for i in range(2)]
                    c.step(dve.tensor_tensor(hd(t[:, r, :]), hd(m.rtmp[:]), tb[0], ALU.mult))
                    halves = m.rtmp[:].rearrange("p (h a d) -> p h a d", a=2, d=32)
                    for a in range(2):
                        s_ = m.ropeg[:, ki, r, 1:2, 32 * a:32 * a + 32].to_broadcast([P, 8, 32])
                        c.step(dve.tensor_tensor(hd(m.rtmp2[:])[:, :, 32 * a:32 * a + 32], halves[:, :, 1 - a, :], s_,
                                                 ALU.mult))
                    c.wait()
                    dve.tensor_tensor(t[:, r, :], t[:, r, :], m.rtmp2[:], ALU.add).then_inc(sem(st + "_ready"), 1)
                    dve.wait_ge(*m.past(st + "_ready", r + 1))

            conv(8)
            m.split_low(dve, 6)
            conv(8)
            m.split_low(dve, 7)
            head_norms("q", (4, 5), m.qn, 0)
            m.split_low(dve, 8)
            m.split_low(dve, 9)
            head_norms("k", (6, 7), m.kn, 1)
            m.split_low(dve, 10)
            conv(8)
            m.split_low(dve, 11)
            conv(12)
            m.dve_attention(dve, "a1", H1, m.pt1, nmax, (4, 5), (6, 7), lambda h: conv(9))
            c.wait()

            def attention_out(st, H, base, nb, final, gate=None):
                dve.wait_ge(*m.past(st + "_out", H))
                c(dve.reciprocal(rinv[:, :, 0:H], rsum[:, :, 0:H]))
                for r in range(RT):
                    o = ps[:, base + nb * r:base + nb * (r + 1), :].rearrange("p a (h d) -> p (a h) d", d=HD)
                    dst = m.nat[:, r, 0:H * HD]
                    i = dve.tensor_tensor(dst.rearrange("p (h d) -> p h d", d=HD), o,
                                          rinv[:, r, 0:H].unsqueeze(2).to_broadcast([P, H, HD]), ALU.mult)
                    if gate is None:
                        i.then_inc(sem(final), 1)
                    else:
                        c(i)
                        dve.tensor_tensor(dst, dst, gate[:, r, :], ALU.mult).then_inc(sem(final), 1)

            attention_out("a1", H1, 0, 1, "ao_nat_ready")
            m.dve_turn(dve, "ao", (6, 7), n=4)
            conv(200)
            c.wait()
            dve.memset(m.zero1[:], 0.0).then_inc(sem("conv_done"), 1)
            dve.wait_ge(*m.past("ln_sum", 1))
            dve.scalar_tensor_tensor(m.cacc[:], ps[:, 4:5, 0:TOK].to_broadcast([P, 4, TOK]), -1.0 / AW, m.cacc[:],
                                     ALU.mult, ALU.add).then_inc(sem("ln_centred"), 1)
            m.split_low(dve, 12)
            dve.wait_ge(*m.past("ln_second", 1))
            dve.tensor_copy(m.ss[:, 0:2], ps[:, 5, 0:2]).then_inc(sem("ln_head_sums"), 1)
            dve.wait_ge(*m.past("ln_rstd", 1))
            for r in range(RT):
                dve.tensor_scalar(m.diag[:, r * P:(r + 1) * P], m.ident[:], m.rs[:, r:r + 1], None, ALU.mult)\
                   .then_inc(sem("ln_diag"), 1)
            m.split_low(dve, 13)
            dve.wait_ge(*m.past("ln_spread", 1))
            dve.tensor_tensor(m.cacc[:], m.cacc[:], ps[:, 4:5, 0:TOK].to_broadcast([P, 4, TOK]), ALU.mult)\
               .then_inc(sem("ln_normed"), 1)
            dve.wait_ge(*m.past("cv_high", 1))
            dve.tensor_tensor(m.actL[:, 4:8, :], m.csq[:], m.actH[:, 4:8, :].bitcast(F32), ALU.subtract)\
               .then_inc(sem("cv_act_ready"), 1)
            m.split_low(dve, 14)

            def residual(st, base):
                for r in range(RT):
                    xr = m.x[:, r, :].rearrange("p (a b) -> p a b", a=2)
                    dve.tensor_tensor(xr, xr, m.acc_row(base, r), ALU.add).then_inc(sem(st + "_x_ready"), 1)

            dve.wait_ge(m.used, first["o1"] + 4)
            residual("f1", 0)
            m.dve_scale(dve, "f1")
            m.dve_turn(dve, "f1", (4, 5, 6, 7), gain=N2)
            m.split_low(dve, 15)
            m.dve_ffn(dve, "f1", 0)
            n = first["fk"]
            dve.wait_ge(m.used, n)
            residual("fp", 4)
            dve.wait_ge(*m.past("wf_high", 1))
            dve.tensor_tensor(m.wfL[:], m.wf[:], m.wfH[:].bitcast(F32), ALU.subtract).then_inc(sem("wf_split"), 2)
            m.dve_scale(dve, "fp")
            m.dve_turn(dve, "fp", (0, 1, 2, 3), gain=MIXPRE)
            m.split_low(dve, n + 1)
            dve.wait_ge(*m.past("f_done", 1))
            dve.wait_ge(*m.past("fb_in", 16))
            c(dve.tensor_tensor(m.fl[:, 0], ps[:, 0, 0:2 * H2].rearrange("p (r h) -> p r h", r=2),
                                m.fb[:].unsqueeze(1).to_broadcast([P, RT, H2]), ALU.add))
            dve.scalar_tensor_tensor(m.fl[:, 1], m.fl[:, 0], -1.0, m.fl[:, 0], ALU.mult, ALU.max)\
               .then_inc(sem("f_abs"), 1)
            dve.wait_ge(*m.past("f_ln", 1))
            dve.scalar_tensor_tensor(m.fl[:, 1], m.fl[:, 0], 0.0, m.fl[:, 3], ALU.min, ALU.subtract)\
               .then_inc(sem("logf"), 1)
            for i in range(8):
                banks = (4, 5) if i % 2 == 0 else (6, 7)
                for h in range(2):
                    m.split_low(dve, n + 2 * i + 2 + h)
                if i == 0:
                    dve.wait_ge(*m.past("csum", 1))
                    for r in range(RT):
                        cs = ps[:, 1, H2 * r:H2 * r + H2].unsqueeze(2)
                        dve.tensor_copy(m.qa[:, r, :, HD + 1:HD + 2], cs).then_inc(sem("c_cols"), 1)
                        dve.tensor_scalar(m.ka[:, r, :, HD:HD + 1], cs, -1.0, None, ALU.mult).then_inc(sem("c_cols"), 1)
                if i < 4:
                    st = f"blk{i}"
                    t = m.ka if i < 2 else m.qa
                    dve.wait_ge(*m.past(st + "_sq", 2))
                    dve.reduce_sum(m.ss[:], m.sq2[:].rearrange("p r (h d) -> p (r h) d", d=HD), AX.X)\
                       .then_inc(sem(st + "_head_sums"), 1)
                    dve.wait_ge(*m.past(st + "_rstd", 1))
                    for r in range(RT):
                        dve.tensor_tensor(t[:, r, 8 * (i % 2):8 * (i % 2) + 8, 0:HD],
                                          ps[:, banks[r], :].rearrange("p (h d) -> p h d", d=HD),
                                          m.rs[:, 8 * r:8 * r + 8].unsqueeze(2).to_broadcast([P, 8, HD]), ALU.mult)\
                           .then_inc(sem(st + "_out"), 1)
            m.dve_attention(dve, "a2", H2, m.pt2, nmax, (0, 1), (2, 3))
            attention_out("a2", H2, 4, 2, "fo_nat_ready", m.ga)
            m.dve_turn(dve, "fo", (0, 1, 2, 3))
            n = first["o2"]
            for i in range(3):
                m.split_low(dve, n + 2 + i)
            m.dve_postnorm(dve, "pm0", 4, m.gb[0], "gain0_in", 16)
            m.dve_scale(dve, "f2")
            m.dve_turn(dve, "f2", (0, 1, 2, 3), gain=FFNPRE)
            m.split_low(dve, n + 5)
            m.dve_ffn(dve, "f2", 4)
            m.dve_postnorm(dve, "pf0", 0, m.gb[1], "gain1_in", 16)
            n = first["s"]
            m.dve_scale(dve, "s")
            m.dve_turn(dve, "s", (4, 5, 6, 7), gain=MIXPRE + 8)
            for i in range(1, 4):
                m.split_low(dve, n + i)
            dve.wait_ge(m.used, n + 2)
            dve.tensor_copy(m.nat[:, 1, 0:512], ps[:, 1, :]).then_inc(sem("u_nat_d"), 1)
            m.split_low(dve, n + 4)
            dve.wait_ge(m.used, n + 4)
            dve.tensor_copy(m.nat[:, 1, 512:D], ps[:, 3, :]).then_inc(sem("u_nat_d"), 1)
            m.split_low(dve, n + 5)
            dve.wait_ge(*m.past("un_in", 64))
            dve.tensor_copy(m.Ur[:, 8:16, :, :], m.Un[:, :, 8:16, :].rearrange("p t q c -> p q t c"))\
               .then_inc(sem("ur_d"), 1)
            for b in range(2, 4):
                dve.wait_ge(*m.past("u_turned", b + 1))
                dve.tensor_copy(m.Uall[:, 4 * b:4 * b + 4, :, :],
                                ps[:, 4 + b, :].rearrange("p (q j c) -> p q j c", q=4, j=4)).then_inc(sem("u_out_d"), 1)
            flat = lambda a: a.rearrange("p g c -> p (g c)")
            grp = [slice(16 * j, 16 * j + 16) for j in range(4)]
            for j in range(2, 4):
                dve.wait_ge(*m.past("v_done", j + 1))
                dve.tensor_copy(m.V[:, grp[j], :], ps[:, j, :].rearrange("p (g c) -> p g c", c=NCH))\
                   .then_inc(sem("vo_d"), 1)
            dve.wait_ge(*m.past("phases", 1))
            for j in range(4):
                dve.wait_ge(*m.past("vs_done", j + 1))
                k = c.step(dve.tensor_tensor(flat(m.W[:, grp[j], :]), ps[:, 4 + j, :], flat(m.ST[:, grp[j], :]), ALU.mult))
                dve.wait_ge(*m.past("vc", j + 1))
                c.wait(k)
                c(dve.tensor_tensor(m.V[:, grp[j], :], m.V[:, grp[j], :], m.W[:, grp[j], :], ALU.add))
                dve.tensor_tensor_scan(flat(m.W[:, grp[j], :]), flat(m.D0[:, grp[j], :]), flat(m.V[:, grp[j], :]), 0.0,
                                       ALU.mult, ALU.add).then_inc(sem("scanned"), 1)
            dve.wait_ge(*m.past("scanned", 4))
            c.step(dve.memset(m.X33[:, :, 0:1], 0.0))
            for j in range(4):
                dve.wait_ge(*m.past("zs_done", j + 1))
                c(dve.tensor_tensor(flat(m.V[:, grp[j], :]), ps[:, j, :], flat(m.ST[:, grp[j], :]), ALU.mult))
                dve.wait_ge(*m.past("zc", j + 1))
                dve.tensor_tensor(m.X33[:, grp[j], 1:NCH + 1], m.W[:, grp[j], :], m.V[:, grp[j], :], ALU.subtract)\
                   .then_inc(sem("states"), 1)
            for b in range(2, 4):
                dve.wait_ge(*m.past("y_done", b + 1))
                dve.tensor_copy(m.Ysb[:, :, 4 * b:4 * b + 4, :].rearrange("p t q c -> p q t c"),
                                ps[:, 4 + b, :].rearrange("p (q t c) -> p q t c", q=4, t=T)).then_inc(sem("y_out_d"), 1)
            for r in range(RT):
                dve.wait_ge(*m.past(f"y_in{r}", 16))
                dve.wait_ge(*m.past("du", r + 1))
                dve.tensor_tensor(m.nat[:, r, :], m.nat[:, r, :], m.ud[:, r, :], ALU.add).then_inc(sem("y_sum"), 1)
            m.dve_turn(dve, "yg", (0, 1, 2, 3))
            n = first["glu"]
            for i in range(3):
                m.split_low(dve, n + 2 + i)
            for r in range(RT):
                dve.wait_ge(*m.past("glu_sig", r + 1))
                dve.tensor_tensor(m.nat[:, r, :], m.nat[:, r, :], m.sgl[:, r, :], ALU.mult)\
                   .then_inc(sem("yo_nat_ready"), 1)
            m.dve_turn(dve, "yo", (0, 1, 2, 3))
            n = first["o3"]
            for i in range(4):
                m.split_low(dve, n + 1 + i)
            m.dve_postnorm(dve, "pm1", 4, m.gb[0], "gain0_in", 32)
            m.dve_scale(dve, "f3")
            m.dve_turn(dve, "f3", (0, 1, 2, 3), gain=FFNPRE + 8)
            m.split_low(dve, n + 5)
            m.dve_ffn(dve, "f3", 4)
            m.dve_postnorm(dve, "pf1", 0, m.gb[1], "gain1_in", 32)


_INS = ["x", "w_in", "norm1_g", "glu_b", "q_norm_g", "k_norm_g", "dw_w", "dw_b", "conv_ln_g", "conv_ln_b", "w_out",
        "norm2_g", "w_gate", "w_up", "w_down", "fox_w_in_2", "fox_b_f_2", "fox_q_gain_2", "fox_k_gain_2",
        "fox_w_out_2", "s5_w_in_2", "s5_log_dt_2", "s5_lam_re_2", "s5_lam_im_2", "s5_b_re_2", "s5_b_im_2",
        "s5_c_re_2", "s5_c_im_2", "s5_d_2", "s5_w_glu_2", "s5_w_out_2", "mix_pre_gain_2", "mix_post_gain_2",
        "ffn_pre_gain_2", "ffn_post_gain_2", "ffn_w_gate_2", "ffn_w_up_2", "ffn_w_down_2"]


def rope_table():
    pos = np.arange(TOK, dtype=np.float32)
    inv = np.float32(10000.0) ** (-np.arange(0, HD, 2, dtype=np.float32) / np.float32(HD))
    ang = pos[:, None] * inv[None, :]
    cos, sin = np.cos(ang), np.sin(ang)
    return np.stack([np.concatenate([cos, cos], 1), np.concatenate([-sin, sin], 1)], 1).astype(np.float32)


def kernel(**inputs):
    import concourse.bacc as bacc
    from concourse.bass_utils import run_bass_kernel_spmd

    nc = bacc.Bacc("TRN2", target_bir_lowering=False, num_devices=1)
    arrays = {name: np.ascontiguousarray(inputs[name]) for name in _INS}
    arrays["rope"] = rope_table()
    io = {name: nc.dram_tensor(f"in_{name}", a.shape, mybir.dt.from_np(a.dtype), kind="ExternalInput").ap()
          for name, a in arrays.items()}
    out = nc.dram_tensor("out", (1, TOK, D), F32, kind="ExternalOutput").ap()
    build(nc, io, out)
    r = run_bass_kernel_spmd(nc, [{f"in_{n}": a for n, a in arrays.items()}], core_ids=[0])
    return r.results[0]["out"]
```

```python
import math
from contextlib import ExitStack

import numpy as np

import concourse.bass as bass
from concourse import mybir

F32 = mybir.dt.float32
F32R = mybir.dt.float32r
BF16 = mybir.dt.bfloat16
ACT = mybir.ActivationFunctionType
ALU = mybir.AluOpType
AX = mybir.AxisListType

P = 128
TOK = 256
RT = TOK // P
D = 1024
KT = D // P
DFF = 2816
FT = DFF // P
FP = FT // 2
EPS = 1e-6
HD = 64
H1 = 8
H2 = 16
AW = H1 * HD
TAPS = 31
TAPG = 8
VCOLS = 72
NG = 64
SC = 16
T = 8
NCH = TOK // T
GB = 4
NBLK = NG // GB
UNIT = 2048
RAW = 4
RING = 2
NEG = -3.0e38


class Program:
    def __init__(self, nc, ctx, io):
        self.nc, self.ctx, self.io = nc, ctx, io
        self.sems = {}
        self.plan_units()
        self.place()

    KINDS = {
        "nat_ready": (("n1", "ao", "f1", "fp", "fo", "f2", "s", "yg", "yo", "f3"), 2),
        "transposed": (("n1", "ao", "f1", "fp", "fo", "f2", "s", "yg", "yo", "f3"), 8),
        "high_ready": (("n1", "ao", "f1", "fp", "fo", "f2", "s", "yg", "yo", "f3"), 8),
        "act_ready": (("n1", "ao", "f1", "fp", "fo", "f2", "s", "yg", "yo", "f3"), 8),
        "squares": (("n1", "f1", "fp", "pm0", "f2", "pf0", "s", "pm1", "f3", "pf1"), 2),
        "head_sums": (("q", "k", "ln", "blk0", "blk1", "blk2", "blk3"), 1),
        "var": (("n1", "q", "k", "ln", "f1", "fp", "blk0", "blk1", "blk2", "blk3", "pm0", "f2", "pf0", "s",
                 "pm1", "f3", "pf1"), 1),
        "rstd": (("n1", "q", "k", "ln", "f1", "fp", "blk0", "blk1", "blk2", "blk3", "pm0", "f2", "pf0", "s",
                  "pm1", "f3", "pf1"), 1),
        "x_ready": (("f1", "fp", "pm0", "pf0", "pm1", "pf1"), 2),
        "normed": (("pm0", "pf0", "pm1", "pf1"), 2),
        "sq": (("q", "k", "blk0", "blk1", "blk2", "blk3"), 2),
        "silu": (("f1", "f2", "f3"), FP), "prod": (("f1", "f2", "f3"), FP),
        "ghigh": (("f1", "f2", "f3"), FP), "glow": (("f1", "f2", "f3"), FP),
        "probs": (("a1", "a2"), {"a1": 2 * H1, "a2": 2 * H2}), "max": (("a1", "a2"), {"a1": 2 * H1, "a2": 2 * H2}),
        "scores": (("a1", "a2"), {"a1": H1, "a2": H2}), "turned": (("a1", "a2"), {"a1": H1, "a2": H2}),
        "pt": (("a1", "a2"), {"a1": H1, "a2": H2}), "out": (("a1", "a2"), {"a1": H1, "a2": H2}),
        "heads_in": (("a1", "a2"), {"a1": H1, "a2": H2}), "heads_out": (("a1", "a2"), {"a1": H1, "a2": H2}),
    }

    def resolve(self, name):
        stage, _, kind = name.partition("_")
        stages, count = self.KINDS.get(kind, ((), 0))
        if stage not in stages:
            return name, 0
        counts = {s: count[s] if isinstance(count, dict) else count for s in stages}
        if kind in ("transposed", "high_ready", "act_ready"):
            counts["ao"] = KT // 2
        return "all_" + kind, sum(counts[s] for s in stages[:stages.index(stage)])

    def sem(self, name):
        shared, _ = self.resolve(name)
        if shared not in self.sems:
            self.sems[shared] = self.ctx.enter_context(self.nc.semaphore(shared))
        return self.sems[shared]

    def past(self, name, value):
        return self.sem(name), self.resolve(name)[1] + value

    def plan_units(self):
        io = self.io
        self.units = []
        self.first = {}

        def rows_by(w, cols, width):
            return w[:, cols:cols + width].rearrange("(k p) c -> p k c", p=P)

        def feature_pairs(name, w, c0, n):
            self.first[name] = len(self.units)
            for i in range(n):
                self.units.append((rows_by(w, c0 + 256 * i, 256), 8))

        def half_k(name, w, c0, blocks):
            self.first[name] = len(self.units)
            for b in range(blocks):
                for hk in range(2):
                    v = w[hk * 512:(hk + 1) * 512, c0 + 512 * b:c0 + 512 * b + 512]
                    self.units.append((v.rearrange("(k p) c -> p k c", p=P), 4))

        def k_pairs(name, w, n):
            self.first[name] = len(self.units)
            for i in range(n):
                self.units.append((w[i * 256:(i + 1) * 256, :].rearrange("(k p) c -> p k c", p=P), 2))

        def ffn(name, wg, wu, wd):
            self.first[name + ".up"] = len(self.units)
            for f in range(FP):
                self.units.append((rows_by(wg, 256 * f, 256), 8))
                self.units.append((rows_by(wu, 256 * f, 256), 8))
            k_pairs(name + ".down", wd, FT // 2)

        w_in = io["w_in"][0]
        feature_pairs("u", w_in, 3 * AW, 4)
        half_k("q", w_in, 0, 1)
        half_k("k", w_in, AW, 1)
        half_k("v", w_in, 2 * AW, 1)
        k_pairs("o1", io["w_out"][0], 4)
        ffn("f1", io["w_gate"][0], io["w_up"][0], io["w_down"][0])
        fox = io["fox_w_in_2"][0]
        for name, c0 in (("fox", D), ("q0", 0), ("v0", 2 * D), ("k1", D + 512), ("q1", 512), ("v1", 2 * D + 512),
                         ("g0", 3 * D), ("g1", 3 * D + 512)):
            half_k(name, fox, c0, 1)
        k_pairs("o2", io["fox_w_out_2"][0], 4)
        ffn("f2", io["ffn_w_gate_2"][0], io["ffn_w_up_2"][0], io["ffn_w_down_2"][0])
        half_k("s", io["s5_w_in_2"][0], 0, 2)
        k_pairs("glu", io["s5_w_glu_2"][0], 4)
        k_pairs("o3", io["s5_w_out_2"][0], 4)
        ffn("f3", io["ffn_w_gate_2"][1], io["ffn_w_up_2"][1], io["ffn_w_down_2"][1])

    def place(self):
        nc, ctx = self.nc, self.ctx
        end = nc.sbuf_usable_end
        cur = (nc.sbuf_base + 63) // 64 * 64

        def at(name, shape, dt, offset):
            return nc.alloc_sbuf_tensor_at(name, shape, dt, offset=offset)

        def fixed(name, shape, dt):
            nonlocal cur
            t = at(name, shape, dt, cur)
            self.where[name] = cur
            cur += (int(np.prod(shape[1:])) * (2 if dt == BF16 else 4) + 31) // 32 * 32
            return t

        self.where = {}
        self.x = fixed("x_res", [P, RT, D], F32)
        self.nat = fixed("nat", [P, RT, D], F32)
        self.actH = fixed("actH", [P, KT, TOK], F32R)
        self.actL = fixed("actL", [P, KT, TOK], F32R)
        self.wraw = fixed("wraw", [P, RAW, UNIT], F32)
        self.whi = fixed("whi", [P, RING, UNIT], F32R)
        self.wlo = fixed("wlo", [P, RING, UNIT], F32R)
        self.gb = [fixed(f"postgain{i}", [P, D], F32) for i in range(2)]
        self.ident = fixed("ident", [P, P], F32)
        self.ones = fixed("ones", [P, P], F32)
        self.tri = fixed("tri", [P, P], F32)
        self.swap = fixed("swap", [P, P], F32)
        self.identb = fixed("identb", [P, P], BF16)
        self.maskb = fixed("maskb", [P, P], BF16)
        self.vectors = fixed("vectors", [P, VCOLS + TAPS * 4], F32)
        self.vec, self.taps = self.vectors[:, 0:VCOLS], self.vectors[:, VCOLS:]
        self.mhalf = fixed("mhalf", [P, 16], F32)
        self.halfpi = fixed("halfpi", [P, 1], F32)
        self.zero1 = fixed("zero1", [P, 1], F32)
        self.ss = fixed("ss", [P, 16], F32)
        self.rs = fixed("rs", [P, 16], F32)
        self.cosT = fixed("cosT", [P, NG], F32)
        self.sinT = fixed("sinT", [P, NG], F32)
        self.magT = fixed("magT", [P, NG], F32)
        self.qkg = fixed("qkg", [P, 4, HD], F32)
        self.nmax, self.rsum, self.rinv = (fixed(n, [P, RT, H2], F32) for n in ("nmax", "rsum", "rinv"))
        R0 = cur

        class Pen:
            def __init__(s, base, top=end):
                s.cur, s.top = base, top

            def __call__(s, name, shape, dt=F32):
                t = at(name, shape, dt, s.cur)
                self.where[name] = s.cur
                s.cur += (int(np.prod(shape[1:])) * (2 if dt == BF16 else 4) + 31) // 32 * 32
                assert s.cur <= s.top, (name, s.cur, s.top)
                return t

        prep_bytes = 4 * 4096 + 2 * 2304 + 2 * 2048
        work_bytes = 2 * 2048 + 2304 + 2 * 2304 + 2 * 2048 + 2 * 4096
        W0 = end - end % 32 - work_bytes
        P0 = W0 - prep_bytes
        pen = Pen(P0, W0)
        self.BB1, self.BB2 = pen("BB1", [P, NG, SC]), pen("BB2", [P, NG, SC])
        self.C12 = pen("C12", [P, 2, NG, SC])
        self.C1, self.C2 = self.C12[:, 0], self.C12[:, 1]
        self.F1, self.F2 = pen("F1", [P, NG, T + 1]), pen("F2", [P, NG, T + 1])
        self.G1, self.G2 = pen("G1", [P, NG, T]), pen("G2", [P, NG, T])
        pen = Pen(W0)
        self.rtb = pen("rtb", [P, 2, GB, T, SC])
        self.ob = pen("ob", [P, 2, GB, T + 1, SC])
        self.otmp = pen("otmp", [P, GB, T + 1, SC])
        self.rsb = pen("rsb", [P, 2, GB, P])
        self.ksb = pen("ksb", [SC, 2, GB, 2 * P])
        pen = Pen(W0)
        self.Bri = pen("Bri", [P, 2, NG, SC])
        self.btmp = pen("btmp", [P, NG, SC])
        pen = Pen(W0)
        self.AR, self.AI = pen("AR", [P, NG, T + 1]), pen("AI", [P, NG, T + 1])
        self.atmp, self.atmp2 = pen("atmp", [P, NG, 4]), pen("atmp2", [P, NG, 4])
        pen = Pen(self.where["postgain0"], self.where["postgain0"] + 8192)
        self.lamdt = pen("s5_lamdt", [P, 3, NG])
        self.small = {n: self.lamdt[:, i] for i, n in enumerate(("LR", "LI", "ldt"))}
        self.small |= {n: pen("s5_" + n, [P, NG]) for n in
                      ("dt lr th k t thr ab sh tt lrc lrb eb r1 r2 den rden em ar ai nre zr zi "
                       "m1").split()}

        pen = Pen(R0, P0)
        self.hpad = pen("hpad", [P, 4, TAPS - 1 + TOK])
        self.cacc = pen("cacc", [P, 4, TOK])
        self.csig = pen("csig", [P, 4, TOK])
        self.qn, self.kn = pen("qn", [P, RT, AW]), pen("kn", [P, RT, AW])
        self.vn = pen("vn", [P, RT, AW])
        self.qt, self.kt1 = pen("qt1", [HD, H1, TOK]), pen("kt1", [HD, H1, TOK])
        self.p1 = pen("p1", [P, 2, 384])
        self.pt1 = pen("pt1", [P, 2, 384])
        self.ropeg = pen("ropeg", [P, 2, RT, 2, HD])
        self.ctmp = pen("ctmp", [P, TOK])
        self.dtaps = at("dtaps", [P, 2 * TAPG, P], F32, self.where["nat"])
        self.sq1 = at("sq1", [P, RT, AW], F32, self.where["csig"])
        self.csq = at("csq", [P, 4, TOK], F32, self.where["csig"])
        self.rope = at("rope", [P, RT, 2, HD], F32, self.where["pt1"] + 2048)
        self.diag = at("diag", [P, 2 * P], F32, self.where["p1"])
        self.rtmp = at("rtmp", [P, AW], F32, self.where["p1"])
        self.rtmp2 = at("rtmp2", [P, AW], F32, self.where["pt1"])

        pen = Pen(R0, P0)
        self.gH, self.gL = pen("gH", [P, FT, TOK], F32R), pen("gL", [P, FT, TOK], F32R)
        self.sg = pen("sg", [P, 2 * TOK])
        self.prod = pen("prod", [P, 2 * TOK])

        pen = Pen(R0)
        AUG = HD + 2
        self.qa, self.ka = pen("qa", [P, RT, H2, AUG]), pen("ka", [P, RT, H2, AUG])
        self.va = pen("va", [P, RT, D])
        self.ga = pen("ga", [P, RT, D])
        self.qt2, self.kt2 = pen("qt2", [AUG, H2, TOK]), pen("kt2", [AUG, H2, TOK])
        self.p2, self.pt2 = pen("p2", [P, 2, 384]), pen("pt2", [P, 2, 384])
        self.sq2 = pen("sq2", [P, RT, 512])
        self.wf = pen("wf", [P, KT, H2])
        self.wfH, self.wfL = pen("wfH", [P, KT, H2], F32R), pen("wfL", [P, KT, H2], F32R)
        self.fb = pen("fb", [P, H2])
        self.fl = pen("fl", [P, 4, RT, H2])

        pen = Pen(R0)
        self.RTab = pen("RTab", [P, NG, P])
        self.OTab = pen("OTab", [P, NG, P])
        self.Uall = pen("Uall", [P, 16, 4, NCH])
        self.CT, self.ST = pen("CT", [P, NG, NCH]), pen("ST", [P, NG, NCH])
        d0 = pen.cur
        self.D0 = pen("D0", [P, NG, NCH])
        self.X33 = at("X33", [P, NG, NCH + 1], F32, d0)
        self.dsk = self.gb[1]
        self.TTab = at("TTab", [P, NG, P], F32, R0)
        self.sgl = at("sgl", [P, RT, D], F32, R0)
        self.V = at("Vst", [P, NG, NCH], F32, self.where["actH"])
        self.W = at("Wst", [P, NG, NCH], F32, self.where["actL"])
        self.Un = at("Un", [P, T, 16, SC], F32, self.where["actH"])
        self.Ur = at("Ur", [P, 16, T, SC], F32, self.where["actL"])
        self.Ysb = at("Ysb", [P, T, 16, SC], F32, self.where["actH"])
        self.ud = at("ud", [P, RT, D], F32, self.where["actL"])
        self.ctmp1 = at("ctmp1", [P, NG, 16], F32, self.where["Uall"])
        self.ctmp2 = at("ctmp2", [P, NG, 16], F32, self.where["Uall"] + 4096)

        self.ps = ctx.enter_context(nc.psum_tensor("ps", [P, 8, 512], F32))
        dr = lambda n, s: nc.dram_tensor(n, s, F32, kind="Internal").ap()
        self.Rd, self.Od = dr("R_dram", [P, NG, P]), dr("O_dram", [P, NG, P])
        self.Kd = dr("K_dram", [SC, NG, 2 * P])
        self.ud_d, self.yd_d = dr("u_dram", [TOK, D]), dr("y_dram", [TOK, D])
        s = self.sem
        self.landed = [s(f"raw_landed{i}") for i in range(RAW)]
        self.hi_done, self.lo_done, self.used = s("hi_done"), s("lo_done"), s("unit_used")

    def load_unit(self, sp, n0, view, it=0):
        n = n0 + 4 * it
        if n0 >= RAW:
            sp.wait_ge(self.lo_done, n - RAW + 1)
        k = view.shape[1]
        dst = self.wraw[:, n0 % RAW, :].rearrange("p (k c) -> p k c", k=k)
        sp.dma_start(dst, view).then_inc(self.landed[n0 % RAW], 16)

    def split_high(self, act, n0, it=0):
        n = n0 + 4 * it
        act.wait_ge(self.landed[n0 % RAW], 16 * (n0 // RAW + 1) + 16 * it)
        if n0 >= RING:
            act.wait_ge(self.used, n - RING + 1)
        act.activation(self.whi[:, n0 % RING, :], self.wraw[:, n0 % RAW, :], ACT.Copy).then_inc(self.hi_done, 1)

    def split_low(self, dve, n0, it=0):
        n = n0 + 4 * it
        dve.wait_ge(self.hi_done, n + 1)
        dve.tensor_tensor(self.wlo[:, n0 % RING, :], self.wraw[:, n0 % RAW, :],
                          self.whi[:, n0 % RING, :].bitcast(F32), ALU.subtract).then_inc(self.lo_done, 1)

    def mm_features(self, pe, n0, bank, it=0, ready=None):
        pe.wait_ge(self.lo_done, n0 + 4 * it + 1)
        s = n0 % RING
        for f in range(2):
            out = self.ps[:, bank, f * TOK:(f + 1) * TOK]
            for k in range(KT):
                if ready is not None and f == 0:
                    pe.wait_ge(*self.past(ready, k + 1))
                c = k * 256 + f * P
                wh, wl = self.whi[:, s, c:c + P], self.wlo[:, s, c:c + P]
                pe.matmul(out, wh, self.actH[:, k, :], start=(k == 0), stop=False)
                pe.matmul(out, wh, self.actL[:, k, :], start=False, stop=False)
                last = pe.matmul(out, wl, self.actH[:, k, :], start=False, stop=(k == KT - 1))
        last.then_inc(self.used, 1)

    def mm_quarter(self, pe, n0, banks, half, k, ready=None):
        if k == 0:
            pe.wait_ge(self.lo_done, n0 + 1)
        s = n0 % RING
        ka = 4 * half + k
        if ready is not None:
            pe.wait_ge(*self.past(ready, ka + 1))
        wh, wl = self.whi[:, s, k * 512:(k + 1) * 512], self.wlo[:, s, k * 512:(k + 1) * 512]
        for r in range(RT):
            out = self.ps[:, banks[r], :]
            xh, xl = self.actH[:, ka, r * P:(r + 1) * P], self.actL[:, ka, r * P:(r + 1) * P]
            pe.matmul(out, xh, wh, start=(ka == 0), stop=False)
            pe.matmul(out, xh, wl, start=False, stop=False)
            last = pe.matmul(out, xl, wh, start=False, stop=(ka == KT - 1))
        if k == 3:
            last.then_inc(self.used, 1)

    def mm_half_k(self, pe, n0, banks, half, ready=None):
        for k in range(4):
            self.mm_quarter(pe, n0, banks, half, k, ready)

    def mm_k_pair(self, pe, n0, base, xh, xl, k0, kn, waits=()):
        pe.wait_ge(self.lo_done, n0 + 1)
        s = n0 % RING
        for k in range(2):
            for name, value in waits:
                pe.wait_ge(*self.past(name, value + k))
            for r in range(RT):
                h, l = xh[:, k0 + k, r * P:(r + 1) * P], xl[:, k0 + k, r * P:(r + 1) * P]
                w = [[t[:, s, k * 1024 + c * 512:k * 1024 + (c + 1) * 512] for c in range(2)]
                     for t in (self.whi, self.wlo)]
                st, sp_ = k0 + k == 0, k0 + k == kn - 1
                for c in range(2):
                    pe.matmul(self.ps[:, base + 2 * r + c, :], h, w[0][c], start=st, stop=False)
                for c in range(2):
                    pe.matmul(self.ps[:, base + 2 * r + c, :], h, w[1][c], start=False, stop=False)
                for c in range(2):
                    last = pe.matmul(self.ps[:, base + 2 * r + c, :], l, w[0][c], start=False, stop=sp_)
        last.then_inc(self.used, 1)

    def tp_spot(self, kt, banks):
        b, h = banks[kt % len(banks)], kt // len(banks)
        return self.ps[:, b, h * TOK:(h + 1) * TOK]

    def pe_turn(self, pe, st, banks, n=KT, natural_ready=None):
        tp = self.sem(st + "_transposed")
        for kt in range(n):
            if kt >= len(banks):
                pe.wait_ge(*self.past(st + "_act_ready", kt - len(banks) + 1))
            for r in range(RT):
                if kt == 0:
                    pe.wait_ge(*self.past(st + "_nat_ready", r + 1))
                last = pe.transpose(self.tp_spot(kt, banks)[:, r * P:(r + 1) * P],
                                    self.nat[:, r, kt * P:(kt + 1) * P], self.ident[:])
            last.then_inc(tp, 1)

    def act_turn(self, act, st, banks, n=KT, gain=None):
        for kt in range(n):
            act.wait_ge(*self.past(st + "_transposed", kt + 1))
            g = 1.0 if gain is None else self.vec[:, gain + kt:gain + kt + 1]
            act.activation(self.actH[:, kt, :], self.tp_spot(kt, banks), ACT.Copy, scale=g)\
               .then_inc(self.sem(st + "_high_ready"), 1)

    def dve_turn(self, dve, st, banks, n=KT, gain=None):
        for kt in range(n):
            dve.wait_ge(*self.past(st + "_high_ready", kt + 1))
            hi = self.actH[:, kt, :].bitcast(F32)
            if gain is None:
                i = dve.tensor_tensor(self.actL[:, kt, :], self.tp_spot(kt, banks), hi, ALU.subtract)
            else:
                i = dve.scalar_tensor_tensor(self.actL[:, kt, :], self.tp_spot(kt, banks),
                                             self.vec[:, gain + kt:gain + kt + 1], hi, ALU.mult, ALU.subtract)
            i.then_inc(self.sem(st + "_act_ready"), 1)

    def act_squares(self, act, st, src, ready=None, values=None):
        for r in range(RT):
            if ready is not None:
                act.wait_ge(*self.past(ready, values[r]))
            act.activation(self.nat[:, r, :], src(r), ACT.Square, accum_out=self.ss[:, r:r + 1])\
               .then_inc(self.sem(st + "_squares"), 1)

    def pool_rstd(self, pool, st, n, mean_of, ready, value):
        pool.wait_ge(*self.past(ready, value))
        pool.tensor_scalar(self.rs[:, 0:n], self.ss[:, 0:n], 1.0 / mean_of, EPS, ALU.mult, ALU.add)\
            .then_inc(self.sem(st + "_var"), 1)
        pool.wait_ge(*self.past(st + "_var", 1))
        pool.tensor_tensor(self.rs[:, 0:n], self.rs[:, 0:n], self.mhalf[:, 0:n], ALU.pow)\
            .then_inc(self.sem(st + "_rstd"), 1)

    def dve_scale(self, dve, st):
        dve.wait_ge(*self.past(st + "_rstd", 1))
        for r in range(RT):
            dve.tensor_scalar(self.nat[:, r, :], self.x[:, r, :], self.rs[:, r:r + 1], None, ALU.mult)\
               .then_inc(self.sem(st + "_nat_ready"), 1)

    def acc_row(self, base, r):
        return self.ps[:, base + 2 * r:base + 2 * r + 2, :]

    def dve_postnorm(self, dve, st, base, gain, gain_ready, gain_value):
        dve.wait_ge(*self.past(st + "_rstd", 1))
        dve.wait_ge(*self.past(gain_ready, gain_value))
        g = gain[:].rearrange("p (a b) -> p a b", a=2)
        for r in range(RT):
            t = self.nat[:, r, :].rearrange("p (a b) -> p a b", a=2)
            dve.scalar_tensor_tensor(t, self.acc_row(base, r), self.rs[:, r:r + 1], g, ALU.mult, ALU.mult)\
               .then_inc(self.sem(st + "_normed"), 1)
        for r in range(RT):
            dve.wait_ge(*self.past(st + "_normed", r + 1))
            dve.tensor_tensor(self.x[:, r, :], self.x[:, r, :], self.nat[:, r, :], ALU.add)\
               .then_inc(self.sem(st + "_x_ready"), 1)

    def ffn_banks(self, a):
        return a, a + 1, (4 if a == 0 else 0)

    def pe_pair(self, pe, st, n0, a, f0, it=0, f_step=0, ready=None):
        f = f0 + f_step * it
        if f0 > 0:
            pe.wait_ge(*self.past(st + "_silu", f))
        self.mm_features(pe, n0, a, it, ready)
        if f0 > 0:
            pe.wait_ge(*self.past(st + "_prod", f))
        self.mm_features(pe, n0 + 1, a + 1, it)

    def act_pair(self, act, st, n0, a, f0, it=0, f_step=0):
        f = f0 + f_step * it
        act.wait_ge(self.used, n0 + 4 * it + 1)
        if f0 > 0:
            act.wait_ge(*self.past(st + "_prod", f))
        act.activation(self.sg[:], self.ps[:, a, :], ACT.Silu).then_inc(self.sem(st + "_silu"), 1)
        self.split_high(act, n0 + 2, it)
        self.split_high(act, n0 + 3, it)
        act.wait_ge(*self.past(st + "_prod", f + 1))
        dst = self.gH[:, bass.ds(2 * f, 2), :] if f_step else self.gH[:, 2 * f:2 * f + 2, :]
        act.activation(dst, self.prod[:].rearrange("p (a b) -> p a b", a=2), ACT.Copy)\
           .then_inc(self.sem(st + "_ghigh"), 1)

    def dve_pair(self, dve, st, n0, a, f0, it=0, f_step=0):
        f = f0 + f_step * it
        self.split_low(dve, n0 + 2, it)
        dve.wait_ge(self.used, n0 + 4 * it + 2)
        dve.wait_ge(*self.past(st + "_silu", f + 1))
        if f0 > 0:
            dve.wait_ge(*self.past(st + "_glow", f))
        dve.tensor_tensor(self.prod[:], self.sg[:], self.ps[:, a + 1, :], ALU.mult)\
           .then_inc(self.sem(st + "_prod"), 1)
        self.split_low(dve, n0 + 3, it)
        dve.wait_ge(*self.past(st + "_ghigh", f + 1))
        hi = self.gH[:, bass.ds(2 * f, 2), :] if f_step else self.gH[:, 2 * f:2 * f + 2, :]
        lo = self.gL[:, bass.ds(2 * f, 2), :] if f_step else self.gL[:, 2 * f:2 * f + 2, :]
        dve.tensor_tensor(lo, self.prod[:].rearrange("p (a b) -> p a b", a=2), hi.bitcast(F32), ALU.subtract)\
           .then_inc(self.sem(st + "_glow"), 1)

    def over_pairs(self, eng, one, prep=None):
        one(0, 0, 0, 0)
        if prep:
            prep(0, 0, 0)
        with eng.Fori(0, (FP - 1) // 2) as it:
            for j in range(2):
                one(2 + 2 * j, 1 + j, it, 2)
                if prep:
                    prep(1 + j, it, 2)

    def pe_ffn(self, pe, st, a, prep=False):
        n = self.first[st + ".up"]
        act_ready = st + "_act_ready"
        self.over_pairs(pe, lambda dn, f0, it, fs: self.pe_pair(
            pe, st, n + dn, a, f0, it, fs, act_ready if dn == 0 else None),
            (lambda b0, it, bs: self.pe_prep(pe, a, b0, it, bs)) if prep else None)
        n = self.first[st + ".down"]
        base = self.ffn_banks(a)[2]
        for i in range(FT // 2):
            if i == 0:
                pe.wait_ge(*self.past(act_ready, KT))
            pe.wait_ge(*self.past(st + "_glow", i + 1))
            self.mm_k_pair(pe, n + i, base, self.gH, self.gL, 2 * i, FT)
            if prep and i % 2 == 1:
                self.pe_prep(pe, a, FP + i // 2)

    def act_ffn(self, act, st, a, prep=False):
        n = self.first[st + ".up"]
        self.over_pairs(act, lambda dn, f0, it, fs: self.act_pair(act, st, n + dn, a, f0, it, fs),
                        (lambda b0, it, bs: self.act_prep(act, a, b0, it, bs)) if prep else None)
        n = self.first[st + ".down"]
        for i in range(FT // 2):
            if n + i + 2 < len(self.units) and i < FT // 2 - 1:
                self.split_high(act, n + i + 2)
            if prep and i % 2 == 1:
                self.act_prep(act, a, FP + i // 2)

    def dve_ffn(self, dve, st, a):
        n = self.first[st + ".up"]
        self.over_pairs(dve, lambda dn, f0, it, fs: self.dve_pair(dve, st, n + dn, a, f0, it, fs))
        n = self.first[st + ".down"]
        for i in range(FT // 2 - 1):
            if n + i + 2 < len(self.units):
                self.split_low(dve, n + i + 2)

    def pool_prep(self, pool, b0, it=0, step=0):
        b = b0 + step * it
        half = b0 // 2 + it if step else b0 // 2
        done = self.sem("prep_pool")
        s = b0 % 2
        if b0 > 0:
            pool.wait_ge(*self.past("prep_kmul", b if b0 == 1 else b - 1))
            pool.wait_ge(*self.past(f"prep_stored{s}", 48 * half + 1))
        g = bass.ds(GB * b, GB) if step else slice(GB * b, GB * b + GB)

        def times(out, f, w, n):
            return pool.tensor_tensor(out, f[:, g, :].unsqueeze(3).to_broadcast([P, GB, n, SC]),
                                      w[:, g, :].unsqueeze(2).to_broadcast([P, GB, n, SC]), ALU.mult)

        if b0 > 0:
            pool.wait_ge(done, 6 * b)
        r, o, t = self.rtb[:, s], self.ob[:, s], self.otmp
        times(r, self.G1, self.BB1, T).then_inc(done, 1)
        times(t[:, :, 0:T, :], self.G2, self.BB2, T).then_inc(done, 1)
        pool.wait_ge(done, 6 * b + 2)
        pool.tensor_tensor(r, r, t[:, :, 0:T, :], ALU.add).then_inc(done, 1)
        times(o, self.F1, self.C1, T + 1).then_inc(done, 1)
        pool.wait_ge(done, 6 * b + 3)
        times(t[:], self.F2, self.C2, T + 1).then_inc(done, 1)
        pool.wait_ge(done, 6 * b + 5)
        pool.tensor_tensor(o, o, t[:], ALU.add).then_inc(done, 1)

    def pe_prep(self, pe, a, b0, it=0, step=0):
        b = b0 + step * it
        s = b0 % 2
        pe.wait_ge(*self.past("prep_pool", 6 * b + 6))
        if b0 > 0:
            pe.wait_ge(*self.past("prep_rout", b))
            pe.wait_ge(*self.past("prep_kout", b))
        for i in range(GB):
            last = pe.transpose(self.ps[:, a + 2, i * P:(i + 1) * P],
                                self.rtb[:, s, i, :, :].rearrange("p t c -> p (t c)"), self.ident[:])
        last.then_inc(self.sem("prep_turned"), 1)
        for i in range(GB):
            last = pe.matmul(self.ps[0:SC, a + 3, i * P:(i + 1) * P], self.rtb[:, s, i, T - 1, :],
                             self.ob[:, s, i, 0:T, :].rearrange("p t c -> p (t c)"), start=True, stop=True)
        last.then_inc(self.sem("prep_kmul"), 1)

    def act_prep(self, act, a, b0, it=0, step=0):
        b = b0 + step * it
        half = b0 // 2 + it if step else b0 // 2
        s = b0 % 2
        act.wait_ge(*self.past("prep_turned", b + 1))
        act.wait_ge(*self.past(f"prep_stored{s}", 48 * half + 1))
        act.activation(self.rsb[:, s], self.ps[:, a + 2, :].rearrange("p (i c) -> p i c", i=GB), ACT.Copy)\
           .then_inc(self.sem("prep_rout"), 1)
        act.wait_ge(*self.past("prep_kmul", b + 1))
        act.activation(self.ksb[:, s, :, P:2 * P],
                       self.ps[0:SC, a + 3, :].rearrange("p (i c) -> p i c", i=GB), ACT.Copy)\
           .then_inc(self.sem("prep_kout"), 1)
        act.wait_ge(*self.past("prep_kout", b + 1))
        g = bass.ds(GB * b, GB) if step else slice(GB * b, GB * b + GB)
        stored = self.sem(f"prep_stored{s}")
        act.dma_start(self.Rd[:, g, :], self.rsb[:, s]).then_inc(stored, 16)
        act.dma_start(self.Kd[:, g, :], self.ksb[:, s]).then_inc(stored, 16)
        act.dma_start(self.Od[:, g, :].rearrange("p g (t c) -> p g t c", c=SC),
                      self.ob[:, s, :, 1:T + 1, :]).then_inc(stored, 16)

    def pe_attention(self, pe, st, heads, qt, kt, v, p, pt, sb, tb, o_at, between=None):
        h0, h1 = heads

        def scores(h):
            if h >= 2:
                pe.wait_ge(*self.past(st + "_probs", 2 * (h - 1)))
            b = sb[h % 2]
            for r in range(RT):
                c0, nk = (0, P) if r == 0 else (P, 2 * P)
                out = self.ps[:, b, c0:c0 + nk]
                pe.matmul(out, qt[:, h, r * P:(r + 1) * P], kt[:, h, 0:nk], start=True, stop=False)
                last = pe.matmul(self.ps[:, b, c0 + nk - P:c0 + nk], self.identb[:], self.maskb[:],
                                 start=False, stop=True)
            last.then_inc(self.sem(st + "_scores"), 1)

        def turn(h):
            pe.wait_ge(*self.past(st + "_probs", 2 * (h + 1)))
            if h >= 2:
                pe.wait_ge(*self.past(st + "_pt", h - 1))
            for i in range(3):
                last = pe.transpose(self.ps[:, tb[h % 2], i * P:(i + 1) * P], p[:, h % 2, i * P:(i + 1) * P],
                                    self.ident[:])
            last.then_inc(self.sem(st + "_turned"), 1)

        def values(h):
            pe.wait_ge(*self.past(st + "_pt", h + 1))
            for r in range(RT):
                for k in range(r + 1):
                    i = r + k
                    last = pe.matmul(o_at(r, h), pt[:, h % 2, i * P:(i + 1) * P],
                                     v[:, k, h * HD:(h + 1) * HD], start=(k == 0), stop=(k == r))
            last.then_inc(self.sem(st + "_out"), 1)

        for h in range(h0, h1 + 2):
            if h < h1:
                scores(h)
                if between:
                    between(3 * h)
            if h0 + 1 <= h <= h1:
                turn(h - 1)
            if h < h1 and between:
                between(3 * h + 1)
            if h >= h0 + 2:
                values(h - 2)
            if h < h1 and between:
                between(3 * h + 2)

    def act_attention(self, act, st, h, p, rsum, nmax, sb):
        act.wait_ge(*self.past(st + "_max", 2 * (h + 1)))
        if h >= 2:
            act.wait_ge(*self.past(st + "_turned", h - 1))
        for r in range(RT):
            c0, nk = (0, P) if r == 0 else (P, 2 * P)
            act.activation(p[:, h % 2, c0:c0 + nk], self.ps[:, sb[h % 2], c0:c0 + nk], ACT.Exp,
                           bias=nmax[:, r, h:h + 1], accum_out=rsum[:, r, h:h + 1])\
               .then_inc(self.sem(st + "_probs"), 1)

    def dve_attention(self, dve, st, heads, pt, nmax, sb, tb, between=None):
        h0, h1 = heads
        for h in range(h0, h1 + 1):
            if h < h1:
                dve.wait_ge(*self.past(st + "_scores", h + 1))
                for r in range(RT):
                    c0, nk = (0, P) if r == 0 else (P, 2 * P)
                    dve.reduce_max(nmax[:, r, h:h + 1], self.ps[:, sb[h % 2], c0:c0 + nk], AX.X, negate=True)\
                       .then_inc(self.sem(st + "_max"), 1)
            if h > h0:
                g = h - 1
                dve.wait_ge(*self.past(st + "_turned", g + 1))
                if g >= 2:
                    dve.wait_ge(*self.past(st + "_out", g - 1))
                dve.tensor_copy(pt[:, g % 2, :], self.ps[:, tb[g % 2], 0:384]).then_inc(self.sem(st + "_pt"), 1)
            if between:
                between(h)

    def pe_heads(self, pe, st, src, heads, ready, value, banks, first_fill):
        pe.wait_ge(*self.past(ready, value))
        w = src.shape[-1]
        for f in range((heads[1] - heads[0]) // 2):
            n = first_fill + f
            if n >= 2:
                pe.wait_ge(*self.past(st + "_heads_out", n - 1))
            for i in range(2):
                for r in range(RT):
                    c = (2 * i + r) * P
                    last = pe.transpose(self.ps[0:w, banks[n % 2], c:c + P], src[:, r, heads[0] + 2 * f + i, :],
                                        self.ident[:])
            last.then_inc(self.sem(st + "_heads_in"), 1)

    def act_heads(self, act, st, dst, heads, banks, first_fill):
        w = dst.shape[0]
        for f in range((heads[1] - heads[0]) // 2):
            n = first_fill + f
            h = heads[0] + 2 * f
            act.wait_ge(*self.past(st + "_heads_in", n + 1))
            act.activation(dst[:, h:h + 2, :], self.ps[0:w, banks[n % 2], :].rearrange("p (h t) -> p h t", h=2),
                           ACT.Copy).then_inc(self.sem(st + "_heads_out"), 1)


class Chain:

    def __init__(self, eng, sem):
        self.eng, self.sem, self.n = eng, sem, 0

    def step(self, ins):
        ins.then_inc(self.sem, 1)
        self.n += 1
        return self.n

    def wait(self, n=None):
        self.eng.wait_ge(self.sem, self.n if n is None else n)

    def __call__(self, ins):
        self.step(ins)
        self.wait()


def pool_constants(m, pool):
    c = Chain(pool, m.sem("pool_chain"))
    for t, v in ((m.ident, 0.0), (m.ones, 1.0), (m.tri, 1.0), (m.swap, 0.0), (m.identb, 0.0), (m.maskb, 0.0),
                 (m.mhalf, -0.5), (m.halfpi, math.pi / 2), (m.hpad[:, :, 0:TAPS - 1], 0.0)):
        c.step(pool.memset(t[:] if not isinstance(t, bass.AP) else t, v))
    c.wait()

    def select(t, op, fill, base, step, mult):
        c.step(pool.affine_select(out=t, in_=t, compare_op=op, fill=fill, base=base,
                                  pattern=[[step, t.shape[-1]]], channel_multiplier=mult))

    select(m.ident[:], ALU.not_equal, 1.0, 0, -1, 1)
    select(m.identb[:], ALU.not_equal, 1.0, 0, -1, 1)
    select(m.tri[:], ALU.is_ge, 0.0, 0, 1, -1)
    select(m.maskb[:], ALU.is_ge, NEG, 0, -1, 1)
    select(m.swap[:, 0:64], ALU.not_equal, 1.0, -64, -1, 1)
    select(m.swap[:, 64:128], ALU.not_equal, 1.0, 0, -1, 1)
    c.wait()
    pool.memset(m.zero1[:], 0.0).then_inc(m.sem("consts"), 1)
    return c


def cmul(c, pool, out, x, y, tmp, shape):
    (orr, oi), (xr, xi), (yr, yi) = out, x, y
    t1, t2 = tmp
    c.step(pool.tensor_tensor(orr, xr, yr, ALU.mult))
    c.step(pool.tensor_tensor(t1, xi, yi, ALU.mult))
    c.step(pool.tensor_tensor(oi, xr, yi, ALU.mult))
    c.step(pool.tensor_tensor(t2, xi, yr, ALU.mult))
    c.wait()
    c.step(pool.tensor_tensor(orr, orr, t1, ALU.subtract))
    c.step(pool.tensor_tensor(oi, oi, t2, ALU.add))
    c.wait()


def powers(c, pool, tr, ti, base, tmp1, tmp2, count):
    c.step(pool.memset(tr[:, :, 0:1], 1.0))
    c.step(pool.memset(ti[:, :, 0:1], 0.0))
    c.step(pool.tensor_copy(tr[:, :, 1:2], base[0].unsqueeze(2)))
    c.step(pool.tensor_copy(ti[:, :, 1:2], base[1].unsqueeze(2)))
    c.wait()
    n = 1
    while n < count - 1:
        k = min(n, count - 1 - n)
        b = [t[:, :, n:n + 1].to_broadcast([P, NG, k]) for t in (tr, ti)]
        cmul(c, pool, (tr[:, :, n + 1:n + 1 + k], ti[:, :, n + 1:n + 1 + k]),
             (tr[:, :, 1:1 + k], ti[:, :, 1:1 + k]), b, (tmp1[:, :, 0:k], tmp2[:, :, 0:k]), None)
        n += k


TWO_PI = 2 * math.pi
PI_A = 6.28125
PI_B = math.floor((TWO_PI - PI_A) * 2 ** 21) / 2 ** 21
PI_C = float(np.float32(TWO_PI - PI_A - PI_B))
ROUND = 12582912.0


def pool_s5_scalars(m, c, pool):
    s = {k: v[:] for k, v in m.small.items()}
    pool.wait_ge(*m.past("lamdt_in", 16))
    pool.wait_ge(*m.past("dt", 1))
    tt, ts = pool.tensor_tensor, pool.tensor_scalar
    c.step(tt(s["lr"], s["LR"], s["dt"], ALU.mult))
    c.step(tt(s["th"], s["LI"], s["dt"], ALU.mult))
    c.wait()
    c.step(ts(s["lrc"], s["lr"], 1.0, None, ALU.min))
    c.step(ts(s["lrb"], s["lr"], 88.0, None, ALU.min))
    c(ts(s["k"], s["th"], 1.0 / TWO_PI, ROUND, ALU.mult, ALU.add))
    c(ts(s["k"], s["k"], ROUND, None, ALU.subtract))
    for i, part in enumerate((PI_A, PI_B, PI_C)):
        c(ts(s["t"], s["k"], part, None, ALU.mult))
        c(tt(s["thr"], s["th"] if i == 0 else s["thr"], s["t"], ALU.subtract))
    ts(s["thr"], s["thr"], 3.1415925, -3.1415925, ALU.min, ALU.max).then_inc(m.sem("angle"), 1)
    c.step(tt(s["den"], s["LR"], s["LR"], ALU.mult))
    c.step(tt(s["m1"], s["LI"], s["LI"], ALU.mult))
    c.wait()
    tt(s["den"], s["den"], s["m1"], ALU.add).then_inc(m.sem("den"), 1)


def pool_s5_growth(m, c, pool):
    s = {k: v[:] for k, v in m.small.items()}
    tt, ts = pool.tensor_tensor, pool.tensor_scalar
    pool.wait_ge(*m.past("s5_functions", 5))
    pool.wait_ge(*m.past("s5_recips", 2))
    c.step(ts(s["tt"], s["tt"], 2.0, None, ALU.mult))
    c.step(ts(s["eb"], s["eb"], 1.0, None, ALU.subtract))
    c.step(ts(s["m1"], s["lr"], 1.0, None, ALU.is_gt))
    c.wait()
    c(tt(s["em"], s["tt"], s["r1"], ALU.mult))
    c(tt(s["eb"], s["eb"], s["em"], ALU.subtract))
    c(tt(s["eb"], s["eb"], s["m1"], ALU.mult))
    c(tt(s["em"], s["em"], s["eb"], ALU.add))
    c.step(ts(m.magT[:], s["em"], 1.0, None, ALU.add))
    c.step(tt(s["nre"], s["em"], m.cosT[:], ALU.mult))
    c.step(tt(s["sh"], s["sh"], s["sh"], ALU.mult))
    c.wait()
    c.step(ts(s["sh"], s["sh"], 2.0, None, ALU.mult))
    c.step(tt(s["ar"], m.magT[:], m.cosT[:], ALU.mult))
    c.step(tt(s["ai"], m.magT[:], m.sinT[:], ALU.mult))
    c.wait()
    c(tt(s["nre"], s["nre"], s["sh"], ALU.subtract))
    for out, (a, b), (d, e), op in (("zr", ("nre", "LR"), ("ai", "LI"), ALU.add),
                                    ("zi", ("ai", "LR"), ("nre", "LI"), ALU.subtract)):
        c.step(tt(s[out], s[a], s[b], ALU.mult))
        c(tt(s["t"], s[d], s[e], ALU.mult))
        c(tt(s[out], s[out], s["t"], op))
        c(tt(s[out], s[out], s["rden"], ALU.mult))


def pool_s5_inputs(m, c, pool):
    s = m.small
    pool.wait_ge(*m.past("b_in", 16))
    z = [s[n][:].unsqueeze(2).to_broadcast([P, NG, SC]) for n in ("zr", "zi")]
    re, im = m.Bri[:, 0], m.Bri[:, 1]
    for out, a, b, op in ((m.BB1, re, im, ALU.subtract), (m.BB2, im, re, ALU.add)):
        c.step(pool.tensor_tensor(out[:], a, z[0], ALU.mult))
        c(pool.tensor_tensor(m.btmp[:], b, z[1], ALU.mult))
        c(pool.tensor_tensor(out[:], out[:], m.btmp[:], op))


def pool_s5_powers(m, c, pool):
    powers(c, pool, m.AR, m.AI, (m.small["ar"][:], m.small["ai"][:]), m.atmp, m.atmp2, T + 1)
    up, dn = slice(0, 64), slice(64, 128)
    rev = slice(T - 1, None, -1)
    for out, top, sign_t, bottom, sign_b, ks in (
            (m.F1, m.AR, 1.0, m.AI, -1.0, slice(0, T + 1)), (m.F2, m.AI, -1.0, m.AR, -1.0, slice(0, T + 1)),
            (m.G1, m.AR, 1.0, m.AI, 1.0, rev), (m.G2, m.AI, -1.0, m.AR, 1.0, rev)):
        c.step(pool.tensor_scalar(out[up, :, :], top[up, :, ks], sign_t, None, ALU.mult))
        c.step(pool.tensor_scalar(out[dn, :, :], bottom[dn, :, ks], sign_b, None, ALU.mult))
    c.wait()
    for s in range(2):
        pool.memset(m.ksb[:, s, :, 0:P], 0.0).then_inc(m.sem(f"prep_stored{s}"), 1)


def pool_s5_phases(m, c, pool):
    t = [m.ctmp1[:, :, i] for i in range(6)]
    cr, ci, mg = m.cosT[:], m.sinT[:], m.magT[:]
    n = 1
    while n < T:
        c.step(pool.tensor_tensor(t[0], cr, cr, ALU.mult))
        c.step(pool.tensor_tensor(t[1], ci, ci, ALU.mult))
        c.step(pool.tensor_tensor(t[2], cr, ci, ALU.mult))
        c.step(pool.tensor_tensor(t[3], mg, mg, ALU.mult))
        c.wait()
        c.step(pool.tensor_tensor(cr, t[0], t[1], ALU.subtract))
        c.step(pool.tensor_scalar(ci, t[2], 2.0, None, ALU.mult))
        c.step(pool.tensor_copy(mg, t[3]))
        c.wait()
        n *= 2
    powers(c, pool, m.CT, m.ST, (cr, ci), m.ctmp1, m.ctmp2, NCH)
    c(pool.tensor_scalar(m.ST[64:128, :, :], m.ST[64:128, :, :], -1.0, None, ALU.mult))
    c.step(pool.memset(m.D0[:, :, 0:1], 0.0))
    c.step(pool.tensor_copy(m.D0[:, :, 1:NCH], mg.unsqueeze(2).to_broadcast([P, NG, NCH - 1])))
    c.wait()
    pool.memset(m.zero1[:], 0.0).then_inc(m.sem("phases"), 1)


N1, N2, MIXPRE, FFNPRE, GLUB, DWB, LNG, LNB = 0, 8, 16, 32, 48, 56, 60, 64


def units_done(h):
    done = lambda h: 6 + 3 * h // 4 if h <= 8 else 12 + (h - 8) // 2
    return range(done(h), done(h + 1))


def build(nc, io, out):
    with ExitStack() as ctx:
        m = Program(nc, ctx, io)
        sem, ps, first = m.sem, m.ps, m.first
        nmax, rsum, rinv = m.nmax, m.rsum, m.rinv
        block = ctx.enter_context(nc.Block())
        X_IN = io["x"][0]

        @block.sync
        def _(sp):
            for r in range(RT):
                sp.dma_start(m.x[:, r, :], X_IN[r * P:(r + 1) * P, :]).then_inc(sem(f"x_in{r}"), 16)

            def ffn(st, wg, wu):
                n = first[st + ".up"]

                def pair(n0, c, it):
                    for i, w in enumerate((wg, wu)):
                        v = w[:, bass.ds(c, 256)] if it is not None else w[:, c:c + 256]
                        m.load_unit(sp, n0 + i, v.rearrange("(k p) c -> p k c", p=P), 0 if it is None else it)

                pair(n, 0, None)
                with sp.Fori(0, (FP - 1) // 2) as it:
                    for j in range(2):
                        pair(n + 2 + 2 * j, 256 * (1 + j) + 512 * it, it)
                return n + 2 * FP

            n = 0
            starts = {first["f1.up"]: ("f1", io["w_gate"][0], io["w_up"][0]),
                      first["f2.up"]: ("f2", io["ffn_w_gate_2"][0], io["ffn_w_up_2"][0]),
                      first["f3.up"]: ("f3", io["ffn_w_gate_2"][1], io["ffn_w_up_2"][1])}
            while n < len(m.units):
                if n in starts:
                    n = ffn(*starts[n])
                else:
                    m.load_unit(sp, n, m.units[n][0])
                    n += 1
            for r in range(RT):
                sp.wait_ge(*m.past("pf1_x_ready", r + 1))
                sp.dma_start(out[0, r * P:(r + 1) * P, :], m.x[:, r, :]).then_inc(sem("stored"), 16)
            sp.wait_ge(*m.past("stored", 16 * RT))

        @block.gpsimd
        def _(pool):
            c = pool_constants(m, pool)
            m.pool_rstd(pool, "n1", 2, D, "n1_squares", 2)
            pool.wait_ge(*m.past("qk_in", 16 * 2))
            for i in (0, 2):
                c(pool.tensor_scalar(m.qkg[:, i, :], m.qkg[:, i, :], HD ** -0.5, None, ALU.mult))
            for i in range(2):
                for r in range(RT):
                    g = m.qkg[:, i, :]
                    c.step(pool.tensor_tensor(m.ropeg[:, i, r, 0, :], m.rope[:, r, 0, :], g, ALU.mult))
                    for h in range(2):
                        a, b = slice(32 * h, 32 * h + 32), slice(32 - 32 * h, 64 - 32 * h)
                        last = pool.tensor_tensor(m.ropeg[:, i, r, 1, a], m.rope[:, r, 1, a], m.qkg[:, i, b],
                                                  ALU.mult)
                        if (i, r, h) == (1, RT - 1, 1):
                            last.then_inc(sem("rope_ready"), 1)
                        else:
                            c.step(last)
            pool_s5_scalars(m, c, pool)
            pool.wait_ge(*m.past("vectors_in", 16))
            pool.wait_ge(*m.past("glu", 3))

            def conv(k0, k1):
                acc = m.cacc[:, 2, :]
                for k in range(k0, k1):
                    w = m.taps[:, 4 * k + 2:4 * k + 3].to_broadcast([P, TOK])
                    src, out = m.hpad[:, 2, k:k + TOK], acc if k == 0 else m.ctmp[:]
                    c(pool.tensor_tensor(out, src, w, ALU.mult))
                    if k == 0:
                        c(pool.tensor_tensor(acc, acc, m.vec[:, DWB + 2:DWB + 3].to_broadcast([P, TOK]), ALU.add))
                    elif k < TAPS - 1:
                        c(pool.tensor_tensor(acc, acc, m.ctmp[:], ALU.add))
                    else:
                        pool.tensor_tensor(acc, acc, m.ctmp[:], ALU.add).then_inc(sem("conv_pool"), 1)

            conv(0, 5)
            m.pool_rstd(pool, "q", 16, HD, "q_head_sums", 1)
            conv(5, 7)
            m.pool_rstd(pool, "k", 16, HD, "k_head_sums", 1)
            conv(7, TAPS)
            pool_s5_growth(m, c, pool)
            m.pool_rstd(pool, "ln", 2, AW, "ln_head_sums", 1)
            pool_s5_inputs(m, c, pool)
            pool_s5_powers(m, c, pool)
            m.pool_rstd(pool, "f1", 2, D, "f1_squares", 2)
            pool.wait_ge(*m.past("c_in", 16))
            m.pool_prep(pool, 0)
            with pool.Fori(0, (FP - 1) // 2) as it:
                for j in range(2):
                    m.pool_prep(pool, 1 + j, it, 2)
            for b in range(FP, NBLK):
                m.pool_prep(pool, b)
            m.pool_rstd(pool, "fp", 2, D, "fp_squares", 2)
            for r in range(RT):
                c.step(pool.memset(m.qa[:, r, :, HD:HD + 1], 1.0))
                c.step(pool.memset(m.ka[:, r, :, HD + 1:HD + 2], 1.0))
            for i, (t, g) in enumerate(((m.ka, 3), (m.qa, 2), (m.ka, 3), (m.qa, 2))):
                m.pool_rstd(pool, f"blk{i}", 16, HD, f"blk{i}_head_sums", 1)
                for r in range(RT):
                    pool.wait_ge(*m.past("head_normed", 2 * i + r + 1))
                    v = t[:, r, 8 * (i // 2):8 * (i // 2) + 8, 0:HD]
                    pool.tensor_tensor(v, v, m.qkg[:, g:g + 1, :].to_broadcast([P, 8, HD]), ALU.mult)\
                        .then_inc(sem("gained"), 1)
            m.pool_rstd(pool, "pm0", 2, D, "pm0_squares", 2)
            m.pool_rstd(pool, "f2", 2, D, "f2_squares", 2)
            pool_s5_phases(m, c, pool)
            m.pool_rstd(pool, "pf0", 2, D, "pf0_squares", 2)
            m.pool_rstd(pool, "s", 2, D, "s_squares", 2)
            for j in range(4):
                pool.wait_ge(*m.past("vs_done", j + 1))
                g = slice(16 * j, 16 * j + 16)
                pool.tensor_tensor(m.V[:, g, :], m.V[:, g, :], m.CT[:, g, :], ALU.mult).then_inc(sem("vc"), 1)
            for j in range(4):
                pool.wait_ge(*m.past("zs_done", j + 1))
                g = slice(16 * j, 16 * j + 16)
                pool.tensor_tensor(m.W[:, g, :], m.W[:, g, :], m.CT[:, g, :], ALU.mult).then_inc(sem("zc"), 1)
            pool.wait_ge(*m.past("u_back", 32))
            pool.wait_ge(*m.past("d_in", 16))
            for r in range(RT):
                pool.tensor_tensor(m.ud[:, r, :], m.ud[:, r, :], m.dsk[:], ALU.mult).then_inc(sem("du"), 1)
            m.pool_rstd(pool, "pm1", 2, D, "pm1_squares", 2)
            m.pool_rstd(pool, "f3", 2, D, "f3_squares", 2)
            m.pool_rstd(pool, "pf1", 2, D, "pf1_squares", 2)

        @block.tensor
        def _(pe):
            idn = m.ident
            pe.wait_ge(*m.past("consts", 1))
            m.pe_turn(pe, "n1", (4, 5, 6, 7))
            for i in range(4):
                m.mm_features(pe, first["u"] + i, i, ready="n1_act_ready" if i == 0 else None)
            for name, banks in (("q", (4, 5)), ("k", (6, 7)), ("v", (0, 1))):
                if name == "v":
                    pe.wait_ge(*m.past("glu", 4))
                for h in range(2):
                    m.mm_half_k(pe, first[name] + h, banks, h)
            m.pe_heads(pe, "a1", m.qn[:].rearrange("p r (h d) -> p r h d", d=HD), (0, H1), "q_ready", 2, (2, 3), 0)
            m.pe_heads(pe, "a1", m.kn[:].rearrange("p r (h d) -> p r h d", d=HD), (0, H1), "k_ready", 2, (2, 3),
                       H1 // 2)
            pe.wait_ge(*m.past("a1_heads_out", H1))
            pe.wait_ge(*m.past("v_out", 2))

            def conv_and_norm(i):
                h, part = divmod(i, 3)
                if h < 4:
                    for k in range(TAPG * h + 3 * part, min(TAPG * h + 3 * part + 3, TAPG * h + TAPG, TAPS)):
                        if k % TAPG == 0:
                            pe.wait_ge(*m.past("dtaps_ready", h + 1))
                        last = pe.matmul(ps[:, 2, 0:TOK], m.dtaps[:, k % (2 * TAPG), :], m.hpad[:, 3, k:k + TOK],
                                         start=(k == 0), stop=(k == TAPS - 1))
                    if part == 2:
                        last.then_inc(sem("conv_tensor"), 1)
                elif (h, part) == (5, 0):
                    pe.wait_ge(*m.past("conv_done", 1))
                    pe.wait_ge(*m.past("conv_pool", 1))
                    for j in range(4):
                        last = pe.matmul(ps[:, 3, 0:TOK], m.ones[:], m.cacc[:, j, :], start=(j == 0), stop=(j == 3))
                    last.then_inc(sem("ln_sum"), 1)
                elif (h, part) == (7, 0):
                    pe.wait_ge(*m.past("ln_sq", 1))
                    for r in range(RT):
                        for j in range(4):
                            last = pe.matmul(ps[:, 3, r:r + 1], m.csq[:, j, r * P:(r + 1) * P], m.ones[:, 0:1],
                                             start=(j == 0), stop=(j == 3))
                    last.then_inc(sem("ln_second"), 1)

            m.pe_attention(pe, "a1", (0, H1), m.qt, m.kt1, m.vn, m.p1, m.pt1, (4, 5), (6, 7),
                           lambda r, h: ps[:, r, h * HD:(h + 1) * HD], conv_and_norm)
            m.pe_turn(pe, "ao", (0, 1, 2), n=4)
            n = first["o1"]
            ao = (("ao_act_ready", 1),)
            m.mm_k_pair(pe, n, 4, m.actH, m.actL, 0, KT, ao)
            pe.wait_ge(*m.past("ln_diag", 2))
            pe.matmul(ps[:, 3, 0:TOK], m.ones[:], m.diag[:], start=True, stop=True).then_inc(sem("ln_spread"), 1)
            m.mm_k_pair(pe, n + 1, 4, m.actH, m.actL, 2, KT, (("ao_act_ready", 3),))
            pe.wait_ge(*m.past("cv_act_ready", 1))
            m.mm_k_pair(pe, n + 2, 4, m.actH, m.actL, 4, KT)
            m.mm_k_pair(pe, n + 3, 4, m.actH, m.actL, 6, KT)
            m.pe_turn(pe, "f1", (0, 1, 2, 3))
            m.pe_ffn(pe, "f1", 4, prep=True)
            m.pe_turn(pe, "fp", (0, 1, 2, 3))
            pe.wait_ge(*m.past("fp_act_ready", KT))
            pe.wait_ge(*m.past("wf_split", 2))
            for r in range(RT):
                for k in range(KT):
                    xh, xl = m.actH[:, k, r * P:(r + 1) * P], m.actL[:, k, r * P:(r + 1) * P]
                    o = ps[:, 0, H2 * r:H2 * r + H2]
                    pe.matmul(o, xh, m.wfH[:, k, :], start=(k == 0), stop=False)
                    pe.matmul(o, xh, m.wfL[:, k, :], start=False, stop=False)
                    last = pe.matmul(o, xl, m.wfH[:, k, :], start=False, stop=(k == KT - 1))
            last.then_inc(sem("f_done"), 1)
            n = first["fox"]
            for i, banks in enumerate(((4, 5), (6, 7), (4, 5))):
                if i == 2:
                    pe.wait_ge(*m.past("fox_out", 2))
                for h in range(2):
                    m.mm_half_k(pe, n + 2 * i + h, banks, h)
                if i == 0:
                    pe.wait_ge(*m.past("logf", 1))
                    lf = m.fl[:, 1]
                    pe.matmul(ps[:, 1, 0:H2], m.tri[:], lf[:, 0, :], start=True, stop=True)
                    pe.matmul(ps[:, 1, H2:2 * H2], m.ones[:], lf[:, 0, :], start=True, stop=False)
                    pe.matmul(ps[:, 1, H2:2 * H2], m.tri[:], lf[:, 1, :], start=False, stop=True)\
                      .then_inc(sem("csum"), 1)
            pe.wait_ge(*m.past("c_cols", 4))
            m.pe_heads(pe, "a2", m.ka, (0, 8), "gained", 2, (2, 3), 0)
            m.pe_heads(pe, "a2", m.qa, (0, 8), "gained", 4, (2, 3), 4)
            pe.wait_ge(*m.past("a2_heads_out", 8))
            pe.wait_ge(*m.past("fox_out", 6))

            def others_a(i):
                if i in (8, 16):
                    pe.wait_ge(*m.past("fox_out", 6 + i // 4))
                m.mm_quarter(pe, n + 6 + i // 4, (6, 7), i // 4 % 2, i % 4)

            m.pe_attention(pe, "a2", (0, 8), m.qt2, m.kt2, m.va, m.p2, m.pt2, (0, 1), (2, 3),
                           lambda r, h: ps[:, 4 + r, h * HD:(h + 1) * HD], others_a)
            pe.wait_ge(*m.past("a2_pt", 8))
            m.pe_heads(pe, "a2", m.ka, (8, 16), "gained", 6, (2, 3), 8)
            m.pe_heads(pe, "a2", m.qa, (8, 16), "gained", 8, (2, 3), 12)
            pe.wait_ge(*m.past("a2_heads_out", 16))
            pe.wait_ge(*m.past("fox_out", 12))

            def others_b(i):
                i -= 24
                if i % 3 == 2:
                    return
                i = i // 3 * 2 + i % 3
                if i == 0:
                    pe.wait_ge(*m.past("half_out", 2))
                if i == 8:
                    pe.wait_ge(*m.past("fox_out", 14))
                m.mm_quarter(pe, n + 12 + i // 4, (4, 5), i // 4 % 2, i % 4)

            m.pe_attention(pe, "a2", (8, 16), m.qt2, m.kt2, m.va, m.p2, m.pt2, (0, 1), (2, 3),
                           lambda r, h: ps[:, 6 + r, (h - 8) * HD:(h - 7) * HD], others_b)
            m.pe_turn(pe, "fo", (0, 1, 2, 3))
            for i in range(4):
                m.mm_k_pair(pe, first["o2"] + i, 4, m.actH, m.actL, 2 * i, KT,
                            (("fo_act_ready", 2 * i + 1),))
            m.pe_turn(pe, "f2", (0, 1, 2, 3))
            m.pe_ffn(pe, "f2", 4)
            m.pe_turn(pe, "s", (4, 5, 6, 7))
            for b in range(2):
                for h in range(2):
                    m.mm_half_k(pe, first["s"] + 2 * b + h, (2 * b, 2 * b + 1), h,
                                "s_act_ready" if b == 0 else None)
            pe.wait_ge(*m.past("ur_a", 1))
            pe.wait_ge(*m.past("ur_d", 1))
            for q in range(16):
                last = pe.transpose(ps[:, 4 + q // 4, (q % 4) * P:(q % 4 + 1) * P],
                                    m.Ur[:, q, :, :].rearrange("p t c -> p (t c)"), idn[:])
                if q % 4 == 3:
                    last.then_inc(sem("u_turned"), 1)
            pe.wait_ge(*m.past("u_out_a", 2))
            pe.wait_ge(*m.past("u_out_d", 2))
            pe.wait_ge(*m.past("r_in", 16))
            for j in range(4):
                for q in range(16):
                    last = pe.matmul(ps[:, j, q * NCH:(q + 1) * NCH], m.RTab[:, 16 * j + q, :], m.Uall[:, q, j, :],
                                     start=True, stop=True)
                last.then_inc(sem("v_done"), 1)

            def swap(j, src, bank, ready, value, done):
                pe.wait_ge(*m.past(ready, value))
                pe.matmul(ps[:, bank, :], m.swap[:],
                          src[:, 16 * j:16 * j + 16, :].rearrange("p g c -> p (g c)"), start=True, stop=True)\
                  .then_inc(sem(done), 1)

            for j in range(4):
                swap(j, m.V, 4 + j, "vo_a" if j < 2 else "vo_d", j % 2 + 1, "vs_done")
            for j in range(4):
                swap(j, m.W, j, "scanned", j + 1, "zs_done")
            pe.wait_ge(*m.past("t_in", 16 * T))
            pe.wait_ge(*m.past("o_in", 16))
            pe.wait_ge(*m.past("states", 4))
            for q in range(16):
                for j in range(4):
                    o = ps[32 * j:32 * j + 32, 4 + q // 4, (q % 4) * P:(q % 4 + 1) * P]
                    pe.matmul(o, m.Uall[:, q, j, :], m.TTab[:, 16 * j + q, :], start=True, stop=False)
                    last = pe.matmul(o, m.X33[:, 16 * j + q, 0:NCH], m.OTab[:, 16 * j + q, :], start=False, stop=True)
                if q % 4 == 3:
                    last.then_inc(sem("y_done"), 1)
            m.pe_turn(pe, "yg", (0, 1, 2, 3))
            for i in range(4):
                m.mm_k_pair(pe, first["glu"] + i, 4, m.actH, m.actL, 2 * i, KT, (("yg_act_ready", 2 * i + 1),))
            m.pe_turn(pe, "yo", (0, 1, 2, 3))
            for i in range(4):
                m.mm_k_pair(pe, first["o3"] + i, 4, m.actH, m.actL, 2 * i, KT, (("yo_act_ready", 2 * i + 1),))
            m.pe_turn(pe, "f3", (0, 1, 2, 3))
            m.pe_ffn(pe, "f3", 4)

        @block.scalar
        def _(act):
            s5 = {k: v[:] for k, v in m.small.items()}
            for t, name in ((m.vectors, "vectors"), (m.lamdt, "lamdt")):
                act.dma_start(t[:], io[name]).then_inc(sem(name + "_in"), 16)
            for r in range(RT):
                act.wait_ge(*m.past(f"x_in{r}", 16))
                act.activation(m.nat[:, r, :], m.x[:, r, :], ACT.Square, accum_out=m.ss[:, r:r + 1])\
                   .then_inc(sem("n1_squares"), 1)
            m.split_high(act, 0)
            act.wait_ge(*m.past("vectors_in", 16))
            m.act_turn(act, "n1", (4, 5, 6, 7), gain=N1)
            m.split_high(act, 1)
            act.dma_start(m.qkg[:].rearrange("p a d -> p (a d)"), io["head_gains"].to_broadcast([P, 4 * HD]))\
               .then_inc(sem("qk_in"), 16)
            act.dma_start(m.rope[:], io["rope"]).then_inc(sem("qk_in"), 16)
            act.dma_start(m.Bri[:], io["s5_b"]).then_inc(sem("b_in"), 16)
            act.dma_start(m.C12[:], io["s5_c"]).then_inc(sem("c_in"), 16)
            act.wait_ge(*m.past("lamdt_in", 16))
            act.activation(s5["dt"], s5["ldt"], ACT.Exp).then_inc(sem("dt"), 1)
            m.split_high(act, 2)
            m.split_high(act, 3)
            m.split_high(act, 4)
            for j in range(4):
                act.wait_ge(m.used, first["u"] + 3 + j // 2)
                act.activation(m.csig[:, j, :], ps[:, 2 + j // 2, (j % 2) * TOK:(j % 2 + 1) * TOK], ACT.Sigmoid,
                               bias=m.vec[:, GLUB + 4 + j:GLUB + 5 + j]).then_inc(sem("sig"), 1)
            m.split_high(act, 5)
            m.split_high(act, 6)
            m.split_high(act, 7)

            def head_squares(st, banks, unit, sq):
                act.wait_ge(m.used, unit)
                for r in range(RT):
                    act.activation(sq[:, r, :], ps[:, banks[r], :], ACT.Square).then_inc(sem(st + "_sq"), 1)

            act.wait_ge(*m.past("glu", 4))
            head_squares("q", (4, 5), first["q"] + 2, m.sq1)
            f5 = sem("s5_functions")
            act.wait_ge(*m.past("angle", 1))
            act.activation(m.sinT[:], s5["thr"], ACT.Sin).then_inc(f5, 1)
            act.activation(s5["sh"], s5["thr"], ACT.Sin, scale=0.5).then_inc(f5, 1)
            act.wait_ge(*m.past("abs_angle", 1))
            act.activation(m.cosT[:], s5["ab"], ACT.Sin, scale=-1.0, bias=m.halfpi[:]).then_inc(f5, 1)
            act.activation(s5["tt"], s5["lrc"], ACT.Tanh, scale=0.5).then_inc(f5, 1)
            act.activation(s5["eb"], s5["lrb"], ACT.Exp).then_inc(f5, 1)
            m.split_high(act, 8)

            def tap_diagonals(g):
                ks = range(TAPG * g, min(TAPG * g + TAPG, TAPS))
                for k in ks:
                    i = act.activation(m.dtaps[:, k % (2 * TAPG), :], m.ident[:], ACT.Copy,
                                       scale=m.taps[:, 4 * k + 3:4 * k + 4])
                i.then_inc(sem("dtaps_ready"), 1)

            act.wait_ge(*m.past("n1_transposed", KT))
            tap_diagonals(0)
            m.split_high(act, 9)
            act.wait_ge(*m.past("q_head_sums", 1))
            head_squares("k", (6, 7), first["k"] + 2, m.sq1)
            m.split_high(act, 10)
            m.split_high(act, 11)
            for r in range(RT):
                act.wait_ge(m.used, first["v"] + 2)
                act.activation(m.vn[:, r, :], ps[:, r, :], ACT.Copy).then_inc(sem("v_out"), 1)
            m.act_heads(act, "a1", m.qt, (0, H1), (2, 3), 0)
            m.act_heads(act, "a1", m.kt1, (0, H1), (2, 3), H1 // 2)
            tap_diagonals(1)
            for h in range(H1):
                m.act_attention(act, "a1", h, m.p1, rsum, nmax, (4, 5))
                if h < 2:
                    act.wait_ge(*m.past("conv_tensor", h + 1))
                    tap_diagonals(2 + h)
                if h == 5:
                    act.wait_ge(*m.past("ln_centred", 1))
                    act.activation(m.csq[:], m.cacc[:], ACT.Square).then_inc(sem("ln_sq"), 1)
            m.act_turn(act, "ao", (0, 1, 2), n=4)
            m.split_high(act, 12)
            act.wait_ge(*m.past("ln_second", 1))
            act.wait_ge(*m.past("ln_normed", 1))
            for j in range(4):
                act.activation(m.csq[:, j, :], m.cacc[:, j, :], ACT.Silu, scale=m.vec[:, LNG + j:LNG + j + 1],
                               bias=m.vec[:, LNB + j:LNB + j + 1]).then_inc(sem("cv_silu"), 1)
            act.wait_ge(*m.past("cv_silu", 4))
            act.activation(m.actH[:, 4:8, :], m.csq[:], ACT.Copy).then_inc(sem("cv_high"), 1)
            m.split_high(act, 13)
            m.split_high(act, 14)
            m.act_squares(act, "f1", lambda r: m.x[:, r, :], "f1_x_ready", (1, 2))
            m.act_turn(act, "f1", (0, 1, 2, 3), gain=N2)
            m.split_high(act, 15)
            m.act_ffn(act, "f1", 4, prep=True)
            for i in range(2):
                act.wait_ge(*m.past(f"prep_stored{i}", 48 * (NBLK // 2) + 1))
            act.dma_start(m.wf[:], io["fox_w_in_2"][0][:, 4 * D:4 * D + H2].rearrange("(k p) c -> p k c", p=P))\
               .then_inc(sem("wf_in"), 16)
            act.dma_start(m.fb[:], io["fox_b_f_2"].to_broadcast([P, H2])).then_inc(sem("fb_in"), 16)
            act.dma_start(m.gb[0][:], io["mix_post_gain_2"][0:1, :].to_broadcast([P, D])).then_inc(sem("gain0_in"), 16)
            act.dma_start(m.gb[1][:], io["ffn_post_gain_2"][0:1, :].to_broadcast([P, D])).then_inc(sem("gain1_in"), 16)
            m.act_squares(act, "fp", lambda r: m.x[:, r, :], "fp_x_ready", (1, 2))
            act.wait_ge(*m.past("wf_in", 16))
            act.activation(m.wfH[:], m.wf[:], ACT.Copy).then_inc(sem("wf_high"), 1)
            m.act_turn(act, "fp", (0, 1, 2, 3), gain=MIXPRE)
            m.split_high(act, first["fox"] + 1)
            act.wait_ge(*m.past("f_abs", 1))
            act.activation(m.fl[:, 2], m.fl[:, 1], ACT.Exp, scale=-1.0).then_inc(sem("f_exp"), 1)
            act.wait_ge(*m.past("f_exp", 1))
            act.activation(m.fl[:, 3], m.fl[:, 2], ACT.Ln, bias=1.0).then_inc(sem("f_ln"), 1)
            n = first["fox"]

            def block_out(i, banks):
                act.wait_ge(m.used, n + 2 * i + 2)
                half = i // 3 if i < 6 else i - 6
                for r in range(RT):
                    b = ps[:, banks[r], :]
                    if i < 6 and i % 3 < 2:
                        t = (m.ka, m.qa)[i % 3]
                        act.activation(t[:, r, 8 * half:8 * half + 8, 0:HD], b.rearrange("p (h d) -> p h d", d=HD),
                                       ACT.Copy).then_inc(sem("fox_out"), 1)
                    else:
                        f, dst = (ACT.Copy, m.va) if i < 6 else (ACT.Sigmoid, m.ga)
                        act.activation(dst[:, r, 512 * half:512 * half + 512], b, f).then_inc(sem("fox_out"), 1)
                if i < 6 and i % 3 < 2:
                    blk = i if i < 2 else i - 1
                    if blk > 0:
                        act.wait_ge(*m.past(f"blk{blk - 1}_head_sums", 1))
                    for r in range(RT):
                        act.wait_ge(*m.past("fox_out", 2 * i + r + 1))
                        act.activation(m.sq2[:, r, :].rearrange("p (h d) -> p h d", d=HD),
                                       t[:, r, 8 * half:8 * half + 8, 0:HD], ACT.Square)\
                           .then_inc(sem(f"blk{blk}_sq"), 1)

            for i in range(3):
                for h in range(2):
                    m.split_high(act, n + 2 * i + 2 + h)
                block_out(i, (6, 7) if i == 1 else (4, 5))
            m.act_heads(act, "a2", m.kt2, (0, 8), (2, 3), 0)
            m.act_heads(act, "a2", m.qt2, (0, 8), (2, 3), 4)
            for h in range(16):
                m.act_attention(act, "a2", h, m.p2, rsum, nmax, (0, 1))
                for j in units_done(h):
                    if j % 2 == 1:
                        block_out(j // 2, (6, 7) if h < 8 else (4, 5))
                    m.split_high(act, n + j + 2)
                if h == 7:
                    m.act_heads(act, "a2", m.kt2, (8, 16), (2, 3), 8)
                    m.act_heads(act, "a2", m.qt2, (8, 16), (2, 3), 12)
            m.act_turn(act, "fo", (0, 1, 2, 3))
            n = first["o2"]
            for i in range(3):
                m.split_high(act, n + 2 + i)
            act.wait_ge(m.used, n + 4)
            m.act_squares(act, "pm0", lambda r: m.acc_row(4, r))
            m.act_squares(act, "f2", lambda r: m.x[:, r, :], "pm0_x_ready", (1, 2))
            act.dma_start(m.gb[0][:], io["mix_post_gain_2"][1:2, :].to_broadcast([P, D])).then_inc(sem("gain0_in"), 16)
            m.act_turn(act, "f2", (0, 1, 2, 3), gain=FFNPRE)
            m.split_high(act, n + 5)
            m.act_ffn(act, "f2", 4)
            n = first["s"]
            act.wait_ge(m.used, n)
            m.act_squares(act, "pf0", lambda r: m.acc_row(0, r))
            act.dma_start(m.RTab[:], m.Rd).then_inc(sem("r_in"), 16)
            act.dma_start(m.OTab[:], m.Od).then_inc(sem("o_in"), 16)
            m.act_squares(act, "s", lambda r: m.x[:, r, :], "pf0_x_ready", (1, 2))
            act.dma_start(m.dsk[:], io["s5_d_2"].to_broadcast([P, D])).then_inc(sem("d_in"), 16)
            m.act_turn(act, "s", (4, 5, 6, 7), gain=MIXPRE + 8)
            m.split_high(act, n + 1)
            m.split_high(act, n + 2)
            m.split_high(act, n + 3)
            act.wait_ge(m.used, n + 2)
            act.activation(m.nat[:, 0, 0:512], ps[:, 0, :], ACT.Copy).then_inc(sem("u_nat_a"), 1)
            m.split_high(act, n + 4)
            act.wait_ge(m.used, n + 4)
            act.activation(m.nat[:, 0, 512:D], ps[:, 2, :], ACT.Copy).then_inc(sem("u_nat_a"), 1)
            act.wait_ge(*m.past("u_nat_a", 2))
            act.dma_start(m.ud_d[0:P, :], m.nat[:, 0, :]).then_inc(sem("u_stored"), 16)
            act.wait_ge(*m.past("u_nat_d", 2))
            act.dma_start(m.ud_d[P:2 * P, :], m.nat[:, 1, :]).then_inc(sem("u_stored"), 16)
            m.split_high(act, n + 5)
            act.wait_ge(*m.past("u_stored", 32))

            def chunked(dram, j):
                return dram.rearrange("(c t) f -> c t f", t=T)[:, :, 256 * j:256 * j + 256]

            for j in range(4):
                act.dma_start(m.Un[32 * j:32 * j + 32].rearrange("p t q c -> p t (q c)"), chunked(m.ud_d, j))\
                   .then_inc(sem("un_in"), 16)
            act.wait_ge(*m.past("un_in", 64))
            act.activation(m.Ur[:, 0:8, :, :], m.Un[:, :, 0:8, :].rearrange("p t q c -> p q t c"), ACT.Copy)\
               .then_inc(sem("ur_a"), 1)
            for b in range(2):
                act.wait_ge(*m.past("u_turned", b + 1))
                act.activation(m.Uall[:, 4 * b:4 * b + 4, :, :],
                               ps[:, 4 + b, :].rearrange("p (q j c) -> p q j c", q=4, j=4), ACT.Copy)\
                   .then_inc(sem("u_out_a"), 1)
            for j in range(2):
                act.wait_ge(*m.past("v_done", j + 1))
                act.activation(m.V[:, 16 * j:16 * j + 16, :], ps[:, j, :].rearrange("p (g c) -> p g c", c=NCH), ACT.Copy)\
                   .then_inc(sem("vo_a"), 1)
            act.wait_ge(*m.past("v_done", 4))
            for s in range(T):
                act.dma_start(m.TTab[SC * s:SC * s + SC, :, :], m.Kd[:, :, P - SC * s:2 * P - SC * s])\
                   .then_inc(sem("t_in"), 16)
            act.wait_ge(*m.past("states", 4))
            for r in range(RT):
                act.dma_start(m.ud[:, r, :], m.ud_d[r * P:(r + 1) * P, :]).then_inc(sem("u_back"), 16)
            for b in range(2):
                act.wait_ge(*m.past("y_done", b + 1))
                act.activation(m.Ysb[:, :, 4 * b:4 * b + 4, :].rearrange("p t q c -> p q t c"),
                               ps[:, 4 + b, :].rearrange("p (q t c) -> p q t c", q=4, t=T), ACT.Copy)\
                   .then_inc(sem("y_out_a"), 1)
            act.wait_ge(*m.past("y_out_a", 2))
            act.wait_ge(*m.past("y_out_d", 2))
            for j in range(4):
                act.dma_start(chunked(m.yd_d, j), m.Ysb[32 * j:32 * j + 32].rearrange("p t q c -> p t (q c)"))\
                   .then_inc(sem("y_stored"), 16)
            act.wait_ge(*m.past("y_stored", 64))
            for r in range(RT):
                act.dma_start(m.nat[:, r, :], m.yd_d[r * P:(r + 1) * P, :]).then_inc(sem(f"y_in{r}"), 16)
            act.wait_ge(*m.past("du", 2))
            act.dma_start(m.gb[1][:], io["ffn_post_gain_2"][1:2, :].to_broadcast([P, D])).then_inc(sem("gain1_in"), 16)
            for r in range(RT):
                act.wait_ge(*m.past("y_sum", r + 1))
                act.activation(m.nat[:, r, :], m.nat[:, r, :], ACT.Gelu_apprx_tanh).then_inc(sem("yg_nat_ready"), 1)
            m.act_turn(act, "yg", (0, 1, 2, 3))
            n = first["glu"]
            for i in range(3):
                m.split_high(act, n + 2 + i)
            act.wait_ge(m.used, n + 4)
            for r in range(RT):
                act.activation(m.sgl[:, r, :].rearrange("p (a b) -> p a b", a=2), m.acc_row(4, r), ACT.Sigmoid)\
                   .then_inc(sem("glu_sig"), 1)
            m.act_turn(act, "yo", (0, 1, 2, 3))
            n = first["o3"]
            for i in range(4):
                m.split_high(act, n + 1 + i)
            act.wait_ge(m.used, n + 4)
            m.act_squares(act, "pm1", lambda r: m.acc_row(4, r))
            m.act_squares(act, "f3", lambda r: m.x[:, r, :], "pm1_x_ready", (1, 2))
            m.act_turn(act, "f3", (0, 1, 2, 3), gain=FFNPRE + 8)
            m.split_high(act, n + 5)
            m.act_ffn(act, "f3", 4)
            act.wait_ge(m.used, len(m.units))
            m.act_squares(act, "pf1", lambda r: m.acc_row(0, r))

        @block.vector
        def _(dve):
            c = Chain(dve, sem("dve_chain"))
            s5 = {k: v[:] for k, v in m.small.items()}
            m.dve_scale(dve, "n1")
            m.split_low(dve, 0)
            dve.wait_ge(*m.past("vectors_in", 16))
            m.dve_turn(dve, "n1", (4, 5, 6, 7), gain=N1)
            for i in range(1, 5):
                m.split_low(dve, i)
            for j in range(4):
                dve.wait_ge(*m.past("sig", j + 1))
                dve.scalar_tensor_tensor(m.hpad[:, j, TAPS - 1:], ps[:, j // 2, (j % 2) * TOK:(j % 2 + 1) * TOK],
                                         m.vec[:, GLUB + j:GLUB + j + 1], m.csig[:, j, :], ALU.add, ALU.mult)\
                   .then_inc(sem("glu"), 1)
            m.split_low(dve, 5)
            dve.wait_ge(*m.past("angle", 1))
            dve.scalar_tensor_tensor(s5["ab"], s5["thr"], -1.0, s5["thr"], ALU.mult, ALU.max)\
               .then_inc(sem("abs_angle"), 1)
            taps_left = [(k, j) for k in range(TAPS) for j in range(2)]
            steps = {}

            def conv(count):
                for _ in range(min(count, len(taps_left))):
                    k, j = taps_left.pop(0)
                    w = m.taps[:, 4 * k + j:4 * k + j + 1]
                    src = m.hpad[:, j, k:k + TOK]
                    if k == 0:
                        if j == 0:
                            dve.wait_ge(*m.past("glu", 4))
                        i = dve.tensor_scalar(m.cacc[:, j, :], src, w, m.vec[:, DWB + j:DWB + j + 1], ALU.mult, ALU.add)
                    else:
                        c.wait(steps[j])
                        i = dve.scalar_tensor_tensor(m.cacc[:, j, :], src, w, m.cacc[:, j, :], ALU.mult, ALU.add)
                    steps[j] = c.step(i)

            def head_norms(st, banks, t, ki, unit):
                dve.wait_ge(*m.past(st + "_sq", 2))
                dve.reduce_sum(m.ss[:], m.sq1[:].rearrange("p r (h d) -> p (r h) d", d=HD), AX.X)\
                   .then_inc(sem(st + "_head_sums"), 1)
                conv(4)
                if st == "q":
                    m.split_low(dve, unit)
                dve.wait_ge(*m.past(st + "_rstd", 1))
                dve.wait_ge(*m.past("rope_ready", 1))
                hd = lambda a: a.rearrange("p (h d) -> p h d", d=HD)
                for r in range(RT):
                    rs = m.rs[:, 8 * r:8 * r + 8].unsqueeze(2).to_broadcast([P, 8, HD])
                    c(dve.tensor_tensor(hd(m.rtmp[:]), hd(ps[:, banks[r], :]), rs, ALU.mult))
                    tb = [m.ropeg[:, ki, r, i:i + 1, :].to_broadcast([P, 8, HD]) for i in range(2)]
                    c.step(dve.tensor_tensor(hd(t[:, r, :]), hd(m.rtmp[:]), tb[0], ALU.mult))
                    halves = m.rtmp[:].rearrange("p (h a d) -> p h a d", a=2, d=32)
                    for a in range(2):
                        s_ = m.ropeg[:, ki, r, 1:2, 32 * a:32 * a + 32].to_broadcast([P, 8, 32])
                        c.step(dve.tensor_tensor(hd(m.rtmp2[:])[:, :, 32 * a:32 * a + 32], halves[:, :, 1 - a, :], s_,
                                                 ALU.mult))
                    c.wait()
                    dve.tensor_tensor(t[:, r, :], t[:, r, :], m.rtmp2[:], ALU.add).then_inc(sem(st + "_ready"), 1)
                    if st == "k" or r == 0:
                        m.split_low(dve, unit + (r if st == "k" else 1))
                    dve.wait_ge(*m.past(st + "_ready", r + 1))

            conv(6)
            m.split_low(dve, 6)
            conv(4)
            m.split_low(dve, 7)
            head_norms("q", (4, 5), m.qn, 0, 8)
            dve.wait_ge(*m.past("s5_functions", 4))
            c(dve.tensor_scalar(s5["r2"], s5["tt"], -1.0, 1.0, ALU.mult, ALU.add))
            dve.reciprocal(s5["r1"], s5["r2"]).then_inc(sem("s5_recips"), 1)
            dve.wait_ge(*m.past("den", 1))
            dve.reciprocal(s5["rden"], s5["den"]).then_inc(sem("s5_recips"), 1)
            conv(4)
            head_norms("k", (6, 7), m.kn, 1, 10)

            def conv_and_norm(h):
                if h < 5:
                    conv(12)
                if h == 4:
                    dve.wait_ge(*m.past("conv_tensor", 4))
                    c.wait()
                    dve.tensor_scalar(m.cacc[:, 3, :], ps[:, 2, 0:TOK], m.vec[:, DWB + 3:DWB + 4], None, ALU.add)\
                       .then_inc(sem("conv_done"), 1)
                if h == 5:
                    dve.wait_ge(*m.past("ln_sum", 1))
                    dve.scalar_tensor_tensor(m.cacc[:], ps[:, 3:4, 0:TOK].to_broadcast([P, 4, TOK]), -1.0 / AW,
                                             m.cacc[:], ALU.mult, ALU.add).then_inc(sem("ln_centred"), 1)
                if h == 7:
                    dve.wait_ge(*m.past("ln_second", 1))
                    dve.tensor_copy(m.ss[:, 0:2], ps[:, 3, 0:2]).then_inc(sem("ln_head_sums"), 1)

            m.dve_attention(dve, "a1", (0, H1), m.pt1, nmax, (4, 5), (6, 7), conv_and_norm)
            dve.wait_ge(*m.past("a1_out", H1))
            c(dve.reciprocal(rinv[:, :, 0:H1], rsum[:, :, 0:H1]))
            for r in range(RT):
                dve.tensor_tensor(m.nat[:, r, 0:AW].rearrange("p (h d) -> p h d", d=HD),
                                  ps[:, r, :].rearrange("p (h d) -> p h d", d=HD),
                                  rinv[:, r, 0:H1].unsqueeze(2).to_broadcast([P, H1, HD]), ALU.mult)\
                   .then_inc(sem("ao_nat_ready"), 1)
            m.dve_turn(dve, "ao", (0, 1, 2), n=4)
            dve.wait_ge(*m.past("ln_rstd", 1))
            for r in range(RT):
                dve.tensor_scalar(m.diag[:, r * P:(r + 1) * P], m.ident[:], m.rs[:, r:r + 1], None, ALU.mult)\
                   .then_inc(sem("ln_diag"), 1)
            m.split_low(dve, 12)
            dve.wait_ge(*m.past("ln_spread", 1))
            dve.tensor_tensor(m.cacc[:], m.cacc[:], ps[:, 3:4, 0:TOK].to_broadcast([P, 4, TOK]), ALU.mult)\
               .then_inc(sem("ln_normed"), 1)
            dve.wait_ge(*m.past("cv_high", 1))
            dve.tensor_tensor(m.actL[:, 4:8, :], m.csq[:], m.actH[:, 4:8, :].bitcast(F32), ALU.subtract)\
               .then_inc(sem("cv_act_ready"), 1)
            m.split_low(dve, 13)
            m.split_low(dve, 14)

            def residual(st, base):
                for r in range(RT):
                    xr = m.x[:, r, :].rearrange("p (a b) -> p a b", a=2)
                    dve.tensor_tensor(xr, xr, m.acc_row(base, r), ALU.add).then_inc(sem(st + "_x_ready"), 1)

            dve.wait_ge(m.used, first["o1"] + 4)
            residual("f1", 4)
            m.dve_scale(dve, "f1")
            m.dve_turn(dve, "f1", (0, 1, 2, 3), gain=N2)
            m.split_low(dve, 15)
            m.dve_ffn(dve, "f1", 4)
            n = first["fox"]
            dve.wait_ge(m.used, n)
            residual("fp", 0)
            dve.wait_ge(*m.past("wf_high", 1))
            dve.tensor_tensor(m.wfL[:], m.wf[:], m.wfH[:].bitcast(F32), ALU.subtract).then_inc(sem("wf_split"), 2)
            m.dve_scale(dve, "fp")
            m.dve_turn(dve, "fp", (0, 1, 2, 3), gain=MIXPRE)
            m.split_low(dve, n + 1)
            dve.wait_ge(*m.past("f_done", 1))
            dve.wait_ge(*m.past("fb_in", 16))
            c(dve.tensor_tensor(m.fl[:, 0], ps[:, 0, 0:2 * H2].rearrange("p (r h) -> p r h", r=2),
                                m.fb[:].unsqueeze(1).to_broadcast([P, RT, H2]), ALU.add))
            dve.scalar_tensor_tensor(m.fl[:, 1], m.fl[:, 0], -1.0, m.fl[:, 0], ALU.mult, ALU.max)\
               .then_inc(sem("f_abs"), 1)
            dve.wait_ge(*m.past("f_ln", 1))
            dve.scalar_tensor_tensor(m.fl[:, 1], m.fl[:, 0], 0.0, m.fl[:, 3], ALU.min, ALU.subtract)\
               .then_inc(sem("logf"), 1)

            def head_sums(blk):
                st = f"blk{blk}"
                dve.wait_ge(*m.past(st + "_sq", 2))
                dve.reduce_sum(m.ss[:], m.sq2[:].rearrange("p r (h d) -> p (r h) d", d=HD), AX.X)\
                   .then_inc(sem(st + "_head_sums"), 1)

            def head_norm(blk):
                dve.wait_ge(*m.past(f"blk{blk}_rstd", 1))
                t, h0 = (m.ka, m.qa)[blk % 2], 8 * (blk // 2)
                for r in range(RT):
                    v = t[:, r, h0:h0 + 8, 0:HD]
                    dve.tensor_tensor(v, v, m.rs[:, 8 * r:8 * r + 8].unsqueeze(2).to_broadcast([P, 8, HD]),
                                      ALU.mult).then_inc(sem("head_normed"), 1)

            for i in range(3):
                for h in range(2):
                    m.split_low(dve, n + 2 * i + 2 + h)
                if i == 0:
                    dve.wait_ge(*m.past("csum", 1))
                    for r in range(RT):
                        cs = ps[:, 1, H2 * r:H2 * r + H2].unsqueeze(2)
                        dve.tensor_copy(m.qa[:, r, :, HD + 1:HD + 2], cs).then_inc(sem("c_cols"), 1)
                        dve.tensor_scalar(m.ka[:, r, :, HD:HD + 1], cs, -1.0, None, ALU.mult).then_inc(sem("c_cols"), 1)
                if i < 2:
                    head_sums(i)
                    head_norm(i)

            def others(h):
                if h == 3:
                    head_sums(2)
                if h == 4:
                    head_norm(2)
                if h == 6:
                    head_sums(3)
                if h == 7:
                    head_norm(3)
                if h == 14:
                    dve.wait_ge(*m.past("fox_out", 14))
                    for r in range(RT):
                        t = m.nat[:, r, 0:512]
                        dve.tensor_tensor(t, t, m.ga[:, r, 0:512], ALU.mult).then_inc(sem("fo_gated"), 1)
                if h not in (8, 16) or (h == 8 and second):
                    for j in units_done(h):
                        m.split_low(dve, n + j + 2)

            def half_out(half, banks, done):
                h0 = 8 * half
                dve.wait_ge(*m.past("a2_out", h0 + 8))
                c(dve.reciprocal(rinv[:, :, h0:h0 + 8], rsum[:, :, h0:h0 + 8]))
                for r in range(RT):
                    dve.tensor_tensor(m.nat[:, r, 64 * h0:64 * h0 + 512].rearrange("p (h d) -> p h d", d=HD),
                                      ps[:, banks[r], :].rearrange("p (h d) -> p h d", d=HD),
                                      rinv[:, r, h0:h0 + 8].unsqueeze(2).to_broadcast([P, 8, HD]), ALU.mult)\
                       .then_inc(sem(done), 1)

            second = False
            m.dve_attention(dve, "a2", (0, 8), m.pt2, nmax, (0, 1), (2, 3), others)
            half_out(0, (4, 5), "half_out")
            second = True
            m.dve_attention(dve, "a2", (8, 16), m.pt2, nmax, (0, 1), (2, 3), others)
            half_out(1, (6, 7), "half_out")
            dve.wait_ge(*m.past("fox_out", 16))
            for r in range(RT):
                dve.wait_ge(*m.past("half_out", 3 + r))
                dve.wait_ge(*m.past("fo_gated", r + 1))
                t = m.nat[:, r, 512:D]
                dve.tensor_tensor(t, t, m.ga[:, r, 512:D], ALU.mult).then_inc(sem("fo_nat_ready"), 1)
            m.dve_turn(dve, "fo", (0, 1, 2, 3))
            n = first["o2"]
            for i in range(3):
                m.split_low(dve, n + 2 + i)
            m.dve_postnorm(dve, "pm0", 4, m.gb[0], "gain0_in", 16)
            m.dve_scale(dve, "f2")
            m.dve_turn(dve, "f2", (0, 1, 2, 3), gain=FFNPRE)
            m.split_low(dve, n + 5)
            m.dve_ffn(dve, "f2", 4)
            m.dve_postnorm(dve, "pf0", 0, m.gb[1], "gain1_in", 16)
            n = first["s"]
            m.dve_scale(dve, "s")
            m.dve_turn(dve, "s", (4, 5, 6, 7), gain=MIXPRE + 8)
            for i in range(1, 4):
                m.split_low(dve, n + i)
            dve.wait_ge(m.used, n + 2)
            dve.tensor_copy(m.nat[:, 1, 0:512], ps[:, 1, :]).then_inc(sem("u_nat_d"), 1)
            m.split_low(dve, n + 4)
            dve.wait_ge(m.used, n + 4)
            dve.tensor_copy(m.nat[:, 1, 512:D], ps[:, 3, :]).then_inc(sem("u_nat_d"), 1)
            m.split_low(dve, n + 5)
            dve.wait_ge(*m.past("un_in", 64))
            dve.tensor_copy(m.Ur[:, 8:16, :, :], m.Un[:, :, 8:16, :].rearrange("p t q c -> p q t c"))\
               .then_inc(sem("ur_d"), 1)
            for b in range(2, 4):
                dve.wait_ge(*m.past("u_turned", b + 1))
                dve.tensor_copy(m.Uall[:, 4 * b:4 * b + 4, :, :],
                                ps[:, 4 + b, :].rearrange("p (q j c) -> p q j c", q=4, j=4)).then_inc(sem("u_out_d"), 1)
            flat = lambda a: a.rearrange("p g c -> p (g c)")
            grp = [slice(16 * j, 16 * j + 16) for j in range(4)]
            for j in range(2, 4):
                dve.wait_ge(*m.past("v_done", j + 1))
                dve.tensor_copy(m.V[:, grp[j], :], ps[:, j, :].rearrange("p (g c) -> p g c", c=NCH))\
                   .then_inc(sem("vo_d"), 1)
            dve.wait_ge(*m.past("phases", 1))
            for j in range(4):
                dve.wait_ge(*m.past("vs_done", j + 1))
                k = c.step(dve.tensor_tensor(flat(m.W[:, grp[j], :]), ps[:, 4 + j, :], flat(m.ST[:, grp[j], :]), ALU.mult))
                dve.wait_ge(*m.past("vc", j + 1))
                c.wait(k)
                c(dve.tensor_tensor(m.V[:, grp[j], :], m.V[:, grp[j], :], m.W[:, grp[j], :], ALU.add))
                dve.tensor_tensor_scan(flat(m.W[:, grp[j], :]), flat(m.D0[:, grp[j], :]), flat(m.V[:, grp[j], :]), 0.0,
                                       ALU.mult, ALU.add).then_inc(sem("scanned"), 1)
            dve.wait_ge(*m.past("scanned", 4))
            c.step(dve.memset(m.X33[:, :, 0:1], 0.0))
            for j in range(4):
                dve.wait_ge(*m.past("zs_done", j + 1))
                c(dve.tensor_tensor(flat(m.V[:, grp[j], :]), ps[:, j, :], flat(m.ST[:, grp[j], :]), ALU.mult))
                dve.wait_ge(*m.past("zc", j + 1))
                dve.tensor_tensor(m.X33[:, grp[j], 1:NCH + 1], m.W[:, grp[j], :], m.V[:, grp[j], :], ALU.subtract)\
                   .then_inc(sem("states"), 1)
            for b in range(2, 4):
                dve.wait_ge(*m.past("y_done", b + 1))
                dve.tensor_copy(m.Ysb[:, :, 4 * b:4 * b + 4, :].rearrange("p t q c -> p q t c"),
                                ps[:, 4 + b, :].rearrange("p (q t c) -> p q t c", q=4, t=T)).then_inc(sem("y_out_d"), 1)
            for r in range(RT):
                dve.wait_ge(*m.past(f"y_in{r}", 16))
                dve.wait_ge(*m.past("du", r + 1))
                dve.tensor_tensor(m.nat[:, r, :], m.nat[:, r, :], m.ud[:, r, :], ALU.add).then_inc(sem("y_sum"), 1)
            m.dve_turn(dve, "yg", (0, 1, 2, 3))
            n = first["glu"]
            for i in range(3):
                m.split_low(dve, n + 2 + i)
            for r in range(RT):
                dve.wait_ge(*m.past("glu_sig", r + 1))
                dve.tensor_tensor(m.nat[:, r, :], m.nat[:, r, :], m.sgl[:, r, :], ALU.mult)\
                   .then_inc(sem("yo_nat_ready"), 1)
            m.dve_turn(dve, "yo", (0, 1, 2, 3))
            n = first["o3"]
            for i in range(4):
                m.split_low(dve, n + 1 + i)
            m.dve_postnorm(dve, "pm1", 4, m.gb[0], "gain0_in", 32)
            m.dve_scale(dve, "f3")
            m.dve_turn(dve, "f3", (0, 1, 2, 3), gain=FFNPRE + 8)
            m.split_low(dve, n + 5)
            m.dve_ffn(dve, "f3", 4)
            m.dve_postnorm(dve, "pf1", 0, m.gb[1], "gain1_in", 32)


BIG = ["x", "w_in", "w_out", "w_gate", "w_up", "w_down", "fox_w_in_2", "fox_b_f_2", "fox_w_out_2", "s5_w_in_2",
       "s5_d_2", "s5_w_glu_2", "s5_w_out_2", "mix_post_gain_2", "ffn_post_gain_2", "ffn_w_gate_2", "ffn_w_up_2",
       "ffn_w_down_2"]


def rope_table():
    pos = np.arange(TOK, dtype=np.float32)
    inv = np.float32(10000.0) ** (-np.arange(0, HD, 2, dtype=np.float32) / np.float32(HD))
    ang = pos[:, None] * inv[None, :]
    cos, sin = np.cos(ang), np.sin(ang)
    table = np.stack([np.concatenate([cos, cos], 1), np.concatenate([-sin, sin], 1)], 1).astype(np.float32)
    return table.reshape(RT, P, 2, HD).transpose(1, 0, 2, 3)


def lay_out(inputs):
    a = {name: np.asarray(inputs[name]) for name in inputs}
    pieces = lambda v: v.reshape(-1, P).T
    twice = lambda v: np.concatenate([v, v], 0)
    vec = [pieces(a[n]) for n in ("norm1_g", "norm2_g", "mix_pre_gain_2", "ffn_pre_gain_2", "glu_b", "dw_b",
                                  "conv_ln_g", "conv_ln_b")]
    vec.append(np.zeros((P, VCOLS - 68), np.float32))
    taps = a["dw_w"][0].reshape(TAPS, 4, P).transpose(2, 0, 1).reshape(P, TAPS * 4)
    arrays = {name: a[name] for name in BIG}
    arrays["vectors"] = np.concatenate(vec + [taps], 1)
    arrays["lamdt"] = np.stack([twice(a["s5_lam_re_2"][0].T), twice(a["s5_lam_im_2"][0].T),
                                np.broadcast_to(a["s5_log_dt_2"], (P, NG))], 1)
    arrays["head_gains"] = np.concatenate([a[n].reshape(1, HD) for n in ("q_norm_g", "k_norm_g", "fox_q_gain_2",
                                                                          "fox_k_gain_2")], 1)
    arrays["s5_b"] = np.stack([twice(a[n][0].transpose(1, 0, 2)) for n in ("s5_b_re_2", "s5_b_im_2")], 1)
    arrays["s5_c"] = np.stack([twice(a[n][0].transpose(2, 0, 1)) for n in ("s5_c_re_2", "s5_c_im_2")], 1)
    arrays["rope"] = rope_table()
    return {name: np.ascontiguousarray(v) for name, v in arrays.items()}


def kernel(**inputs):
    import concourse.bacc as bacc
    from concourse.bass_utils import run_bass_kernel_spmd

    nc = bacc.Bacc("TRN2", target_bir_lowering=False, num_devices=1)
    arrays = lay_out(inputs)
    io = {name: nc.dram_tensor(f"in_{name}", a.shape, mybir.dt.from_np(a.dtype), kind="ExternalInput").ap()
          for name, a in arrays.items()}
    out = nc.dram_tensor("out", (1, TOK, D), F32, kind="ExternalOutput").ap()
    build(nc, io, out)
    r = run_bass_kernel_spmd(nc, [{f"in_{n}": a for n, a in arrays.items()}], core_ids=[0])
    return r.results[0]["out"]
```

```python
import math
from contextlib import ExitStack

import numpy as np

import concourse.bass as bass
from concourse import mybir

F32 = mybir.dt.float32
F32R = mybir.dt.float32r
BF16 = mybir.dt.bfloat16
ACT = mybir.ActivationFunctionType
ALU = mybir.AluOpType
AX = mybir.AxisListType

P = 128
TOK = 256
RT = TOK // P
D = 1024
KT = D // P
DFF = 2816
FT = DFF // P
FP = FT // 2
EPS = 1e-6
HD = 64
H1 = 8
H2 = 16
AW = H1 * HD
TAPS = 31
TAPG = 8
WARM = 17
VCOLS = 80
NG = 64
SC = 16
T = 8
NCH = TOK // T
GB = 4
NBLK = NG // GB
UNIT = 2048
RAW = 4
RING = 2
NEG = -3.0e38


NORMS = ("n1", "q", "k", "ln", "f1", "fp", "blk0", "blk1", "blk2", "blk3", "pm0", "f2", "pf0", "s", "pm1", "f3", "pf1")
NORM_COUNTS = {st: 1 if st in ("q", "k", "ln") or st[:3] == "blk" else RT for st in NORMS}


class Program:
    def __init__(self, nc, ctx, io):
        self.nc, self.ctx, self.io = nc, ctx, io
        self.sems = {}
        self.plan_units()
        self.place()

    KINDS = {
        "nat_ready": (("n1", "ao", "f1", "fp", "fo", "f2", "s", "f3"), 2),
        "transposed": (("n1", "ao", "f1", "fp", "fo", "f2", "s", "f3"), 8),
        "high_ready": (("n1", "ao", "f1", "fp", "fo", "f2", "s", "yg", "f3"), 8),
        "act_ready": (("n1", "ao", "f1", "fp", "fo", "f2", "s", "yg", "f3"), 8),
        "squares": (("n1", "f1", "fp", "pm0", "f2", "pf0", "s", "pm1", "f3", "pf1"), 2),
        "head_sums": (("q", "k", "ln", "blk0", "blk1", "blk2", "blk3"), 1),
        "var": (NORMS, NORM_COUNTS), "rstd": (NORMS, NORM_COUNTS),
        "first": (("o1", "f1", "o2", "f2", "o3", "f3"), 1),
        "x_ready": (("f1", "fp", "pm0", "pf0", "pm1", "pf1"), 2),
        "normed": (("pm0", "pf0", "pm1", "pf1"), 2),
        "sq": (("q", "k", "blk0", "blk1", "blk2", "blk3"), 2),
        "silu": (("f1", "f2", "f3"), FP), "prod": (("f1", "f2", "f3"), FP),
        "ghigh": (("f1", "f2", "f3"), FP), "glow": (("f1", "f2", "f3"), FP),
        "probs": (("a1", "a2"), {"a1": 2 * H1, "a2": 2 * H2}), "max": (("a1", "a2"), {"a1": 2 * H1, "a2": 2 * H2}),
        "scores": (("a1", "a2"), {"a1": H1, "a2": H2}), "turned": (("a1", "a2"), {"a1": H1, "a2": H2}),
        "pt": (("a1", "a2"), {"a1": H1, "a2": H2}), "out": (("a1", "a2"), {"a1": H1, "a2": H2}),
        "heads_in": (("a1", "a2"), {"a1": H1, "a2": H2}), "heads_out": (("a1", "a2"), {"a1": H1, "a2": H2}),
    }

    def resolve(self, name):
        stage, _, kind = name.partition("_")
        stages, count = self.KINDS.get(kind, ((), 0))
        if stage not in stages:
            return name, 0
        counts = {s: count[s] if isinstance(count, dict) else count for s in stages}
        if kind in ("transposed", "high_ready", "act_ready"):
            counts["ao"] = KT // 2
        return "all_" + kind, sum(counts[s] for s in stages[:stages.index(stage)])

    def sem(self, name):
        shared, _ = self.resolve(name)
        if shared not in self.sems:
            self.sems[shared] = self.ctx.enter_context(self.nc.semaphore(shared))
        return self.sems[shared]

    def past(self, name, value):
        return self.sem(name), self.resolve(name)[1] + value

    def plan_units(self):
        io = self.io
        self.units = []
        self.first = {}

        def rows_by(w, cols, width):
            return w[:, cols:cols + width].rearrange("(k p) c -> p k c", p=P)

        def feature_pairs(name, w, c0, n):
            self.first[name] = len(self.units)
            for i in range(n):
                self.units.append((rows_by(w, c0 + 256 * i, 256), 8))

        def half_k(name, w, c0, blocks):
            self.first[name] = len(self.units)
            for b in range(blocks):
                for hk in range(2):
                    v = w[hk * 512:(hk + 1) * 512, c0 + 512 * b:c0 + 512 * b + 512]
                    self.units.append((v.rearrange("(k p) c -> p k c", p=P), 4))

        def k_pairs(name, w, n):
            self.first[name] = len(self.units)
            for i in range(n):
                self.units.append((w[i * 256:(i + 1) * 256, :].rearrange("(k p) c -> p k c", p=P), 2))

        def ffn(name, wg, wu, wd):
            self.first[name + ".up"] = len(self.units)
            for f in range(FP):
                self.units.append((rows_by(wg, 256 * f, 256), 8))
                self.units.append((rows_by(wu, 256 * f, 256), 8))
            k_pairs(name + ".down", wd, FT // 2)

        w_in = io["w_in"][0]
        feature_pairs("u", w_in, 3 * AW, 4)
        half_k("q", w_in, 0, 1)
        half_k("k", w_in, AW, 1)
        half_k("v", w_in, 2 * AW, 1)
        k_pairs("o1", io["w_out"][0], 4)
        ffn("f1", io["w_gate"][0], io["w_up"][0], io["w_down"][0])
        fox = io["fox_w_in_2"][0]
        for name, c0 in (("fox", D), ("q0", 0), ("v0", 2 * D), ("k1", D + 512), ("q1", 512), ("v1", 2 * D + 512),
                         ("g0", 3 * D), ("g1", 3 * D + 512)):
            half_k(name, fox, c0, 1)
        k_pairs("o2", io["fox_w_out_2"][0], 4)
        ffn("f2", io["ffn_w_gate_2"][0], io["ffn_w_up_2"][0], io["ffn_w_down_2"][0])
        feature_pairs("s", io["s5_w_in_2"][0], 0, 4)
        feature_pairs("glu", io["s5_w_glu_2"][0], 0, 4)
        k_pairs("o3", io["s5_w_out_2"][0], 4)
        ffn("f3", io["ffn_w_gate_2"][1], io["ffn_w_up_2"][1], io["ffn_w_down_2"][1])

    def place(self):
        nc, ctx = self.nc, self.ctx
        end = nc.sbuf_usable_end
        cur = (nc.sbuf_base + 63) // 64 * 64

        def at(name, shape, dt, offset):
            return nc.alloc_sbuf_tensor_at(name, shape, dt, offset=offset)

        def fixed(name, shape, dt):
            nonlocal cur
            t = at(name, shape, dt, cur)
            self.where[name] = cur
            cur += (int(np.prod(shape[1:])) * (2 if dt == BF16 else 4) + 31) // 32 * 32
            return t

        self.where = {}
        self.x = fixed("x_res", [P, RT, D], F32)
        self.nat = fixed("nat", [P, RT, D], F32)
        self.actH = fixed("actH", [P, KT, TOK], F32R)
        self.actL = fixed("actL", [P, KT, TOK], F32R)
        self.wraw = fixed("wraw", [P, RAW, UNIT], F32)
        self.whi = fixed("whi", [P, RING, UNIT], F32R)
        self.wlo = fixed("wlo", [P, RING, UNIT], F32R)
        self.gb = [fixed(f"postgain{i}", [P, D], F32) for i in range(2)]
        self.ident = fixed("ident", [P, P], F32)
        self.ones = fixed("ones", [P, P], F32)
        self.tri = fixed("tri", [P, P], F32)
        self.swap = fixed("swap", [P, P], F32)
        self.identb = fixed("identb", [P, P], BF16)
        self.maskb = fixed("maskb", [P, P], BF16)
        self.vectors = fixed("vectors", [P, VCOLS + TAPS * 4], F32)
        self.vec, self.taps = self.vectors[:, 0:VCOLS], self.vectors[:, VCOLS:]
        self.mhalf = fixed("mhalf", [P, 16], F32)
        self.halfpi = fixed("halfpi", [P, 1], F32)
        self.zero1 = fixed("zero1", [P, 1], F32)
        self.ss = fixed("ss", [P, 16], F32)
        self.rdiag = fixed("rdiag", [P, RT, P], F32)
        self.rs = fixed("rs", [P, 16], F32)
        self.cosT = fixed("cosT", [P, NG], F32)
        self.sinT = fixed("sinT", [P, NG], F32)
        self.magT = fixed("magT", [P, NG], F32)
        self.qkg = fixed("qkg", [P, 4, HD], F32)
        self.nmax, self.rsum, self.rinv = (fixed(n, [P, RT, H2], F32) for n in ("nmax", "rsum", "rinv"))
        R0 = cur

        class Pen:
            def __init__(s, base, top=end):
                s.cur, s.top = base, top

            def __call__(s, name, shape, dt=F32):
                t = at(name, shape, dt, s.cur)
                self.where[name] = s.cur
                s.cur += (int(np.prod(shape[1:])) * (2 if dt == BF16 else 4) + 31) // 32 * 32
                assert s.cur <= s.top, (name, s.cur, s.top)
                return t

        prep_bytes = 4 * 4096 + 2 * 2304 + 2 * 2048
        work_bytes = 2 * 2048 + 2304 + 2 * 2304 + 2 * 2048 + 2 * 4096
        W0 = end - end % 32 - work_bytes
        P0 = W0 - prep_bytes
        pen = Pen(P0, W0)
        self.BB1, self.BB2 = pen("BB1", [P, NG, SC]), pen("BB2", [P, NG, SC])
        self.C12 = pen("C12", [P, 2, NG, SC])
        self.C1, self.C2 = self.C12[:, 0], self.C12[:, 1]
        self.F1, self.F2 = pen("F1", [P, NG, T + 1]), pen("F2", [P, NG, T + 1])
        self.G1, self.G2 = pen("G1", [P, NG, T]), pen("G2", [P, NG, T])
        pen = Pen(W0)
        self.rtb = pen("rtb", [P, 2, GB, T, SC])
        self.ob = pen("ob", [P, 2, GB, T + 1, SC])
        self.otmp = pen("otmp", [P, GB, T + 1, SC])
        self.rsb = pen("rsb", [P, 2, GB, P])
        self.ksb = pen("ksb", [P, 2, 2 * P])
        pen = Pen(W0)
        self.Bri = pen("Bri", [P, 2, NG, SC])
        self.btmp = pen("btmp", [P, NG, SC])
        self.AR, self.AI = pen("AR", [P, NG, T + 1]), pen("AI", [P, NG, T + 1])
        self.atmp, self.atmp2 = pen("atmp", [P, NG, 4]), pen("atmp2", [P, NG, 4])
        pen = Pen(self.where["postgain0"], self.where["postgain0"] + 8192)
        self.lamdt = pen("s5_lamdt", [P, 3, NG])
        self.small = {n: self.lamdt[:, i] for i, n in enumerate(("LR", "LI", "ldt"))}
        self.small |= {n: pen("s5_" + n, [P, NG]) for n in
                      ("dt lr th k t thr ab sh tt lrc lrb eb r1 r2 den rden em ar ai nre zr zi "
                       "m1").split()}

        pen = Pen(R0, P0)
        self.hpad = pen("hpad", [P, 4, TAPS - 1 + TOK])
        self.cacc = pen("cacc", [P, 4, TOK])
        self.csig = pen("csig", [P, 4, TOK])
        self.qn, self.kn = pen("qn", [P, RT, AW]), pen("kn", [P, RT, AW])
        self.vn = pen("vn", [P, RT, AW])
        self.qt, self.kt1 = pen("qt1", [HD, H1, TOK]), pen("kt1", [HD, H1, TOK])
        self.p1 = pen("p1", [P, 2, 384])
        self.pt1 = pen("pt1", [P, 2, 384])
        self.ropeg = pen("ropeg", [P, 2, RT, 2, HD])
        self.ctmp = pen("ctmp", [P, TOK])
        self.dtaps = at("dtaps", [P, 2 * TAPG, P], F32, self.where["nat"])
        self.sq1 = at("sq1", [P, RT, AW], F32, self.where["csig"])
        self.csq = at("csq", [P, 4, TOK], F32, self.where["csig"])
        self.rope = at("rope", [P, RT, 2, HD], F32, self.where["pt1"] + 2048)
        self.diag = at("diag", [P, 2 * P], F32, self.where["p1"])
        self.rtmp = at("rtmp", [P, AW], F32, self.where["p1"])
        self.rtmp2 = at("rtmp2", [P, AW], F32, self.where["pt1"])

        pen = Pen(R0, P0)
        self.gH, self.gL = pen("gH", [P, FT, TOK], F32R), pen("gL", [P, FT, TOK], F32R)
        self.sg = pen("sg", [P, 2 * TOK])
        self.prod = pen("prod", [P, 2 * TOK])

        pen = Pen(R0)
        AUG = HD + 2
        self.qa, self.ka = pen("qa", [P, RT, H2, AUG]), pen("ka", [P, RT, H2, AUG])
        self.va = pen("va", [P, RT, D])
        self.ga = pen("ga", [P, RT, D])
        self.qt2, self.kt2 = pen("qt2", [AUG, H2, TOK]), pen("kt2", [AUG, H2, TOK])
        self.p2, self.pt2 = pen("p2", [P, 2, 384]), pen("pt2", [P, 2, 384])
        self.sq2 = pen("sq2", [P, RT, 512])
        self.wf = pen("wf", [P, KT, H2])
        self.wfH, self.wfL = pen("wfH", [P, KT, H2], F32R), pen("wfL", [P, KT, H2], F32R)
        self.fb = pen("fb", [P, H2])
        self.fl = pen("fl", [P, 4, RT, H2])
        self.fT = at("fT", [H2, TOK], F32, self.where["p2"])

        pen = Pen(R0)
        self.RTab = pen("RTab", [P, NG, P])
        self.OTab = pen("OTab", [P, NG, P])
        self.Uall = pen("Uall", [P, 16, 4, NCH])
        self.CT, self.ST = pen("CT", [P, NG, NCH]), pen("ST", [P, NG, NCH])
        d0 = pen.cur
        self.D0 = pen("D0", [P, NG, NCH])
        self.X33 = at("X33", [P, NG, NCH + 1], F32, d0)
        self.uT = self.nat[:].rearrange("p h (t j c) -> p h t j c", t=T, j=4)
        self.TTab = at("TTab", [P, NG, P], F32, R0)
        self.sgT, self.yoT = (at(n, [P, KT, TOK], F32, R0 + 8192 * i) for i, n in enumerate(("sgT", "yoT")))
        self.yoH, self.yoL = (at(n, [P, KT, TOK], F32R, R0 + 8192 * i) for i, n in ((2, "yoH"), (3, "yoL")))
        self.ygT = at("ygT", [P, KT, TOK], F32, self.where["Uall"])
        self.V = at("Vst", [P, NG, NCH], F32, self.where["actH"])
        self.W = at("Wst", [P, NG, NCH], F32, self.where["actL"])
        self.Ur = at("Ur", [P, 16, T, SC], F32, self.where["actL"])
        self.Vc = at("Vc", [P, 16, P], F32, self.where["actL"])
        self.Ysb = at("Ysb", [P, T, 16, SC], F32, self.where["CT"])
        self.ctmp1 = at("ctmp1", [P, NG, 16], F32, self.where["Uall"])
        self.ctmp2 = at("ctmp2", [P, NG, 16], F32, self.where["Uall"] + 4096)

        self.ps = ctx.enter_context(nc.psum_tensor("ps", [P, 8, 512], F32))
        dr = lambda n, s: nc.dram_tensor(n, s, F32, kind="Internal").ap()
        self.Rd, self.Od = dr("R_dram", [P, NG, P]), dr("O_dram", [P, NG, P])
        self.Kd = dr("K_dram", [P, NBLK, 2 * P])
        s = self.sem
        self.landed = [s(f"raw_landed{i}") for i in range(RAW)]
        self.hi_done, self.lo_done, self.used = s("hi_done"), s("lo_done"), s("unit_used")

    def load_unit(self, sp, n0, view, it=0):
        n = n0 + 4 * it
        if n0 >= RAW:
            sp.wait_ge(self.lo_done, n - RAW + 1)
        k = view.shape[1]
        dst = self.wraw[:, n0 % RAW, :].rearrange("p (k c) -> p k c", k=k)
        sp.dma_start(dst, view).then_inc(self.landed[n0 % RAW], 16)

    def split_high(self, act, n0, it=0):
        n = n0 + 4 * it
        act.wait_ge(self.landed[n0 % RAW], 16 * (n0 // RAW + 1) + 16 * it)
        if n0 >= RING:
            act.wait_ge(self.used, n - RING + 1)
        act.activation(self.whi[:, n0 % RING, :], self.wraw[:, n0 % RAW, :], ACT.Copy).then_inc(self.hi_done, 1)

    def split_low(self, dve, n0, it=0):
        n = n0 + 4 * it
        dve.wait_ge(self.hi_done, n + 1)
        dve.tensor_tensor(self.wlo[:, n0 % RING, :], self.wraw[:, n0 % RAW, :],
                          self.whi[:, n0 % RING, :].bitcast(F32), ALU.subtract).then_inc(self.lo_done, 1)

    def mm_features(self, pe, n0, bank, it=0, ready=None, order=range(KT)):
        pe.wait_ge(self.lo_done, n0 + 4 * it + 1)
        s = n0 % RING
        for f in range(2):
            out = self.ps[:, bank, f * TOK:(f + 1) * TOK]
            for i, k in enumerate(order):
                if ready is not None and f == 0:
                    pe.wait_ge(*self.past(ready, i + 1))
                c = k * 256 + f * P
                wh, wl = self.whi[:, s, c:c + P], self.wlo[:, s, c:c + P]
                pe.matmul(out, wh, self.actH[:, k, :], start=(i == 0), stop=False)
                pe.matmul(out, wh, self.actL[:, k, :], start=False, stop=False)
                last = pe.matmul(out, wl, self.actH[:, k, :], start=False, stop=(i == KT - 1))
        last.then_inc(self.used, 1)

    def mm_quarter(self, pe, n0, banks, half, k, ready=None):
        if k == 0:
            pe.wait_ge(self.lo_done, n0 + 1)
        s = n0 % RING
        ka = 4 * half + k
        if ready is not None:
            pe.wait_ge(*self.past(ready, ka + 1))
        wh, wl = self.whi[:, s, k * 512:(k + 1) * 512], self.wlo[:, s, k * 512:(k + 1) * 512]
        for r in range(RT):
            out = self.ps[:, banks[r], :]
            xh, xl = self.actH[:, ka, r * P:(r + 1) * P], self.actL[:, ka, r * P:(r + 1) * P]
            pe.matmul(out, xh, wh, start=(ka == 0), stop=False)
            pe.matmul(out, xh, wl, start=False, stop=False)
            last = pe.matmul(out, xl, wh, start=False, stop=(ka == KT - 1))
        if k == 3:
            last.then_inc(self.used, 1)

    def mm_half_k(self, pe, n0, banks, half, ready=None):
        for k in range(4):
            self.mm_quarter(pe, n0, banks, half, k, ready)

    def mm_k_pair(self, pe, n0, base, xh, xl, k0, kn, waits=(), step=1, first=None):
        pe.wait_ge(self.lo_done, n0 + 1)
        s = n0 % RING
        order = [(k, r) for k in range(2) for r in range(RT)] if first is None else \
            [(k, r) for r in range(RT) for k in range(2)]
        for k, r in order:
            if r == 0:
                for name, value in waits:
                    pe.wait_ge(*self.past(name, value + step * k))
            h, l = xh[:, k0 + k, r * P:(r + 1) * P], xl[:, k0 + k, r * P:(r + 1) * P]
            w = [[t[:, s, k * 1024 + c * 512:k * 1024 + (c + 1) * 512] for c in range(2)]
                 for t in (self.whi, self.wlo)]
            st, sp_ = k0 + k == 0, k0 + k == kn - 1
            for c in range(2):
                pe.matmul(self.ps[:, base + 2 * r + c, :], h, w[0][c], start=st, stop=False)
            for c in range(2):
                pe.matmul(self.ps[:, base + 2 * r + c, :], h, w[1][c], start=False, stop=False)
            for c in range(2):
                last = pe.matmul(self.ps[:, base + 2 * r + c, :], l, w[0][c], start=False, stop=sp_)
            if first is not None and (k, r) == (1, 0):
                last.then_inc(self.sem(first), 1)
        last.then_inc(self.used, 1)

    def tp_spot(self, kt, banks):
        b, h = banks[kt % len(banks)], kt // len(banks)
        return self.ps[:, b, h * TOK:(h + 1) * TOK]

    def keep_warm(self, pe, bank, count=WARM):
        for _ in range(count):
            pe.matmul(self.ps[:, bank, :].rearrange("p (a b) -> p a b", a=4), self.identb[:],
                      self.identb[:].unsqueeze(1).to_broadcast([P, 4, P]), start=True, stop=True)

    def pe_turn(self, pe, st, banks, n=KT, scaled=True):
        def one(kt, r):
            out = self.tp_spot(kt, banks)[:, r * P:(r + 1) * P]
            cols = slice(kt * P, (kt + 1) * P)
            if scaled:
                return pe.matmul(out, self.x[:, r, cols], self.rdiag[:, r, :], start=True, stop=True)
            return pe.transpose(out, self.nat[:, r, cols], self.ident[:])

        early = len(banks) if scaled else 0
        for r in range(RT):
            pe.wait_ge(*self.past(st + "_nat_ready", r + 1))
            for kt in range(early):
                last = one(kt, r)
                if r == RT - 1:
                    last.then_inc(self.sem(st + "_transposed"), 1)
        for kt in range(early, n):
            if kt >= len(banks):
                pe.wait_ge(*self.past(st + "_act_ready", kt - len(banks) + 1))
            for r in range(RT):
                last = one(kt, r)
            last.then_inc(self.sem(st + "_transposed"), 1)

    def act_turn(self, act, st, banks, n=KT, gain=None):
        for kt in range(n):
            act.wait_ge(*self.past(st + "_transposed", kt + 1))
            g = 1.0 if gain is None else self.vec[:, gain + kt:gain + kt + 1]
            act.activation(self.actH[:, kt, :], self.tp_spot(kt, banks), ACT.Copy, scale=g)\
               .then_inc(self.sem(st + "_high_ready"), 1)

    def dve_turn(self, dve, st, banks, n=KT, gain=None):
        for kt in range(n):
            dve.wait_ge(*self.past(st + "_high_ready", kt + 1))
            hi = self.actH[:, kt, :].bitcast(F32)
            if gain is None:
                i = dve.tensor_tensor(self.actL[:, kt, :], self.tp_spot(kt, banks), hi, ALU.subtract)
            else:
                i = dve.scalar_tensor_tensor(self.actL[:, kt, :], self.tp_spot(kt, banks),
                                             self.vec[:, gain + kt:gain + kt + 1], hi, ALU.mult, ALU.subtract)
            i.then_inc(self.sem(st + "_act_ready"), 1)

    def act_squares(self, act, st, src, r, *ready):
        act.wait_ge(*ready)
        act.activation(self.nat[:, r, :], src, ACT.Square, accum_out=self.ss[:, r:r + 1])\
           .then_inc(self.sem(st + "_squares"), 1)

    def act_norms(self, act, post, pre, base, first, used):
        for r in range(RT):
            ready = self.past(first, 1) if r == 0 else (self.used, used)
            self.act_squares(act, post, self.acc_row(base, r), r, *ready)
        if pre:
            for r in range(RT):
                self.act_squares(act, pre, self.x[:, r, :], r, *self.past(post + "_x_ready", r + 1))

    def pool_rstd(self, pool, st, mean_of, ready, cols=None):
        for i, c in enumerate((slice(0, 1), slice(1, 2)) if cols is None else (slice(0, cols),)):
            rs = self.rs[:, c]
            pool.wait_ge(*self.past(ready, i + 1))
            pool.tensor_scalar(rs, self.ss[:, c], 1.0 / mean_of, EPS, ALU.mult, ALU.add)\
                .then_inc(self.sem(st + "_var"), 1)
            pool.wait_ge(*self.past(st + "_var", i + 1))
            pool.tensor_tensor(rs, rs, self.mhalf[:, c], ALU.pow).then_inc(self.sem(st + "_rstd"), 1)

    def dve_scale(self, dve, st):
        for r in range(RT):
            dve.wait_ge(*self.past(st + "_rstd", r + 1))
            dve.tensor_scalar(self.rdiag[:, r, :], self.ident[:], self.rs[:, r:r + 1], None, ALU.mult)\
               .then_inc(self.sem(st + "_nat_ready"), 1)

    def acc_row(self, base, r):
        return self.ps[:, base + 2 * r:base + 2 * r + 2, :]

    def dve_postnorm(self, dve, st, base, gain, gain_ready, gain_value):
        dve.wait_ge(*self.past(gain_ready, gain_value))
        g = gain[:].rearrange("p (a b) -> p a b", a=2)
        for r in range(RT):
            dve.wait_ge(*self.past(st + "_squares", r + 1))
            t = self.nat[:, r, :].rearrange("p (a b) -> p a b", a=2)
            dve.tensor_tensor(t, self.acc_row(base, r), g, ALU.mult).then_inc(self.sem(st + "_normed"), 1)
            dve.wait_ge(*self.past(st + "_normed", r + 1))
            dve.wait_ge(*self.past(st + "_rstd", r + 1))
            dve.scalar_tensor_tensor(self.x[:, r, :], self.nat[:, r, :], self.rs[:, r:r + 1], self.x[:, r, :],
                                     ALU.mult, ALU.add).then_inc(self.sem(st + "_x_ready"), 1)

    def ffn_banks(self, a):
        return a, a + 1, (4 if a == 0 else 0)

    def pe_pair(self, pe, st, n0, a, f0, it=0, f_step=0, ready=None):
        f = f0 + f_step * it
        if f0 > 0:
            pe.wait_ge(*self.past(st + "_silu", f))
        self.mm_features(pe, n0, a, it, ready)
        if f0 > 0:
            pe.wait_ge(*self.past(st + "_prod", f))
        self.mm_features(pe, n0 + 1, a + 1, it)

    def act_pair(self, act, st, n0, a, f0, it=0, f_step=0):
        f = f0 + f_step * it
        act.wait_ge(self.used, n0 + 4 * it + 1)
        if f0 > 0:
            act.wait_ge(*self.past(st + "_prod", f))
        act.activation(self.sg[:], self.ps[:, a, :], ACT.Silu).then_inc(self.sem(st + "_silu"), 1)
        self.split_high(act, n0 + 2, it)
        self.split_high(act, n0 + 3, it)
        act.wait_ge(*self.past(st + "_prod", f + 1))
        dst = self.gH[:, bass.ds(2 * f, 2), :] if f_step else self.gH[:, 2 * f:2 * f + 2, :]
        act.activation(dst, self.prod[:].rearrange("p (a b) -> p a b", a=2), ACT.Copy)\
           .then_inc(self.sem(st + "_ghigh"), 1)

    def dve_pair(self, dve, st, n0, a, f0, it=0, f_step=0):
        f = f0 + f_step * it
        self.split_low(dve, n0 + 2, it)
        dve.wait_ge(self.used, n0 + 4 * it + 2)
        dve.wait_ge(*self.past(st + "_silu", f + 1))
        if f0 > 0:
            dve.wait_ge(*self.past(st + "_glow", f))
        dve.tensor_tensor(self.prod[:], self.sg[:], self.ps[:, a + 1, :], ALU.mult)\
           .then_inc(self.sem(st + "_prod"), 1)
        self.split_low(dve, n0 + 3, it)
        dve.wait_ge(*self.past(st + "_ghigh", f + 1))
        hi = self.gH[:, bass.ds(2 * f, 2), :] if f_step else self.gH[:, 2 * f:2 * f + 2, :]
        lo = self.gL[:, bass.ds(2 * f, 2), :] if f_step else self.gL[:, 2 * f:2 * f + 2, :]
        dve.tensor_tensor(lo, self.prod[:].rearrange("p (a b) -> p a b", a=2), hi.bitcast(F32), ALU.subtract)\
           .then_inc(self.sem(st + "_glow"), 1)

    def over_pairs(self, eng, one, prep=None):
        one(0, 0, 0, 0)
        if prep:
            prep(0, 0, 0)
        with eng.Fori(0, (FP - 1) // 2) as it:
            for j in range(2):
                one(2 + 2 * j, 1 + j, it, 2)
                if prep:
                    prep(1 + j, it, 2)

    def pe_ffn(self, pe, st, a, prep=False):
        n = self.first[st + ".up"]
        act_ready = st + "_act_ready"
        self.over_pairs(pe, lambda dn, f0, it, fs: self.pe_pair(
            pe, st, n + dn, a, f0, it, fs, act_ready if dn == 0 else None),
            (lambda b0, it, bs: self.pe_prep(pe, a, b0, it, bs)) if prep else None)
        n = self.first[st + ".down"]
        base = self.ffn_banks(a)[2]
        for i in range(FT // 2):
            if i == 0:
                pe.wait_ge(*self.past(act_ready, KT))
            pe.wait_ge(*self.past(st + "_glow", i + 1))
            self.mm_k_pair(pe, n + i, base, self.gH, self.gL, 2 * i, FT,
                           first=st + "_first" if i == FT // 2 - 1 else None)
            if prep and i % 2 == 1:
                self.pe_prep(pe, a, FP + i // 2)

    def act_ffn(self, act, st, a, prep=False):
        n = self.first[st + ".up"]
        self.over_pairs(act, lambda dn, f0, it, fs: self.act_pair(act, st, n + dn, a, f0, it, fs),
                        (lambda b0, it, bs: self.act_prep(act, a, b0, it, bs)) if prep else None)
        n = self.first[st + ".down"]
        for i in range(FT // 2):
            if n + i + 2 < len(self.units) and i < FT // 2 - 1:
                self.split_high(act, n + i + 2)
            if prep and i % 2 == 1:
                self.act_prep(act, a, FP + i // 2)

    def dve_ffn(self, dve, st, a):
        n = self.first[st + ".up"]
        self.over_pairs(dve, lambda dn, f0, it, fs: self.dve_pair(dve, st, n + dn, a, f0, it, fs))
        n = self.first[st + ".down"]
        for i in range(FT // 2 - 1):
            if n + i + 2 < len(self.units):
                self.split_low(dve, n + i + 2)

    def pool_prep(self, pool, b0, it=0, step=0):
        b = b0 + step * it
        half = b0 // 2 + it if step else b0 // 2
        done = self.sem("prep_pool")
        s = b0 % 2
        if b0 > 0:
            pool.wait_ge(*self.past("prep_kmul", b if b0 == 1 else b - 1))
            pool.wait_ge(*self.past(f"prep_stored{s}", 48 * half + 1))
        g = bass.ds(GB * b, GB) if step else slice(GB * b, GB * b + GB)

        def times(out, f, w, n):
            return pool.tensor_tensor(out, f[:, g, :].unsqueeze(3).to_broadcast([P, GB, n, SC]),
                                      w[:, g, :].unsqueeze(2).to_broadcast([P, GB, n, SC]), ALU.mult)

        if b0 > 0:
            pool.wait_ge(done, 6 * b)
        r, o, t = self.rtb[:, s], self.ob[:, s], self.otmp
        times(r, self.G1, self.BB1, T).then_inc(done, 1)
        times(t[:, :, 0:T, :], self.G2, self.BB2, T).then_inc(done, 1)
        pool.wait_ge(done, 6 * b + 2)
        pool.tensor_tensor(r, r, t[:, :, 0:T, :], ALU.add).then_inc(done, 1)
        times(o, self.F1, self.C1, T + 1).then_inc(done, 1)
        pool.wait_ge(done, 6 * b + 3)
        times(t[:], self.F2, self.C2, T + 1).then_inc(done, 1)
        pool.wait_ge(done, 6 * b + 5)
        pool.tensor_tensor(o, o, t[:], ALU.add).then_inc(done, 1)

    def pe_prep(self, pe, a, b0, it=0, step=0):
        b = b0 + step * it
        s = b0 % 2
        pe.wait_ge(*self.past("prep_pool", 6 * b + 6))
        if b0 > 0:
            pe.wait_ge(*self.past("prep_rout", b))
            pe.wait_ge(*self.past("prep_kout", b))
        for i in range(GB):
            last = pe.transpose(self.ps[:, a + 2, i * P:(i + 1) * P],
                                self.rtb[:, s, i, :, :].rearrange("p t c -> p (t c)"), self.ident[:])
        last.then_inc(self.sem("prep_turned"), 1)
        for i in range(GB):
            last = pe.matmul(self.ps[32 * i:32 * i + 32, a + 3, 0:P],
                             self.rtb[:, s, i, T - 2:T, :].rearrange("p t c -> p (t c)"),
                             self.ob[:, s, i, 0:T, :].rearrange("p t c -> p (t c)"), start=True, stop=True)
        last.then_inc(self.sem("prep_kmul"), 1)

    def act_prep(self, act, a, b0, it=0, step=0):
        b = b0 + step * it
        half = b0 // 2 + it if step else b0 // 2
        s = b0 % 2
        act.wait_ge(*self.past("prep_turned", b + 1))
        act.wait_ge(*self.past(f"prep_stored{s}", 48 * half + 1))
        act.activation(self.rsb[:, s], self.ps[:, a + 2, :].rearrange("p (i c) -> p i c", i=GB), ACT.Copy)\
           .then_inc(self.sem("prep_rout"), 1)
        act.wait_ge(*self.past("prep_kmul", b + 1))
        act.activation(self.ksb[:, s, P:2 * P], self.ps[:, a + 3, 0:P], ACT.Copy)\
           .then_inc(self.sem("prep_kout"), 1)
        act.wait_ge(*self.past("prep_kout", b + 1))
        g = bass.ds(GB * b, GB) if step else slice(GB * b, GB * b + GB)
        stored = self.sem(f"prep_stored{s}")
        act.dma_start(self.Rd[:, g, :], self.rsb[:, s]).then_inc(stored, 16)
        act.dma_start(self.Kd[:, bass.ds(b, 1) if step else slice(b, b + 1), :], self.ksb[:, s:s + 1])\
           .then_inc(stored, 16)
        act.dma_start(self.Od[:, g, :].rearrange("p g (t c) -> p g t c", c=SC),
                      self.ob[:, s, :, 1:T + 1, :]).then_inc(stored, 16)

    def pe_attention(self, pe, st, heads, qt, kt, v, p, pt, sb, tb, o_at, between=None):
        h0, h1 = heads

        def scores(h):
            if h >= 2:
                pe.wait_ge(*self.past(st + "_probs", 2 * (h - 1)))
            b = sb[h % 2]
            for r in range(RT):
                c0, nk = (0, P) if r == 0 else (P, 2 * P)
                out = self.ps[:, b, c0:c0 + nk]
                pe.matmul(out, qt[:, h, r * P:(r + 1) * P], kt[:, h, 0:nk], start=True, stop=False)
                last = pe.matmul(self.ps[:, b, c0 + nk - P:c0 + nk], self.identb[:], self.maskb[:],
                                 start=False, stop=True)
            last.then_inc(self.sem(st + "_scores"), 1)

        def turn(h):
            pe.wait_ge(*self.past(st + "_probs", 2 * (h + 1)))
            if h >= 2:
                pe.wait_ge(*self.past(st + "_pt", h - 1))
            for i in range(3):
                last = pe.transpose(self.ps[:, tb[h % 2], i * P:(i + 1) * P], p[:, h % 2, i * P:(i + 1) * P],
                                    self.ident[:])
            last.then_inc(self.sem(st + "_turned"), 1)

        def values(h):
            pe.wait_ge(*self.past(st + "_pt", h + 1))
            for r in range(RT):
                for k in range(r + 1):
                    i = r + k
                    last = pe.matmul(o_at(r, h), pt[:, h % 2, i * P:(i + 1) * P],
                                     v[:, k, h * HD:(h + 1) * HD], start=(k == 0), stop=(k == r))
            last.then_inc(self.sem(st + "_out"), 1)

        for h in range(h0, h1 + 2):
            if h < h1:
                scores(h)
                if between:
                    between(3 * h)
            if h0 + 1 <= h <= h1:
                turn(h - 1)
            if h < h1 and between:
                between(3 * h + 1)
            if h >= h0 + 2:
                values(h - 2)
            if h < h1 and between:
                between(3 * h + 2)

    def act_attention(self, act, st, h, p, rsum, nmax, sb):
        act.wait_ge(*self.past(st + "_max", 2 * (h + 1)))
        if h >= 2:
            act.wait_ge(*self.past(st + "_turned", h - 1))
        for r in range(RT):
            c0, nk = (0, P) if r == 0 else (P, 2 * P)
            act.activation(p[:, h % 2, c0:c0 + nk], self.ps[:, sb[h % 2], c0:c0 + nk], ACT.Exp,
                           bias=nmax[:, r, h:h + 1], accum_out=rsum[:, r, h:h + 1])\
               .then_inc(self.sem(st + "_probs"), 1)

    def dve_attention(self, dve, st, heads, pt, nmax, sb, tb, between=None):
        h0, h1 = heads
        for h in range(h0, h1 + 1):
            if h < h1:
                dve.wait_ge(*self.past(st + "_scores", h + 1))
                for r in range(RT):
                    c0, nk = (0, P) if r == 0 else (P, 2 * P)
                    dve.reduce_max(nmax[:, r, h:h + 1], self.ps[:, sb[h % 2], c0:c0 + nk], AX.X, negate=True)\
                       .then_inc(self.sem(st + "_max"), 1)
            if h > h0:
                g = h - 1
                dve.wait_ge(*self.past(st + "_turned", g + 1))
                if g >= 2:
                    dve.wait_ge(*self.past(st + "_out", g - 1))
                dve.tensor_copy(pt[:, g % 2, :], self.ps[:, tb[g % 2], 0:384]).then_inc(self.sem(st + "_pt"), 1)
            if between:
                between(h)

    def pe_heads(self, pe, st, src, heads, ready, value, banks, first_fill):
        pe.wait_ge(*self.past(ready, value))
        w = src.shape[-1]
        for f in range((heads[1] - heads[0]) // 2):
            n = first_fill + f
            if n >= 2:
                pe.wait_ge(*self.past(st + "_heads_out", n - 1))
            for i in range(2):
                for r in range(RT):
                    c = (2 * i + r) * P
                    last = pe.transpose(self.ps[0:w, banks[n % 2], c:c + P], src[:, r, heads[0] + 2 * f + i, :],
                                        self.ident[:])
            last.then_inc(self.sem(st + "_heads_in"), 1)

    def act_heads(self, act, st, dst, heads, banks, first_fill):
        w = dst.shape[0]
        for f in range((heads[1] - heads[0]) // 2):
            n = first_fill + f
            h = heads[0] + 2 * f
            act.wait_ge(*self.past(st + "_heads_in", n + 1))
            act.activation(dst[:, h:h + 2, :], self.ps[0:w, banks[n % 2], :].rearrange("p (h t) -> p h t", h=2),
                           ACT.Copy).then_inc(self.sem(st + "_heads_out"), 1)


class Chain:

    def __init__(self, eng, sem):
        self.eng, self.sem, self.n = eng, sem, 0

    def step(self, ins):
        ins.then_inc(self.sem, 1)
        self.n += 1
        return self.n

    def wait(self, n=None):
        self.eng.wait_ge(self.sem, self.n if n is None else n)

    def __call__(self, ins):
        self.step(ins)
        self.wait()


def pool_constants(m, pool):
    c = Chain(pool, m.sem("pool_chain"))
    for t, v in ((m.ident, 0.0), (m.ones, 1.0), (m.tri, 1.0), (m.swap, 0.0), (m.identb, 0.0), (m.maskb, 0.0),
                 (m.mhalf, -0.5), (m.halfpi, math.pi / 2), (m.hpad[:, :, 0:TAPS - 1], 0.0)):
        c.step(pool.memset(t[:] if not isinstance(t, bass.AP) else t, v))
    c.wait()

    def select(t, op, fill, base, step, mult):
        c.step(pool.affine_select(out=t, in_=t, compare_op=op, fill=fill, base=base,
                                  pattern=[[step, t.shape[-1]]], channel_multiplier=mult))

    select(m.ident[:], ALU.not_equal, 1.0, 0, -1, 1)
    select(m.identb[:], ALU.not_equal, 1.0, 0, -1, 1)
    select(m.tri[:], ALU.is_ge, 0.0, 0, 1, -1)
    select(m.maskb[:], ALU.is_ge, NEG, 0, -1, 1)
    select(m.swap[:, 0:64], ALU.not_equal, 1.0, -64, -1, 1)
    select(m.swap[:, 64:128], ALU.not_equal, 1.0, 0, -1, 1)
    c.wait()
    pool.memset(m.zero1[:], 0.0).then_inc(m.sem("consts"), 1)
    return c


def cmul(c, pool, out, x, y, tmp):
    (orr, oi), (xr, xi), (yr, yi) = out, x, y
    t1, t2 = tmp
    c.step(pool.tensor_tensor(orr, xr, yr, ALU.mult))
    c.step(pool.tensor_tensor(t1, xi, yi, ALU.mult))
    c.step(pool.tensor_tensor(oi, xr, yi, ALU.mult))
    c.step(pool.tensor_tensor(t2, xi, yr, ALU.mult))
    c.wait()
    c.step(pool.tensor_tensor(orr, orr, t1, ALU.subtract))
    c.step(pool.tensor_tensor(oi, oi, t2, ALU.add))
    c.wait()


def powers(c, pool, tr, ti, base, tmp1, tmp2, count):
    c.step(pool.memset(tr[:, :, 0:1], 1.0))
    c.step(pool.memset(ti[:, :, 0:1], 0.0))
    c.step(pool.tensor_copy(tr[:, :, 1:2], base[0].unsqueeze(2)))
    c.step(pool.tensor_copy(ti[:, :, 1:2], base[1].unsqueeze(2)))
    c.wait()
    n = 1
    while n < count - 1:
        k = min(n, count - 1 - n)
        b = [t[:, :, n:n + 1].to_broadcast([P, NG, k]) for t in (tr, ti)]
        cmul(c, pool, (tr[:, :, n + 1:n + 1 + k], ti[:, :, n + 1:n + 1 + k]),
             (tr[:, :, 1:1 + k], ti[:, :, 1:1 + k]), b, (tmp1[:, :, 0:k], tmp2[:, :, 0:k]))
        n += k


Y_ORDER = (0, 2, 4, 6, 1, 3, 5, 7)

TWO_PI = 2 * math.pi
PI_A = 6.28125
PI_B = math.floor((TWO_PI - PI_A) * 2 ** 21) / 2 ** 21
PI_C = float(np.float32(TWO_PI - PI_A - PI_B))
ROUND = 12582912.0


def pool_s5_scalars(m, c, pool):
    s = {k: v[:] for k, v in m.small.items()}
    pool.wait_ge(*m.past("lamdt_in", 16))
    pool.wait_ge(*m.past("dt", 1))
    tt, ts = pool.tensor_tensor, pool.tensor_scalar
    c.step(tt(s["lr"], s["LR"], s["dt"], ALU.mult))
    c.step(tt(s["th"], s["LI"], s["dt"], ALU.mult))
    c.wait()
    c.step(ts(s["lrc"], s["lr"], 1.0, None, ALU.min))
    c.step(ts(s["lrb"], s["lr"], 88.0, None, ALU.min))
    c(ts(s["k"], s["th"], 1.0 / TWO_PI, ROUND, ALU.mult, ALU.add))
    c(ts(s["k"], s["k"], ROUND, None, ALU.subtract))
    for i, part in enumerate((PI_A, PI_B, PI_C)):
        c(ts(s["t"], s["k"], part, None, ALU.mult))
        c(tt(s["thr"], s["th"] if i == 0 else s["thr"], s["t"], ALU.subtract))
    ts(s["thr"], s["thr"], 3.1415925, -3.1415925, ALU.min, ALU.max).then_inc(m.sem("angle"), 1)
    c.step(tt(s["den"], s["LR"], s["LR"], ALU.mult))
    c.step(tt(s["m1"], s["LI"], s["LI"], ALU.mult))
    c.wait()
    tt(s["den"], s["den"], s["m1"], ALU.add).then_inc(m.sem("den"), 1)


def pool_s5_growth(m, c, pool):
    s = {k: v[:] for k, v in m.small.items()}
    tt, ts = pool.tensor_tensor, pool.tensor_scalar
    pool.wait_ge(*m.past("s5_functions", 5))
    pool.wait_ge(*m.past("s5_recips", 2))
    c.step(ts(s["tt"], s["tt"], 2.0, None, ALU.mult))
    c.step(ts(s["eb"], s["eb"], 1.0, None, ALU.subtract))
    c.step(ts(s["m1"], s["lr"], 1.0, None, ALU.is_gt))
    c.wait()
    c(tt(s["em"], s["tt"], s["r1"], ALU.mult))
    c(tt(s["eb"], s["eb"], s["em"], ALU.subtract))
    c(tt(s["eb"], s["eb"], s["m1"], ALU.mult))
    c(tt(s["em"], s["em"], s["eb"], ALU.add))
    c.step(ts(m.magT[:], s["em"], 1.0, None, ALU.add))
    c.step(tt(s["nre"], s["em"], m.cosT[:], ALU.mult))
    c.step(tt(s["sh"], s["sh"], s["sh"], ALU.mult))
    c.wait()
    c.step(ts(s["sh"], s["sh"], 2.0, None, ALU.mult))
    c.step(tt(s["ar"], m.magT[:], m.cosT[:], ALU.mult))
    c.step(tt(s["ai"], m.magT[:], m.sinT[:], ALU.mult))
    c.wait()
    c(tt(s["nre"], s["nre"], s["sh"], ALU.subtract))
    for out, (a, b), (d, e), op in (("zr", ("nre", "LR"), ("ai", "LI"), ALU.add),
                                    ("zi", ("ai", "LR"), ("nre", "LI"), ALU.subtract)):
        c.step(tt(s[out], s[a], s[b], ALU.mult))
        c(tt(s["t"], s[d], s[e], ALU.mult))
        c(tt(s[out], s[out], s["t"], op))
        c(tt(s[out], s[out], s["rden"], ALU.mult))


def pool_s5_inputs(m, c, pool):
    s = m.small
    pool.wait_ge(*m.past("b_in", 16))
    z = [s[n][:].unsqueeze(2).to_broadcast([P, NG, SC]) for n in ("zr", "zi")]
    re, im = m.Bri[:, 0], m.Bri[:, 1]
    for out, a, b, op in ((m.BB1, re, im, ALU.subtract), (m.BB2, im, re, ALU.add)):
        c.step(pool.tensor_tensor(out[:], a, z[0], ALU.mult))
        c(pool.tensor_tensor(m.btmp[:], b, z[1], ALU.mult))
        c(pool.tensor_tensor(out[:], out[:], m.btmp[:], op))


def pool_s5_powers(m, c, pool):
    powers(c, pool, m.AR, m.AI, (m.small["ar"][:], m.small["ai"][:]), m.atmp, m.atmp2, T + 1)
    pool.memset(m.zero1[:], 0.0).then_inc(m.sem("powers"), 1)


def s5_power_tables(m):
    up, dn = slice(0, 64), slice(64, 128)
    rev = slice(T - 1, None, -1)
    parts = []
    for out, top, sign_t, bottom, sign_b, ks in (
            (m.F1, m.AR, 1.0, m.AI, -1.0, slice(0, T + 1)), (m.F2, m.AI, -1.0, m.AR, -1.0, slice(0, T + 1)),
            (m.G1, m.AR, 1.0, m.AI, 1.0, rev), (m.G2, m.AI, -1.0, m.AR, 1.0, rev)):
        parts += [(out[up, :, :], top[up, :, ks], sign_t), (out[dn, :, :], bottom[dn, :, ks], sign_b)]
    return parts


def pool_s5_phases(m, c, pool):
    t = [m.ctmp1[:, :, i] for i in range(6)]
    cr, ci, mg = m.cosT[:], m.sinT[:], m.magT[:]
    n = 1
    while n < T:
        c.step(pool.tensor_tensor(t[0], cr, cr, ALU.mult))
        c.step(pool.tensor_tensor(t[1], ci, ci, ALU.mult))
        c.step(pool.tensor_tensor(t[2], cr, ci, ALU.mult))
        c.step(pool.tensor_tensor(t[3], mg, mg, ALU.mult))
        c.wait()
        c.step(pool.tensor_tensor(cr, t[0], t[1], ALU.subtract))
        c.step(pool.tensor_scalar(ci, t[2], 2.0, None, ALU.mult))
        c.step(pool.tensor_copy(mg, t[3]))
        c.wait()
        n *= 2
    powers(c, pool, m.CT, m.ST, (cr, ci), m.ctmp1, m.ctmp2, NCH)
    c(pool.tensor_scalar(m.ST[64:128, :, :], m.ST[64:128, :, :], -1.0, None, ALU.mult))
    c.step(pool.memset(m.D0[:, :, 0:1], 0.0))
    c.step(pool.tensor_copy(m.D0[:, :, 1:NCH], mg.unsqueeze(2).to_broadcast([P, NG, NCH - 1])))
    c.wait()
    pool.memset(m.zero1[:], 0.0).then_inc(m.sem("phases"), 1)


N1, N2, MIXPRE, FFNPRE, GLUB, DWB, LNG, LNB, SKIP = 0, 8, 16, 32, 48, 56, 60, 64, 68


def units_done(h):
    done = lambda h: 6 + 3 * h // 4 if h <= 8 else 12 + (h - 8) // 2
    return range(done(h), done(h + 1))


def build(nc, io, out):
    with ExitStack() as ctx:
        m = Program(nc, ctx, io)
        sem, ps, first = m.sem, m.ps, m.first
        nmax, rsum, rinv = m.nmax, m.rsum, m.rinv
        block = ctx.enter_context(nc.Block())
        X_IN = io["x"][0]

        @block.sync
        def _(sp):
            for r in range(RT):
                sp.dma_start(m.x[:, r, :], X_IN[r * P:(r + 1) * P, :]).then_inc(sem(f"x_in{r}"), 16)

            def ffn(st, wg, wu):
                n = first[st + ".up"]

                def pair(n0, c, it):
                    for i, w in enumerate((wg, wu)):
                        v = w[:, bass.ds(c, 256)] if it is not None else w[:, c:c + 256]
                        m.load_unit(sp, n0 + i, v.rearrange("(k p) c -> p k c", p=P), 0 if it is None else it)

                pair(n, 0, None)
                with sp.Fori(0, (FP - 1) // 2) as it:
                    for j in range(2):
                        pair(n + 2 + 2 * j, 256 * (1 + j) + 512 * it, it)
                return n + 2 * FP

            n = 0
            starts = {first["f1.up"]: ("f1", io["w_gate"][0], io["w_up"][0]),
                      first["f2.up"]: ("f2", io["ffn_w_gate_2"][0], io["ffn_w_up_2"][0]),
                      first["f3.up"]: ("f3", io["ffn_w_gate_2"][1], io["ffn_w_up_2"][1])}
            while n < len(m.units):
                if n in starts:
                    n = ffn(*starts[n])
                else:
                    if n == first["o3"] + 1:
                        sp.wait_ge(*m.past("v_done", 4))
                        for t in range(T):
                            sp.dma_start(m.TTab[SC * t:SC * t + SC].rearrange("c (b i) w -> c b i w", i=GB),
                                         m.Kd.rearrange("(i h c) b w -> h c b i w", i=GB, h=2)[
                                             1, :, :, :, P - SC * t:2 * P - SC * t]).then_inc(sem("t_in"), 16)
                    m.load_unit(sp, n, m.units[n][0])
                    n += 1
            for r in range(RT):
                sp.wait_ge(*m.past("pf1_x_ready", r + 1))
                sp.dma_start(out[0, r * P:(r + 1) * P, :], m.x[:, r, :]).then_inc(sem("stored"), 16)
            sp.wait_ge(*m.past("stored", 16 * RT))

        @block.gpsimd
        def _(pool):
            c = pool_constants(m, pool)
            m.pool_rstd(pool, "n1", D, "n1_squares")
            pool.wait_ge(*m.past("qk_in", 16 * 2))
            for i in (0, 2):
                c(pool.tensor_scalar(m.qkg[:, i, :], m.qkg[:, i, :], HD ** -0.5, None, ALU.mult))
            for i in range(2):
                for r in range(RT):
                    g = m.qkg[:, i, :]
                    c.step(pool.tensor_tensor(m.ropeg[:, i, r, 0, :], m.rope[:, r, 0, :], g, ALU.mult))
                    for h in range(2):
                        a, b = slice(32 * h, 32 * h + 32), slice(32 - 32 * h, 64 - 32 * h)
                        last = pool.tensor_tensor(m.ropeg[:, i, r, 1, a], m.rope[:, r, 1, a], m.qkg[:, i, b],
                                                  ALU.mult)
                        if (i, r, h) == (1, RT - 1, 1):
                            last.then_inc(sem("rope_ready"), 1)
                        else:
                            c.step(last)
            pool_s5_scalars(m, c, pool)
            pool.wait_ge(*m.past("vectors_in", 16))
            pool.wait_ge(*m.past("glu", 3))

            def conv(k0, k1):
                acc = m.cacc[:, 2, :]
                for k in range(k0, k1):
                    w = m.taps[:, 4 * k + 2:4 * k + 3].to_broadcast([P, TOK])
                    src, out = m.hpad[:, 2, k:k + TOK], acc if k == 0 else m.ctmp[:]
                    c(pool.tensor_tensor(out, src, w, ALU.mult))
                    if k == 0:
                        c(pool.tensor_tensor(acc, acc, m.vec[:, DWB + 2:DWB + 3].to_broadcast([P, TOK]), ALU.add))
                    elif k < TAPS - 1:
                        c(pool.tensor_tensor(acc, acc, m.ctmp[:], ALU.add))
                    else:
                        pool.tensor_tensor(acc, acc, m.ctmp[:], ALU.add).then_inc(sem("conv_pool"), 1)

            conv(0, 5)
            m.pool_rstd(pool, "q", HD, "q_head_sums", 16)
            conv(5, 7)
            m.pool_rstd(pool, "k", HD, "k_head_sums", 16)
            conv(7, TAPS)
            pool_s5_growth(m, c, pool)
            m.pool_rstd(pool, "ln", AW, "ln_head_sums", 2)
            pool_s5_powers(m, c, pool)
            pool_s5_inputs(m, c, pool)
            m.pool_rstd(pool, "f1", D, "f1_squares")
            pool.wait_ge(*m.past("c_in", 16))
            pool.wait_ge(*m.past("tables_a", 4))
            pool.wait_ge(*m.past("tables_d", 4))
            for b in range(2):
                pool.memset(m.ksb[:, b, 0:P], 0.0).then_inc(sem(f"prep_stored{b}"), 1)
            m.pool_prep(pool, 0)
            with pool.Fori(0, (FP - 1) // 2) as it:
                for j in range(2):
                    m.pool_prep(pool, 1 + j, it, 2)
            for b in range(FP, NBLK):
                m.pool_prep(pool, b)
            m.pool_rstd(pool, "fp", D, "fp_squares")
            for r in range(RT):
                c.step(pool.memset(m.qa[:, r, :, HD:HD + 1], 1.0))
                c.step(pool.memset(m.ka[:, r, :, HD + 1:HD + 2], 1.0))
            for i, (t, g) in enumerate(((m.ka, 3), (m.qa, 2), (m.ka, 3), (m.qa, 2))):
                m.pool_rstd(pool, f"blk{i}", HD, f"blk{i}_head_sums", 16)
                for r in range(RT):
                    pool.wait_ge(*m.past("head_normed", 2 * i + r + 1))
                    v = t[:, r, 8 * (i // 2):8 * (i // 2) + 8, 0:HD]
                    pool.tensor_tensor(v, v, m.qkg[:, g:g + 1, :].to_broadcast([P, 8, HD]), ALU.mult)\
                        .then_inc(sem("gained"), 1)
            m.pool_rstd(pool, "pm0", D, "pm0_squares")
            m.pool_rstd(pool, "f2", D, "f2_squares")
            pool_s5_phases(m, c, pool)
            m.pool_rstd(pool, "pf0", D, "pf0_squares")
            m.pool_rstd(pool, "s", D, "s_squares")
            for j in range(4):
                pool.wait_ge(*m.past("vs_done", j + 1))
                g = slice(16 * j, 16 * j + 16)
                pool.tensor_tensor(m.V[:, g, :], m.V[:, g, :], m.CT[:, g, :], ALU.mult).then_inc(sem("vc"), 1)
            for j in range(4):
                pool.wait_ge(*m.past("zs_done", j + 1))
                g = slice(16 * j, 16 * j + 16)
                pool.tensor_tensor(m.W[:, g, :], m.W[:, g, :], m.CT[:, g, :], ALU.mult).then_inc(sem("zc"), 1)
            m.pool_rstd(pool, "pm1", D, "pm1_squares")
            m.pool_rstd(pool, "f3", D, "f3_squares")
            m.pool_rstd(pool, "pf1", D, "pf1_squares")

        @block.tensor
        def _(pe):
            idn = m.ident
            pe.wait_ge(*m.past("consts", 1))
            m.keep_warm(pe, 7, 8)
            m.pe_turn(pe, "n1", (4, 5, 6, 7, 2, 3))
            for i in range(4):
                m.mm_features(pe, first["u"] + i, i, ready="n1_act_ready" if i == 0 else None)
            for name, banks in (("q", (4, 5)), ("k", (6, 7)), ("v", (0, 1))):
                if name == "v":
                    pe.wait_ge(*m.past("glu", 4))
                for h in range(2):
                    m.mm_half_k(pe, first[name] + h, banks, h)
            m.pe_heads(pe, "a1", m.qn[:].rearrange("p r (h d) -> p r h d", d=HD), (0, H1), "q_ready", 2, (2, 3), 0)
            m.keep_warm(pe, 4, 16)
            m.pe_heads(pe, "a1", m.kn[:].rearrange("p r (h d) -> p r h d", d=HD), (0, H1), "k_ready", 2, (2, 3),
                       H1 // 2)
            pe.wait_ge(*m.past("a1_heads_out", H1))
            pe.wait_ge(*m.past("v_out", 2))

            def conv_and_norm(i):
                h, part = divmod(i, 3)
                if h < 4:
                    for k in range(TAPG * h + 3 * part, min(TAPG * h + 3 * part + 3, TAPG * h + TAPG, TAPS)):
                        if k % TAPG == 0:
                            pe.wait_ge(*m.past("dtaps_ready", h + 1))
                        last = pe.matmul(ps[:, 2, 0:TOK], m.dtaps[:, k % (2 * TAPG), :], m.hpad[:, 3, k:k + TOK],
                                         start=(k == 0), stop=(k == TAPS - 1))
                    if part == 2:
                        last.then_inc(sem("conv_tensor"), 1)
                elif (h, part) == (6, 0):
                    pe.wait_ge(*m.past("conv_done", 1))
                    pe.wait_ge(*m.past("conv_pool", 1))
                    for j in range(4):
                        last = pe.matmul(ps[:, 3, 0:TOK], m.ones[:], m.cacc[:, j, :], start=(j == 0), stop=(j == 3))
                    last.then_inc(sem("ln_sum"), 1)
                elif (h, part) == (7, 0):
                    pe.wait_ge(*m.past("ln_sq", 1))
                    for r in range(RT):
                        for j in range(4):
                            last = pe.matmul(ps[:, 3, r:r + 1], m.csq[:, j, r * P:(r + 1) * P], m.ones[:, 0:1],
                                             start=(j == 0), stop=(j == 3))
                    last.then_inc(sem("ln_second"), 1)

            m.pe_attention(pe, "a1", (0, H1), m.qt, m.kt1, m.vn, m.p1, m.pt1, (4, 5), (6, 7),
                           lambda r, h: ps[:, r, h * HD:(h + 1) * HD], conv_and_norm)
            m.keep_warm(pe, 6, 7)
            m.pe_turn(pe, "ao", (0, 1, 2), n=4, scaled=False)
            n = first["o1"]
            ao = (("ao_act_ready", 1),)
            m.mm_k_pair(pe, n, 4, m.actH, m.actL, 0, KT, ao)
            pe.wait_ge(*m.past("ln_diag", 2))
            pe.matmul(ps[:, 3, 0:TOK], m.ones[:], m.diag[:], start=True, stop=True).then_inc(sem("ln_spread"), 1)
            m.mm_k_pair(pe, n + 1, 4, m.actH, m.actL, 2, KT, (("ao_act_ready", 3),))
            m.mm_k_pair(pe, n + 2, 4, m.actH, m.actL, 4, KT, (("conv_low", 1),))
            m.mm_k_pair(pe, n + 3, 4, m.actH, m.actL, 6, KT, (("conv_low", 3),), first="o1_first")
            m.keep_warm(pe, 3, 8)
            m.pe_turn(pe, "f1", (0, 1, 2, 3, 6, 7))
            m.pe_ffn(pe, "f1", 4, prep=True)
            m.keep_warm(pe, 4)
            m.pe_turn(pe, "fp", (0, 1, 2, 3, 4, 5))
            n = first["fox"]
            m.mm_half_k(pe, n, (6, 7), 0, "fp_act_ready")
            pe.wait_ge(*m.past("wf_split", 1))
            for k in range(KT):
                pe.wait_ge(*m.past("fp_act_ready", k + 1))
                o = ps[0:H2, 3, 0:TOK]
                pe.matmul(o, m.wfH[:, k, :], m.actH[:, k, :], start=(k == 0), stop=False)
                pe.matmul(o, m.wfL[:, k, :], m.actH[:, k, :], start=False, stop=False)
                last = pe.matmul(o, m.wfH[:, k, :], m.actL[:, k, :], start=False, stop=(k == KT - 1))
            last.then_inc(sem("f_done"), 1)
            for k in range(4):
                m.mm_quarter(pe, n + 1, (6, 7), 1, k)
                if k == 1:
                    pe.wait_ge(*m.past("f_out", 1))
                    for r in range(RT):
                        last = pe.transpose(ps[:, 0, H2 * r:H2 * r + H2], m.fT[:, r * P:(r + 1) * P],
                                            idn[0:H2, 0:H2])
                    last.then_inc(sem("f_turned"), 1)
            for i, banks in ((1, (4, 5)), (2, (6, 7))):
                if i == 2:
                    pe.wait_ge(*m.past("fox_out", 2))
                for h in range(2):
                    m.mm_half_k(pe, n + 2 * i + h, banks, h)
                if i == 1:
                    pe.wait_ge(*m.past("logf", 1))
                    lf = m.fl[:, 1]
                    pe.matmul(ps[:, 1, 0:H2], m.tri[:], lf[:, 0, :], start=True, stop=True)
                    pe.matmul(ps[:, 1, H2:2 * H2], m.ones[:], lf[:, 0, :], start=True, stop=False)
                    pe.matmul(ps[:, 1, H2:2 * H2], m.tri[:], lf[:, 1, :], start=False, stop=True)\
                      .then_inc(sem("csum"), 1)
            pe.wait_ge(*m.past("c_cols", 4))
            m.pe_heads(pe, "a2", m.ka, (0, 8), "gained", 2, (2, 3), 0)
            m.pe_heads(pe, "a2", m.qa, (0, 8), "gained", 4, (2, 3), 4)
            pe.wait_ge(*m.past("a2_heads_out", 8))
            pe.wait_ge(*m.past("fox_out", 6))

            def others_a(i):
                if i in (8, 16):
                    pe.wait_ge(*m.past("fox_out", 6 + i // 4))
                m.mm_quarter(pe, n + 6 + i // 4, (6, 7), i // 4 % 2, i % 4)

            m.pe_attention(pe, "a2", (0, 8), m.qt2, m.kt2, m.va, m.p2, m.pt2, (0, 1), (2, 3),
                           lambda r, h: ps[:, 4 + r, h * HD:(h + 1) * HD], others_a)
            pe.wait_ge(*m.past("a2_pt", 8))
            m.pe_heads(pe, "a2", m.ka, (8, 16), "gained", 6, (2, 3), 8)
            m.pe_heads(pe, "a2", m.qa, (8, 16), "gained", 8, (2, 3), 12)
            pe.wait_ge(*m.past("a2_heads_out", 16))
            pe.wait_ge(*m.past("fox_out", 12))

            def others_b(i):
                i -= 24
                if i % 3 == 2:
                    return
                i = i // 3 * 2 + i % 3
                if i == 0:
                    pe.wait_ge(*m.past("half_out", 2))
                if i == 8:
                    pe.wait_ge(*m.past("fox_out", 14))
                m.mm_quarter(pe, n + 12 + i // 4, (4, 5), i // 4 % 2, i % 4)

            m.pe_attention(pe, "a2", (8, 16), m.qt2, m.kt2, m.va, m.p2, m.pt2, (0, 1), (2, 3),
                           lambda r, h: ps[:, 6 + r, (h - 8) * HD:(h - 7) * HD], others_b)
            m.keep_warm(pe, 2, 12)
            m.pe_turn(pe, "fo", (0, 1, 2, 3), scaled=False)
            for i in range(4):
                m.mm_k_pair(pe, first["o2"] + i, 4, m.actH, m.actL, 2 * i, KT,
                            (("fo_act_ready", 2 * i + 1),), first="o2_first" if i == 3 else None)
            m.keep_warm(pe, 3)
            m.pe_turn(pe, "f2", (0, 1, 2, 3, 6, 7))
            m.pe_ffn(pe, "f2", 4)
            m.keep_warm(pe, 7)
            m.pe_turn(pe, "s", (4, 5, 6, 7, 2, 3))
            for i in range(4):
                m.mm_features(pe, first["s"] + i, i, ready="s_act_ready" if i == 0 else None)
            pe.wait_ge(*m.past("ut_a", 2))
            pe.wait_ge(*m.past("ut_d", 2))
            for h in range(2):
                for t in range(T):
                    i = T * h + t
                    last = pe.transpose(ps[:, 4 + i // 4, (i % 4) * P:(i % 4 + 1) * P],
                                        m.uT[:, h, t, :, :].rearrange("p j c -> p (j c)"), idn[:])
                    if i % 4 == 3:
                        last.then_inc(sem("u_chunked"), 1)
            for q in range(16):
                if q % 8 == 0:
                    pe.wait_ge(*m.past("ur_a", q // 8 + 1))
                    pe.wait_ge(*m.past("ur_d", q // 8 + 1))
                last = pe.transpose(ps[:, q // 4, (q % 4) * P:(q % 4 + 1) * P],
                                    m.Ur[:, q, :, :].rearrange("p t c -> p (t c)"), idn[:])
                if q % 4 == 3:
                    last.then_inc(sem("u_turned"), 1)
            pe.wait_ge(*m.past("u_out_a", 2))
            pe.wait_ge(*m.past("u_out_d", 2))
            pe.wait_ge(*m.past("r_in", 16))
            for q in range(16):
                for j in range(4):
                    last = pe.matmul(ps[32 * j:32 * j + 32, 4 + q // 4, (q % 4) * P:(q % 4 + 1) * P],
                                     m.Uall[:, q, j, :], m.RTab[:, 16 * j + q, :], start=True, stop=True)
                if q % 4 == 3:
                    last.then_inc(sem("v_done"), 1)
            for q in range(16):
                if q % 4 == 0:
                    pe.wait_ge(*m.past("vc_a" if q % 8 == 0 else "vc_d", q // 8 + 1))
                last = pe.transpose(ps[:, q // 4, (q % 4) * P:(q % 4 + 1) * P], m.Vc[:, q, :], idn[:])
                if q % 4 == 3:
                    last.then_inc(sem("v_turned"), 1)

            def swap(j, src, bank, ready, value, done):
                pe.wait_ge(*m.past(ready, value))
                pe.matmul(ps[:, bank, :], m.swap[:],
                          src[:, 16 * j:16 * j + 16, :].rearrange("p g c -> p (g c)"), start=True, stop=True)\
                  .then_inc(sem(done), 1)

            pe.wait_ge(*m.past("vo_a", 2))
            for j in range(4):
                swap(j, m.V, 4 + j, "vo_d", 2, "vs_done")
            for j in range(4):
                swap(j, m.W, j, "scanned", j + 1, "zs_done")
            m.keep_warm(pe, 7, 12)
            pe.wait_ge(*m.past("t_in", 16 * T))
            pe.wait_ge(*m.past("o_in", 16))
            pe.wait_ge(*m.past("states", 4))
            for q in range(16):
                for j in range(4):
                    o = ps[32 * j:32 * j + 32, q // 4, (q % 4) * P:(q % 4 + 1) * P]
                    pe.matmul(o, m.Uall[:, q, j, :], m.TTab[:, 16 * j + q, :], start=True, stop=False)
                    last = pe.matmul(o, m.X33[:, 16 * j + q, 0:NCH], m.OTab[:, 16 * j + q, :], start=False, stop=True)
                if q % 4 == 3:
                    last.then_inc(sem("y_done"), 1)
            for h in range(2):
                pe.wait_ge(*m.past("y_out_a", h + 1))
                pe.wait_ge(*m.past("y_out_d", h + 1))
                for t in range(T):
                    i = T * h + t
                    last = pe.transpose(ps[:, 4 + i // 4, (i % 4) * P:(i % 4 + 1) * P],
                                        m.Ysb[:, t, 8 * h:8 * h + 8, :].rearrange("p q c -> p (q c)"), idn[:])
                last.then_inc(sem("y_turned"), 1)
            for i in range(4):
                m.mm_features(pe, first["glu"] + i, i, ready="yg_act_ready" if i == 0 else None,
                              order=Y_ORDER)
            for i in range(4):
                m.mm_k_pair(pe, first["o3"] + i, 4, m.yoH, m.yoL, 2 * i, KT, (("yo_low", i + 1),), step=0,
                            first="o3_first" if i == 3 else None)
            m.keep_warm(pe, 3)
            m.pe_turn(pe, "f3", (0, 1, 2, 3, 6, 7))
            m.pe_ffn(pe, "f3", 4)

        @block.scalar
        def _(act):
            s5 = {k: v[:] for k, v in m.small.items()}
            for t, name in ((m.vectors, "vectors"), (m.lamdt, "lamdt")):
                act.dma_start(t[:], io[name]).then_inc(sem(name + "_in"), 16)
            for r in range(RT):
                m.act_squares(act, "n1", m.x[:, r, :], r, *m.past(f"x_in{r}", 16))
            m.split_high(act, 0)
            act.wait_ge(*m.past("vectors_in", 16))
            m.act_turn(act, "n1", (4, 5, 6, 7, 2, 3), gain=N1)
            m.split_high(act, 1)
            act.dma_start(m.qkg[:].rearrange("p a d -> p (a d)"), io["head_gains"].to_broadcast([P, 4 * HD]))\
               .then_inc(sem("qk_in"), 16)
            act.dma_start(m.rope[:], io["rope"]).then_inc(sem("qk_in"), 16)
            act.dma_start(m.Bri[:], io["s5_b"]).then_inc(sem("b_in"), 16)
            act.dma_start(m.C12[:], io["s5_c"]).then_inc(sem("c_in"), 16)
            act.wait_ge(*m.past("lamdt_in", 16))
            act.activation(s5["dt"], s5["ldt"], ACT.Exp).then_inc(sem("dt"), 1)
            m.split_high(act, 2)
            m.split_high(act, 3)
            m.split_high(act, 4)
            for j in range(4):
                act.wait_ge(m.used, first["u"] + 3 + j // 2)
                act.activation(m.csig[:, j, :], ps[:, 2 + j // 2, (j % 2) * TOK:(j % 2 + 1) * TOK], ACT.Sigmoid,
                               bias=m.vec[:, GLUB + 4 + j:GLUB + 5 + j]).then_inc(sem("sig"), 1)
            m.split_high(act, 5)
            m.split_high(act, 6)
            m.split_high(act, 7)

            def head_squares(st, banks, unit, sq):
                act.wait_ge(m.used, unit)
                for r in range(RT):
                    act.activation(sq[:, r, :], ps[:, banks[r], :], ACT.Square).then_inc(sem(st + "_sq"), 1)

            act.wait_ge(*m.past("glu", 4))
            head_squares("q", (4, 5), first["q"] + 2, m.sq1)
            f5 = sem("s5_functions")
            act.wait_ge(*m.past("angle", 1))
            act.activation(m.sinT[:], s5["thr"], ACT.Sin).then_inc(f5, 1)
            act.activation(s5["sh"], s5["thr"], ACT.Sin, scale=0.5).then_inc(f5, 1)
            act.wait_ge(*m.past("abs_angle", 1))
            act.activation(m.cosT[:], s5["ab"], ACT.Sin, scale=-1.0, bias=m.halfpi[:]).then_inc(f5, 1)
            act.activation(s5["tt"], s5["lrc"], ACT.Tanh, scale=0.5).then_inc(f5, 1)
            act.activation(s5["eb"], s5["lrb"], ACT.Exp).then_inc(f5, 1)
            m.split_high(act, 8)

            def tap_diagonals(g):
                ks = range(TAPG * g, min(TAPG * g + TAPG, TAPS))
                for k in ks:
                    i = act.activation(m.dtaps[:, k % (2 * TAPG), :], m.ident[:], ACT.Copy,
                                       scale=m.taps[:, 4 * k + 3:4 * k + 4])
                i.then_inc(sem("dtaps_ready"), 1)

            act.wait_ge(*m.past("n1_transposed", KT))
            tap_diagonals(0)
            m.split_high(act, 9)
            act.wait_ge(*m.past("q_head_sums", 1))
            head_squares("k", (6, 7), first["k"] + 2, m.sq1)
            m.split_high(act, 10)
            m.split_high(act, 11)
            m.act_heads(act, "a1", m.qt, (0, H1), (2, 3), 0)
            for r in range(RT):
                act.wait_ge(m.used, first["v"] + 2)
                act.activation(m.vn[:, r, :], ps[:, r, :], ACT.Copy).then_inc(sem("v_out"), 1)
            m.act_heads(act, "a1", m.kt1, (0, H1), (2, 3), H1 // 2)
            tap_diagonals(1)
            for h in range(H1):
                m.act_attention(act, "a1", h, m.p1, rsum, nmax, (4, 5))
                if h < 2:
                    act.wait_ge(*m.past("conv_tensor", h + 1))
                    tap_diagonals(2 + h)
                if h == 5:
                    act.wait_ge(*m.past("ln_centred", 1))
                    act.activation(m.csq[:], m.cacc[:], ACT.Square).then_inc(sem("ln_sq"), 1)
            m.act_turn(act, "ao", (0, 1, 2), n=4)
            act.wait_ge(*m.past("powers", 1))
            for out, src, sign in s5_power_tables(m)[:4]:
                act.activation(out, src, ACT.Copy, scale=sign).then_inc(sem("tables_a"), 1)
            m.split_high(act, 12)
            act.wait_ge(*m.past("ln_second", 1))
            act.wait_ge(*m.past("ln_normed", 1))

            def cv_high(j):
                act.wait_ge(*m.past("cv_silu", j + 1))
                act.activation(m.actH[:, 4 + j, :], m.csq[:, j, :], ACT.Copy).then_inc(sem("cv_high"), 1)

            for j in range(4):
                act.activation(m.csq[:, j, :], m.cacc[:, j, :], ACT.Silu, scale=m.vec[:, LNG + j:LNG + j + 1],
                               bias=m.vec[:, LNB + j:LNB + j + 1]).then_inc(sem("cv_silu"), 1)
                if j > 0:
                    cv_high(j - 1)
            cv_high(3)
            m.split_high(act, 13)
            m.split_high(act, 14)
            for r in range(RT):
                m.act_squares(act, "f1", m.x[:, r, :], r, *m.past("f1_x_ready", r + 1))
            m.act_turn(act, "f1", (0, 1, 2, 3, 6, 7), gain=N2)
            m.split_high(act, 15)
            m.act_ffn(act, "f1", 4, prep=True)
            for r in range(RT):
                m.act_squares(act, "fp", m.x[:, r, :], r, *m.past("fp_x_ready", r + 1))
            for i in range(2):
                act.wait_ge(*m.past(f"prep_stored{i}", 48 * (NBLK // 2) + 1))
            act.dma_start(m.wf[:], io["fox_w_in_2"][0][:, 4 * D:4 * D + H2].rearrange("(k p) c -> p k c", p=P))\
               .then_inc(sem("wf_in"), 16)
            act.dma_start(m.fb[:], io["fox_b_f_2"].to_broadcast([P, H2])).then_inc(sem("fb_in"), 16)
            act.dma_start(m.gb[0][:], io["mix_post_gain_2"][0:1, :].to_broadcast([P, D])).then_inc(sem("gain0_in"), 16)
            act.dma_start(m.gb[1][:], io["ffn_post_gain_2"][0:1, :].to_broadcast([P, D])).then_inc(sem("gain1_in"), 16)
            m.act_turn(act, "fp", (0, 1, 2, 3, 4, 5), gain=MIXPRE)
            act.wait_ge(*m.past("wf_in", 16))
            act.activation(m.wfH[:], m.wf[:], ACT.Copy).then_inc(sem("wf_high"), 1)
            m.split_high(act, first["fox"] + 1)
            m.split_high(act, first["fox"] + 2)
            act.wait_ge(*m.past("f_abs", 1))
            act.activation(m.fl[:, 2], m.fl[:, 1], ACT.Exp, scale=-1.0).then_inc(sem("f_exp"), 1)
            act.wait_ge(*m.past("f_exp", 1))
            act.activation(m.fl[:, 3], m.fl[:, 2], ACT.Ln, bias=1.0).then_inc(sem("f_ln"), 1)
            n = first["fox"]

            def block_out(i, banks):
                act.wait_ge(m.used, n + 2 * i + 2)
                half = i // 3 if i < 6 else i - 6
                for r in range(RT):
                    b = ps[:, banks[r], :]
                    if i < 6 and i % 3 < 2:
                        t = (m.ka, m.qa)[i % 3]
                        act.activation(t[:, r, 8 * half:8 * half + 8, 0:HD], b.rearrange("p (h d) -> p h d", d=HD),
                                       ACT.Copy).then_inc(sem("fox_out"), 1)
                    else:
                        f, dst = (ACT.Copy, m.va) if i < 6 else (ACT.Sigmoid, m.ga)
                        act.activation(dst[:, r, 512 * half:512 * half + 512], b, f).then_inc(sem("fox_out"), 1)

            def block_squares(i):
                if i < 6 and i % 3 < 2:
                    half, t = i // 3, (m.ka, m.qa)[i % 3]
                    blk = i if i < 2 else i - 1
                    if blk > 0:
                        act.wait_ge(*m.past(f"blk{blk - 1}_head_sums", 1))
                    for r in range(RT):
                        act.wait_ge(*m.past("fox_out", 2 * i + r + 1))
                        act.activation(m.sq2[:, r, :].rearrange("p (h d) -> p h d", d=HD),
                                       t[:, r, 8 * half:8 * half + 8, 0:HD], ACT.Square)\
                           .then_inc(sem(f"blk{blk}_sq"), 1)

            for i in range(3):
                if i > 0:
                    m.split_high(act, n + 2 * i + 2)
                block_out(i, (4, 5) if i == 1 else (6, 7))
                m.split_high(act, n + 2 * i + 3)
                block_squares(i)
            m.act_heads(act, "a2", m.kt2, (0, 8), (2, 3), 0)
            m.act_heads(act, "a2", m.qt2, (0, 8), (2, 3), 4)
            for h in range(16):
                m.act_attention(act, "a2", h, m.p2, rsum, nmax, (0, 1))
                for j in units_done(h):
                    if j % 2 == 1:
                        block_out(j // 2, (6, 7) if h < 8 else (4, 5))
                        block_squares(j // 2)
                    m.split_high(act, n + j + 2)
                if h == 7:
                    m.act_heads(act, "a2", m.kt2, (8, 16), (2, 3), 8)
                    m.act_heads(act, "a2", m.qt2, (8, 16), (2, 3), 12)
            m.act_turn(act, "fo", (0, 1, 2, 3))
            n = first["o2"]
            for i in range(3):
                m.split_high(act, n + 2 + i)
            m.act_norms(act, "pm0", "f2", 4, "o2_first", n + 4)
            act.dma_start(m.gb[0][:], io["mix_post_gain_2"][1:2, :].to_broadcast([P, D])).then_inc(sem("gain0_in"), 16)
            m.act_turn(act, "f2", (0, 1, 2, 3, 6, 7), gain=FFNPRE)
            m.split_high(act, n + 5)
            m.act_ffn(act, "f2", 4)
            n = first["s"]
            m.act_norms(act, "pf0", "s", 0, "f2_first", n)
            act.dma_start(m.RTab[:], m.Rd).then_inc(sem("r_in"), 16)
            act.dma_start(m.OTab[:], m.Od).then_inc(sem("o_in"), 16)
            act.wait_ge(*m.past("pf0_normed", 2))
            act.dma_start(m.gb[1][:], io["ffn_post_gain_2"][1:2, :].to_broadcast([P, D])).then_inc(sem("gain1_in"), 16)
            m.act_turn(act, "s", (4, 5, 6, 7, 2, 3), gain=MIXPRE + 8)

            def yo_high(i):
                act.wait_ge(*m.past("gated", i + 1))
                act.activation(m.yoH[:, 2 * i:2 * i + 2, :], m.yoT[:, 2 * i:2 * i + 2, :], ACT.Copy)\
                   .then_inc(sem("yo_high"), 1)

            m.split_high(act, n + 1)
            for i in range(4):
                if i % 2 == 0:
                    act.wait_ge(m.used, n + i + 1)
                    act.activation(m.uT[:, :, :, i, :], ps[:, i, :].rearrange("p (h c t) -> p h t c", h=2, t=T),
                                   ACT.Copy).then_inc(sem("ut_a"), 1)
                if i < 3:
                    m.split_high(act, n + 2 + i)
            for h in range(2):
                act.wait_ge(*m.past("u_chunked", 2 * h + 1))
                act.activation(m.Ur[:, 8 * h:8 * h + 8, 0:4, :].rearrange("p q t c -> p t q c"),
                               ps[:, 4 + 2 * h, :].rearrange("p (t q c) -> p t q c", t=4, q=8), ACT.Copy)\
                   .then_inc(sem("ur_a"), 1)
            for b in range(2):
                act.wait_ge(*m.past("u_turned", b + 1))
                act.activation(m.Uall[:, 4 * b:4 * b + 4, :, :],
                               ps[:, b, :].rearrange("p (q j c) -> p q j c", q=4, j=4), ACT.Copy)\
                   .then_inc(sem("u_out_a"), 1)
            for b in (0, 2):
                act.wait_ge(*m.past("v_done", b + 1))
                act.activation(m.Vc[:, 4 * b:4 * b + 4, :], ps[:, 4 + b, :].rearrange("p (q s) -> p q s", q=4),
                               ACT.Copy).then_inc(sem("vc_a"), 1)
            for b in (0, 2):
                act.wait_ge(*m.past("v_turned", b + 1))
                act.activation(m.V[:].rearrange("p (j q) c -> p q j c", j=4)[:, 4 * b:4 * b + 4],
                               ps[:, b, :].rearrange("p (q j c) -> p q j c", q=4, j=4), ACT.Copy)\
                   .then_inc(sem("vo_a"), 1)
            m.split_high(act, n + 5)
            for b in (0, 2):
                act.wait_ge(*m.past("y_done", b + 1))
                act.activation(m.Ysb[:, :, 4 * b:4 * b + 4, :].rearrange("p t q c -> p q t c"),
                               ps[:, b, :].rearrange("p (q t c) -> p q t c", q=4, t=T), ACT.Copy)\
                   .then_inc(sem("y_out_a"), 1)
            for i, kt in enumerate(Y_ORDER + (None,)):
                if kt is not None:
                    act.wait_ge(*m.past("y_sum", i + 1))
                    act.activation(m.ygT[:, kt, :], m.ygT[:, kt, :], ACT.Gelu_apprx_tanh).then_inc(sem("gelu"), 1)
                if i > 0:
                    act.wait_ge(*m.past("gelu", i))
                    act.activation(m.actH[:, Y_ORDER[i - 1], :], m.ygT[:, Y_ORDER[i - 1], :], ACT.Copy)\
                       .then_inc(sem("yg_high_ready"), 1)
            n = first["glu"]
            for i in range(4):
                act.wait_ge(m.used, n + i + 1)
                act.activation(m.sgT[:, 2 * i:2 * i + 2, :], ps[:, i, :].rearrange("p (k t) -> p k t", k=2), ACT.Sigmoid)\
                   .then_inc(sem("glu_sig"), 1)
                m.split_high(act, n + 2 + i)
                if i > 0:
                    yo_high(i - 1)
            yo_high(3)
            n = first["o3"]
            for i in range(1, 4):
                m.split_high(act, n + 1 + i)
            m.act_norms(act, "pm1", "f3", 4, "o3_first", n + 4)
            m.act_turn(act, "f3", (0, 1, 2, 3, 6, 7), gain=FFNPRE + 8)
            m.split_high(act, n + 5)
            m.act_ffn(act, "f3", 4)
            m.act_norms(act, "pf1", None, 0, "f3_first", len(m.units))

        @block.vector
        def _(dve):
            c = Chain(dve, sem("dve_chain"))
            s5 = {k: v[:] for k, v in m.small.items()}
            m.dve_scale(dve, "n1")
            m.split_low(dve, 0)
            dve.wait_ge(*m.past("vectors_in", 16))
            m.dve_turn(dve, "n1", (4, 5, 6, 7, 2, 3), gain=N1)
            for i in range(1, 5):
                m.split_low(dve, i)
            for j in range(4):
                dve.wait_ge(*m.past("sig", j + 1))
                dve.scalar_tensor_tensor(m.hpad[:, j, TAPS - 1:], ps[:, j // 2, (j % 2) * TOK:(j % 2 + 1) * TOK],
                                         m.vec[:, GLUB + j:GLUB + j + 1], m.csig[:, j, :], ALU.add, ALU.mult)\
                   .then_inc(sem("glu"), 1)
            m.split_low(dve, 5)
            dve.wait_ge(*m.past("angle", 1))
            dve.scalar_tensor_tensor(s5["ab"], s5["thr"], -1.0, s5["thr"], ALU.mult, ALU.max)\
               .then_inc(sem("abs_angle"), 1)
            taps_left = [(k, j) for k in range(TAPS) for j in range(2)]
            steps = {}

            def conv(count):
                for _ in range(min(count, len(taps_left))):
                    k, j = taps_left.pop(0)
                    w = m.taps[:, 4 * k + j:4 * k + j + 1]
                    src = m.hpad[:, j, k:k + TOK]
                    if k == 0:
                        if j == 0:
                            dve.wait_ge(*m.past("glu", 4))
                        i = dve.tensor_scalar(m.cacc[:, j, :], src, w, m.vec[:, DWB + j:DWB + j + 1], ALU.mult, ALU.add)
                    else:
                        c.wait(steps[j])
                        i = dve.scalar_tensor_tensor(m.cacc[:, j, :], src, w, m.cacc[:, j, :], ALU.mult, ALU.add)
                    steps[j] = c.step(i)

            def s5_reciprocals():
                dve.wait_ge(*m.past("s5_functions", 4))
                c(dve.tensor_scalar(s5["r2"], s5["tt"], -1.0, 1.0, ALU.mult, ALU.add))
                dve.reciprocal(s5["r1"], s5["r2"]).then_inc(sem("s5_recips"), 1)
                dve.wait_ge(*m.past("den", 1))
                dve.reciprocal(s5["rden"], s5["den"]).then_inc(sem("s5_recips"), 1)

            def head_norms(st, banks, t, ki, unit):
                dve.wait_ge(*m.past(st + "_sq", 2))
                dve.reduce_sum(m.ss[:], m.sq1[:].rearrange("p r (h d) -> p (r h) d", d=HD), AX.X)\
                   .then_inc(sem(st + "_head_sums"), 1)
                if st == "q":
                    conv(4)
                    m.split_low(dve, unit)
                else:
                    s5_reciprocals()
                    conv(6)
                dve.wait_ge(*m.past(st + "_rstd", 1))
                dve.wait_ge(*m.past("rope_ready", 1))
                hd = lambda a: a.rearrange("p (h d) -> p h d", d=HD)
                for r in range(RT):
                    rs = m.rs[:, 8 * r:8 * r + 8].unsqueeze(2).to_broadcast([P, 8, HD])
                    c(dve.tensor_tensor(hd(m.rtmp[:]), hd(ps[:, banks[r], :]), rs, ALU.mult))
                    tb = [m.ropeg[:, ki, r, i:i + 1, :].to_broadcast([P, 8, HD]) for i in range(2)]
                    c.step(dve.tensor_tensor(hd(t[:, r, :]), hd(m.rtmp[:]), tb[0], ALU.mult))
                    halves = m.rtmp[:].rearrange("p (h a d) -> p h a d", a=2, d=32)
                    for a in range(2):
                        s_ = m.ropeg[:, ki, r, 1:2, 32 * a:32 * a + 32].to_broadcast([P, 8, 32])
                        c.step(dve.tensor_tensor(hd(m.rtmp2[:])[:, :, 32 * a:32 * a + 32], halves[:, :, 1 - a, :], s_,
                                                 ALU.mult))
                    c.wait()
                    dve.tensor_tensor(t[:, r, :], t[:, r, :], m.rtmp2[:], ALU.add).then_inc(sem(st + "_ready"), 1)
                    if st == "q" and r == 0:
                        m.split_low(dve, unit + 1)
                    dve.wait_ge(*m.past(st + "_ready", r + 1))

            conv(6)
            m.split_low(dve, 6)
            conv(4)
            m.split_low(dve, 7)
            head_norms("q", (4, 5), m.qn, 0, 8)
            head_norms("k", (6, 7), m.kn, 1, 10)
            m.split_low(dve, 10)
            m.split_low(dve, 11)

            def conv_and_norm(h):
                if h < 5:
                    conv(12)
                if h == 4:
                    dve.wait_ge(*m.past("conv_tensor", 4))
                    c.wait()
                    dve.tensor_scalar(m.cacc[:, 3, :], ps[:, 2, 0:TOK], m.vec[:, DWB + 3:DWB + 4], None, ALU.add)\
                       .then_inc(sem("conv_done"), 1)
                if h == 5:
                    dve.wait_ge(*m.past("ln_sum", 1))
                    dve.scalar_tensor_tensor(m.cacc[:], ps[:, 3:4, 0:TOK].to_broadcast([P, 4, TOK]), -1.0 / AW,
                                             m.cacc[:], ALU.mult, ALU.add).then_inc(sem("ln_centred"), 1)
                if h == 7:
                    dve.wait_ge(*m.past("ln_second", 1))
                    dve.tensor_copy(m.ss[:, 0:2], ps[:, 3, 0:2]).then_inc(sem("ln_head_sums"), 1)

            m.dve_attention(dve, "a1", (0, H1), m.pt1, nmax, (4, 5), (6, 7), conv_and_norm)
            dve.wait_ge(*m.past("a1_out", H1))
            c(dve.reciprocal(rinv[:, :, 0:H1], rsum[:, :, 0:H1]))
            for r in range(RT):
                dve.tensor_tensor(m.nat[:, r, 0:AW].rearrange("p (h d) -> p h d", d=HD),
                                  ps[:, r, :].rearrange("p (h d) -> p h d", d=HD),
                                  rinv[:, r, 0:H1].unsqueeze(2).to_broadcast([P, H1, HD]), ALU.mult)\
                   .then_inc(sem("ao_nat_ready"), 1)
            m.dve_turn(dve, "ao", (0, 1, 2), n=4)
            dve.wait_ge(*m.past("ln_rstd", 1))
            for r in range(RT):
                dve.tensor_scalar(m.diag[:, r * P:(r + 1) * P], m.ident[:], m.rs[:, r:r + 1], None, ALU.mult)\
                   .then_inc(sem("ln_diag"), 1)
            dve.wait_ge(*m.past("powers", 1))
            for out, src, sign in s5_power_tables(m)[4:]:
                dve.tensor_scalar(out, src, sign, None, ALU.mult).then_inc(sem("tables_d"), 1)
            dve.wait_ge(*m.past("ln_spread", 1))
            dve.tensor_tensor(m.cacc[:], m.cacc[:], ps[:, 3:4, 0:TOK].to_broadcast([P, 4, TOK]), ALU.mult)\
               .then_inc(sem("ln_normed"), 1)
            m.split_low(dve, 12)
            for j in range(4):
                dve.wait_ge(*m.past("cv_high", j + 1))
                dve.tensor_tensor(m.actL[:, 4 + j, :], m.csq[:, j, :], m.actH[:, 4 + j, :].bitcast(F32),
                                  ALU.subtract).then_inc(sem("conv_low"), 1)
            m.split_low(dve, 13)
            m.split_low(dve, 14)

            def residual(st, base, first, used):
                for r in range(RT):
                    dve.wait_ge(*(m.past(first, 1) if r == 0 else (m.used, used)))
                    xr = m.x[:, r, :].rearrange("p (a b) -> p a b", a=2)
                    dve.tensor_tensor(xr, xr, m.acc_row(base, r), ALU.add).then_inc(sem(st + "_x_ready"), 1)

            residual("f1", 4, "o1_first", m.first["o1"] + 4)
            m.dve_scale(dve, "f1")
            m.dve_turn(dve, "f1", (0, 1, 2, 3, 6, 7), gain=N2)
            m.split_low(dve, 15)
            m.dve_ffn(dve, "f1", 4)
            n = first["fox"]
            residual("fp", 0, "f1_first", n)
            m.dve_scale(dve, "fp")
            m.dve_turn(dve, "fp", (0, 1, 2, 3, 4, 5), gain=MIXPRE)
            dve.wait_ge(*m.past("wf_high", 1))
            dve.tensor_tensor(m.wfL[:], m.wf[:], m.wfH[:].bitcast(F32), ALU.subtract).then_inc(sem("wf_split"), 1)
            m.split_low(dve, n + 1)
            dve.wait_ge(*m.past("f_done", 1))
            dve.tensor_copy(m.fT[:], ps[0:H2, 3, 0:TOK]).then_inc(sem("f_out"), 1)
            m.split_low(dve, n + 2)
            dve.wait_ge(*m.past("f_turned", 1))
            dve.wait_ge(*m.past("fb_in", 16))
            c(dve.tensor_tensor(m.fl[:, 0], ps[:, 0, 0:2 * H2].rearrange("p (r h) -> p r h", r=2),
                                m.fb[:].unsqueeze(1).to_broadcast([P, RT, H2]), ALU.add))
            dve.scalar_tensor_tensor(m.fl[:, 1], m.fl[:, 0], -1.0, m.fl[:, 0], ALU.mult, ALU.max)\
               .then_inc(sem("f_abs"), 1)
            dve.wait_ge(*m.past("f_ln", 1))
            dve.scalar_tensor_tensor(m.fl[:, 1], m.fl[:, 0], 0.0, m.fl[:, 3], ALU.min, ALU.subtract)\
               .then_inc(sem("logf"), 1)

            def head_sums(blk):
                st = f"blk{blk}"
                dve.wait_ge(*m.past(st + "_sq", 2))
                dve.reduce_sum(m.ss[:], m.sq2[:].rearrange("p r (h d) -> p (r h) d", d=HD), AX.X)\
                   .then_inc(sem(st + "_head_sums"), 1)

            def head_norm(blk):
                dve.wait_ge(*m.past(f"blk{blk}_rstd", 1))
                t, h0 = (m.ka, m.qa)[blk % 2], 8 * (blk // 2)
                for r in range(RT):
                    v = t[:, r, h0:h0 + 8, 0:HD]
                    dve.tensor_tensor(v, v, m.rs[:, 8 * r:8 * r + 8].unsqueeze(2).to_broadcast([P, 8, HD]),
                                      ALU.mult).then_inc(sem("head_normed"), 1)

            for i in range(3):
                if i > 0:
                    m.split_low(dve, n + 2 * i + 2)
                    head_norm(i - 1)
                m.split_low(dve, n + 2 * i + 3)
                if i == 1:
                    dve.wait_ge(*m.past("csum", 1))
                    for r in range(RT):
                        cs = ps[:, 1, H2 * r:H2 * r + H2].unsqueeze(2)
                        dve.tensor_copy(m.qa[:, r, :, HD + 1:HD + 2], cs).then_inc(sem("c_cols"), 1)
                        dve.tensor_scalar(m.ka[:, r, :, HD:HD + 1], cs, -1.0, None, ALU.mult).then_inc(sem("c_cols"), 1)
                if i < 2:
                    head_sums(i)

            def others(h):
                if h == 3:
                    head_sums(2)
                if h == 4:
                    head_norm(2)
                if h == 6:
                    head_sums(3)
                if h == 7:
                    head_norm(3)
                if h == 14:
                    dve.wait_ge(*m.past("fox_out", 14))
                    for r in range(RT):
                        t = m.nat[:, r, 0:512]
                        dve.tensor_tensor(t, t, m.ga[:, r, 0:512], ALU.mult).then_inc(sem("fo_gated"), 1)
                if h in (7, 15, 16):
                    return
                for j in units_done(7 if h == 8 and not second else h):
                    m.split_low(dve, n + j + 2)

            def half_out(half, banks, done):
                h0 = 8 * half
                dve.wait_ge(*m.past("a2_out", h0 + 8))
                c(dve.reciprocal(rinv[:, :, h0:h0 + 8], rsum[:, :, h0:h0 + 8]))
                for r in range(RT):
                    dve.tensor_tensor(m.nat[:, r, 64 * h0:64 * h0 + 512].rearrange("p (h d) -> p h d", d=HD),
                                      ps[:, banks[r], :].rearrange("p (h d) -> p h d", d=HD),
                                      rinv[:, r, h0:h0 + 8].unsqueeze(2).to_broadcast([P, 8, HD]), ALU.mult)\
                       .then_inc(sem(done), 1)

            second = False
            m.dve_attention(dve, "a2", (0, 8), m.pt2, nmax, (0, 1), (2, 3), others)
            half_out(0, (4, 5), "half_out")
            second = True
            m.dve_attention(dve, "a2", (8, 16), m.pt2, nmax, (0, 1), (2, 3), others)
            half_out(1, (6, 7), "half_out")
            dve.wait_ge(*m.past("fox_out", 16))
            for r in range(RT):
                dve.wait_ge(*m.past("half_out", 3 + r))
                dve.wait_ge(*m.past("fo_gated", r + 1))
                t = m.nat[:, r, 512:D]
                dve.tensor_tensor(t, t, m.ga[:, r, 512:D], ALU.mult).then_inc(sem("fo_nat_ready"), 1)
            m.dve_turn(dve, "fo", (0, 1, 2, 3))
            for j in units_done(15):
                m.split_low(dve, n + j + 2)
            n = first["o2"]
            for i in range(3):
                m.split_low(dve, n + 2 + i)
            m.dve_postnorm(dve, "pm0", 4, m.gb[0], "gain0_in", 16)
            m.dve_scale(dve, "f2")
            m.dve_turn(dve, "f2", (0, 1, 2, 3, 6, 7), gain=FFNPRE)
            m.split_low(dve, n + 5)
            m.dve_ffn(dve, "f2", 4)
            m.dve_postnorm(dve, "pf0", 0, m.gb[1], "gain1_in", 16)
            n = first["s"]
            m.dve_scale(dve, "s")
            m.dve_turn(dve, "s", (4, 5, 6, 7, 2, 3), gain=MIXPRE + 8)
            m.split_low(dve, n + 1)
            for i in range(4):
                if i % 2 == 1:
                    dve.wait_ge(m.used, n + i + 1)
                    dve.tensor_copy(m.uT[:, :, :, i, :], ps[:, i, :].rearrange("p (h c t) -> p h t c", h=2, t=T))\
                       .then_inc(sem("ut_d"), 1)
                if i < 3:
                    m.split_low(dve, n + 2 + i)
            for h in range(2):
                dve.wait_ge(*m.past("u_chunked", 2 * h + 2))
                dve.tensor_copy(m.Ur[:, 8 * h:8 * h + 8, 4:8, :].rearrange("p q t c -> p t q c"),
                                ps[:, 5 + 2 * h, :].rearrange("p (t q c) -> p t q c", t=4, q=8))\
                   .then_inc(sem("ur_d"), 1)
            for b in range(2, 4):
                dve.wait_ge(*m.past("u_turned", b + 1))
                dve.tensor_copy(m.Uall[:, 4 * b:4 * b + 4, :, :],
                                ps[:, b, :].rearrange("p (q j c) -> p q j c", q=4, j=4)).then_inc(sem("u_out_d"), 1)
            flat = lambda a: a.rearrange("p g c -> p (g c)")
            grp = [slice(16 * j, 16 * j + 16) for j in range(4)]
            for b in (1, 3):
                dve.wait_ge(*m.past("v_done", b + 1))
                dve.tensor_copy(m.Vc[:, 4 * b:4 * b + 4, :], ps[:, 4 + b, :].rearrange("p (q s) -> p q s", q=4))\
                   .then_inc(sem("vc_d"), 1)
            for b in (1, 3):
                dve.wait_ge(*m.past("v_turned", b + 1))
                dve.tensor_copy(m.V[:].rearrange("p (j q) c -> p q j c", j=4)[:, 4 * b:4 * b + 4],
                                ps[:, b, :].rearrange("p (q j c) -> p q j c", q=4, j=4)).then_inc(sem("vo_d"), 1)
            dve.wait_ge(*m.past("phases", 1))
            for j in range(4):
                dve.wait_ge(*m.past("vs_done", j + 1))
                k = c.step(dve.tensor_tensor(flat(m.W[:, grp[j], :]), ps[:, 4 + j, :], flat(m.ST[:, grp[j], :]), ALU.mult))
                dve.wait_ge(*m.past("vc", j + 1))
                c.wait(k)
                c(dve.tensor_tensor(m.V[:, grp[j], :], m.V[:, grp[j], :], m.W[:, grp[j], :], ALU.add))
                dve.tensor_tensor_scan(flat(m.W[:, grp[j], :]), flat(m.D0[:, grp[j], :]), flat(m.V[:, grp[j], :]), 0.0,
                                       ALU.mult, ALU.add).then_inc(sem("scanned"), 1)
            dve.wait_ge(*m.past("scanned", 4))
            c.step(dve.memset(m.X33[:, :, 0:1], 0.0))
            for j in range(4):
                dve.wait_ge(*m.past("zs_done", j + 1))
                c(dve.tensor_tensor(flat(m.V[:, grp[j], :]), ps[:, j, :], flat(m.ST[:, grp[j], :]), ALU.mult))
                dve.wait_ge(*m.past("zc", j + 1))
                dve.tensor_tensor(m.X33[:, grp[j], 1:NCH + 1], m.W[:, grp[j], :], m.V[:, grp[j], :], ALU.subtract)\
                   .then_inc(sem("states"), 1)
            m.split_low(dve, n + 5)
            for b in (1, 3):
                dve.wait_ge(*m.past("y_done", b + 1))
                dve.tensor_copy(m.Ysb[:, :, 4 * b:4 * b + 4, :].rearrange("p t q c -> p q t c"),
                                ps[:, b, :].rearrange("p (q t c) -> p q t c", q=4, t=T)).then_inc(sem("y_out_d"), 1)

            def yg_low(i):
                kt = Y_ORDER[i]
                dve.wait_ge(*m.past("yg_high_ready", i + 1))
                dve.tensor_tensor(m.actL[:, kt, :], m.ygT[:, kt, :], m.actH[:, kt, :].bitcast(F32), ALU.subtract)\
                   .then_inc(sem("yg_act_ready"), 1)

            for i, kt in enumerate(Y_ORDER):
                j, h = divmod(kt, 2)
                dve.wait_ge(*m.past("y_turned", h + 1))
                yT = ps[:, 4 + 2 * h:6 + 2 * h, :].rearrange("p b (t j c) -> p (b t) j c", t=4, j=4)
                dve.scalar_tensor_tensor(m.ygT[:, kt, :].rearrange("p (c t) -> p t c", t=T), m.uT[:, h, :, j, :],
                                         m.vec[:, SKIP + kt:SKIP + kt + 1], yT[:, :, j, :], ALU.mult, ALU.add)\
                   .then_inc(sem("y_sum"), 1)
                if i > 2:
                    yg_low(i - 3)
            for i in range(5, 8):
                yg_low(i)

            def yo_low(i):
                dve.wait_ge(*m.past("yo_high", i + 1))
                t = slice(2 * i, 2 * i + 2)
                dve.tensor_tensor(m.yoL[:, t, :], m.yoT[:, t, :], m.yoH[:, t, :].bitcast(F32), ALU.subtract)\
                   .then_inc(sem("yo_low"), 1)

            n = first["glu"]
            for i in range(4):
                dve.wait_ge(*m.past("glu_sig", i + 1))
                t = slice(2 * i, 2 * i + 2)
                dve.tensor_tensor(m.yoT[:, t, :], m.ygT[:, t, :], m.sgT[:, t, :], ALU.mult).then_inc(sem("gated"), 1)
                m.split_low(dve, n + 2 + i)
                if i > 0:
                    yo_low(i - 1)
            yo_low(3)
            n = first["o3"]
            for i in range(1, 4):
                m.split_low(dve, n + 1 + i)
            m.dve_postnorm(dve, "pm1", 4, m.gb[0], "gain0_in", 32)
            m.dve_scale(dve, "f3")
            m.dve_turn(dve, "f3", (0, 1, 2, 3, 6, 7), gain=FFNPRE + 8)
            m.split_low(dve, n + 5)
            m.dve_ffn(dve, "f3", 4)
            m.dve_postnorm(dve, "pf1", 0, m.gb[1], "gain1_in", 32)


BIG = ["x", "w_in", "w_out", "w_gate", "w_up", "w_down", "fox_w_in_2", "fox_b_f_2", "fox_w_out_2", "s5_w_in_2",
       "s5_w_glu_2", "s5_w_out_2", "mix_post_gain_2", "ffn_post_gain_2", "ffn_w_gate_2", "ffn_w_up_2",
       "ffn_w_down_2"]


def rope_table():
    pos = np.arange(TOK, dtype=np.float32)
    inv = np.float32(10000.0) ** (-np.arange(0, HD, 2, dtype=np.float32) / np.float32(HD))
    ang = pos[:, None] * inv[None, :]
    cos, sin = np.cos(ang), np.sin(ang)
    table = np.stack([np.concatenate([cos, cos], 1), np.concatenate([-sin, sin], 1)], 1).astype(np.float32)
    return table.reshape(RT, P, 2, HD).transpose(1, 0, 2, 3)


def lay_out(inputs):
    a = {name: np.asarray(inputs[name]) for name in inputs}
    pieces = lambda v: v.reshape(-1, P).T
    twice = lambda v: np.concatenate([v, v], 0)
    vec = [pieces(a[n]) for n in ("norm1_g", "norm2_g", "mix_pre_gain_2", "ffn_pre_gain_2", "glu_b", "dw_b",
                                  "conv_ln_g", "conv_ln_b", "s5_d_2")]
    vec.append(np.zeros((P, VCOLS - SKIP - KT), np.float32))
    taps = a["dw_w"][0].reshape(TAPS, 4, P).transpose(2, 0, 1).reshape(P, TAPS * 4)
    arrays = {name: a[name] for name in BIG}
    arrays["vectors"] = np.concatenate(vec + [taps], 1)
    arrays["lamdt"] = np.stack([twice(a["s5_lam_re_2"][0].T), twice(a["s5_lam_im_2"][0].T),
                                np.broadcast_to(a["s5_log_dt_2"], (P, NG))], 1)
    arrays["head_gains"] = np.concatenate([a[n].reshape(1, HD) for n in ("q_norm_g", "k_norm_g", "fox_q_gain_2",
                                                                          "fox_k_gain_2")], 1)
    arrays["s5_b"] = np.stack([twice(a[n][0].transpose(1, 0, 2)) for n in ("s5_b_re_2", "s5_b_im_2")], 1)
    arrays["s5_c"] = np.stack([twice(a[n][0].transpose(2, 0, 1)) for n in ("s5_c_re_2", "s5_c_im_2")], 1)
    arrays["rope"] = rope_table()
    return {name: np.ascontiguousarray(v) for name, v in arrays.items()}


def kernel(**inputs):
    import concourse.bacc as bacc
    from concourse.bass_utils import run_bass_kernel_spmd

    nc = bacc.Bacc("TRN2", target_bir_lowering=False, num_devices=1)
    arrays = lay_out(inputs)
    io = {name: nc.dram_tensor(f"in_{name}", a.shape, mybir.dt.from_np(a.dtype), kind="ExternalInput").ap()
          for name, a in arrays.items()}
    out = nc.dram_tensor("out", (1, TOK, D), F32, kind="ExternalOutput").ap()
    build(nc, io, out)
    r = run_bass_kernel_spmd(nc, [{f"in_{n}": a for n, a in arrays.items()}], core_ids=[0])
    return r.results[0]["out"]
```
